# Optimizing a Trainium2 kernel written in Bass

```python
import jax, jax.numpy as jnp
from jax import lax
import numpy as np

D_MODEL = 1024
BATCH = 1
SEQ = 128
DEPTH = 2
DEC_BATCH = 1
DEC_SEQ = 256
PAST_LEN = 128

GRID_W = 64
N_MIX = (DEPTH + 1) // 2
N_CONV = DEPTH // 2

MLA_HEADS = 8
MLA_NOPE = 64
MLA_ROPE = 32
MLA_V = 64
Q_LORA = 384
KV_LORA = 256
ROPE_BASE = 10000.0
Q_BLOCK = 128
RET_HEADS = 8
RET_DK = 64
RET_DV = 64
RET_CHUNK = 128
EVEN_SPLITS = (Q_LORA, KV_LORA, MLA_ROPE, RET_HEADS * RET_DK, RET_HEADS * RET_DK,
               RET_HEADS * RET_DV, RET_HEADS * RET_DV)
IN_EVEN = sum(EVEN_SPLITS)
MIX_WIDTH = MLA_HEADS * MLA_V + RET_HEADS * RET_DV
CONV_W = 3
D_FF = 2816
N_EXPERTS = 8
TOP_K = 2
D_FF_EXPERT = 2816
ALPHA = (2.0 * DEPTH) ** 0.25
BETA = (8.0 * DEPTH) ** -0.25

kernel_name = 'hybrid_mla_retention_shortconv_diffusion_step'

def _layer_norm(x, g, b, eps=1e-5):
    xf = x.astype(jnp.float32)
    mu = jnp.mean(xf, -1, keepdims=True)
    var = jnp.mean(jnp.square(xf - mu), -1, keepdims=True)
    y = (xf - mu) * lax.rsqrt(var + eps)
    return (y * g.astype(jnp.float32) + b.astype(jnp.float32)).astype(x.dtype)

def _rms_norm(x, g, eps=1e-6):
    xf = x.astype(jnp.float32)
    y = xf * lax.rsqrt(jnp.mean(jnp.square(xf), -1, keepdims=True) + eps)
    return (y * g.astype(jnp.float32)).astype(x.dtype)

def _head_norm(x, eps=1e-5):
    xf = x.astype(jnp.float32)
    mu = jnp.mean(xf, -1, keepdims=True)
    var = jnp.mean(jnp.square(xf - mu), -1, keepdims=True)
    return (xf - mu) * lax.rsqrt(var + eps)

def _rope(x, cos, sin):
    xf = x.astype(jnp.float32)
    x1, x2 = xf[..., 0::2], xf[..., 1::2]
    out = jnp.stack([x1 * cos - x2 * sin, x1 * sin + x2 * cos], axis=-1)
    return out.reshape(x.shape).astype(x.dtype)

def _axial_angles(n_tok):
    rows = n_tok // GRID_W
    r, col = jnp.meshgrid(jnp.arange(rows, dtype=jnp.float32), jnp.arange(GRID_W, dtype=jnp.float32),
                          indexing='ij')
    r = r.reshape(-1)
    col = col.reshape(-1)
    n_freq = MLA_ROPE // 4
    freqs = 1.0 / (ROPE_BASE ** (jnp.arange(n_freq, dtype=jnp.float32) / n_freq))
    ang = jnp.concatenate([r[:, None] * freqs, col[:, None] * freqs], axis=-1)
    return jnp.cos(ang), jnp.sin(ang)

def _ret_angles(n_tok):
    theta = 1.0 / (10000.0 ** jnp.linspace(0.0, 1.0, RET_DK // 2, dtype=jnp.float32))
    ang = jnp.arange(n_tok, dtype=jnp.float32)[:, None] * theta
    return jnp.cos(ang), jnp.sin(ang)

def _split(x, sizes):
    idx = np.cumsum(np.array(sizes))[:-1].tolist()
    return jnp.split(x, idx, axis=-1)

def _modulation(cond, w_mod, b_mod):
    m = jax.nn.silu(cond) @ w_mod + b_mod
    return jnp.split(m[:, None, :], 6, axis=-1)

def _modulate(x, shift, scale):
    return x * (1.0 + scale) + shift

def _attention(q, k, v):
    B, Tq, H, dq = q.shape
    dv = v.shape[-1]
    nb = Tq // Q_BLOCK
    scale = dq ** -0.5
    qb = q.reshape(B, nb, Q_BLOCK, H, dq).transpose(1, 0, 2, 3, 4)

    def one_block(qblk):
        s = jnp.einsum('bqhd,bkhd->bhqk', qblk, k).astype(jnp.float32) * scale
        p = jax.nn.softmax(s, axis=-1).astype(v.dtype)
        return jnp.einsum('bhqk,bkhd->bqhd', p, v)

    out = lax.map(one_block, qb)
    return out.transpose(1, 0, 2, 3, 4).reshape(B, Tq, H, dv)

def _retention_scan(q, k, v, log_gamma, s0):
    B, T, H, _ = q.shape
    dv = v.shape[-1]
    C = RET_CHUNK
    n = T // C
    idx = jnp.arange(C, dtype=jnp.float32)
    diff = idx[:, None] - idx[None, :]
    decay_mat = jnp.where(diff >= 0, jnp.exp(jnp.maximum(diff, 0.0) * log_gamma[:, None, None]), 0.0)
    q_decay = jnp.exp((idx + 1.0) * log_gamma[:, None])
    k_decay = jnp.exp((C - 1.0 - idx) * log_gamma[:, None])
    c_decay = jnp.exp(C * log_gamma)

    def to_chunks(a):
        return a.astype(jnp.float32).reshape(B, n, C, H, a.shape[-1]).transpose(1, 0, 3, 2, 4)

    def step(S, qkv):
        qc, kc, vc = qkv
        scores = jnp.einsum('bhid,bhjd->bhij', qc, kc) * decay_mat
        inner = jnp.einsum('bhij,bhjv->bhiv', scores, vc)
        cross = jnp.einsum('bhid,bhdv->bhiv', qc, S) * q_decay[None, :, :, None]
        S = S * c_decay[None, :, None, None] + jnp.einsum('bhjd,bhjv->bhdv', kc * k_decay[None, :, :, None], vc)
        return S, inner + cross

    S_fin, out = lax.scan(step, s0.astype(jnp.float32), (to_chunks(q), to_chunks(k), to_chunks(v)))
    out = out.transpose(1, 0, 3, 2, 4).reshape(B, T, H, dv)
    return out, S_fin

def _retention(rq, rk, rv, rg, lg_f, lg_b, s0_f, s0_b):
    B, T = rq.shape[:2]
    yf, sf = _retention_scan(rq, rk, rv, lg_f, s0_f)
    yb, sb = _retention_scan(jnp.flip(rq, 1), jnp.flip(rk, 1), jnp.flip(rv, 1), lg_b, s0_b)
    y = _head_norm(yf + jnp.flip(yb, 1)).reshape(B, T, RET_HEADS * RET_DV).astype(rv.dtype)
    return y * jax.nn.silu(rg), sf.astype(rv.dtype), sb.astype(rv.dtype)

def _even_project(h, w_in, q_a_gain, kv_a_gain, w_q_b):
    B, T, _ = h.shape
    q_a, kv_a, k_pe, rq, rk, rv, rg = _split(h @ w_in, EVEN_SPLITS)
    q = (_rms_norm(q_a, q_a_gain) @ w_q_b).reshape(B, T, MLA_HEADS, MLA_NOPE + MLA_ROPE)
    ckv = _rms_norm(kv_a, kv_a_gain)
    rq = rq.reshape(B, T, RET_HEADS, RET_DK)
    rk = rk.reshape(B, T, RET_HEADS, RET_DK) * (RET_DK ** -0.5)
    rv = rv.reshape(B, T, RET_HEADS, RET_DV)
    return q, ckv, k_pe, rq, rk, rv, rg

def _mla_kv(ckv, k_pe, w_kv_b):
    B, T, _ = ckv.shape
    kv = (ckv @ w_kv_b).reshape(B, T, MLA_HEADS, MLA_NOPE + MLA_V)
    k_nope, v = kv[..., :MLA_NOPE], kv[..., MLA_NOPE:]
    k = jnp.concatenate([k_nope, jnp.broadcast_to(k_pe[:, :, None, :], (B, T, MLA_HEADS, MLA_ROPE))], axis=-1)
    return k, v

def _mix_context(h, w_in, q_a_gain, kv_a_gain, w_q_b, w_kv_b, lg_f, lg_b, w_out):
    B, L, _ = h.shape
    q, ckv, k_pe, rq, rk, rv, rg = _even_project(h, w_in, q_a_gain, kv_a_gain, w_q_b)
    k, v = _mla_kv(ckv, k_pe, w_kv_b)
    attn = _attention(q, k, v)
    zeros = jnp.zeros((B, RET_HEADS, RET_DK, RET_DV), jnp.float32)
    ret, sf, sb = _retention(rq, rk, rv, rg, lg_f, lg_b, zeros, zeros)
    y = jnp.concatenate([attn.reshape(B, L, MLA_HEADS * MLA_V), ret], axis=-1) @ w_out
    return y, ckv, k_pe, sf, sb

def _mix_latent(h, ckv_c, kpe_c, sf0, sb0, rope_cs, ret_cs, w_in, q_a_gain, kv_a_gain, w_q_b, w_kv_b,
                lg_f, lg_b, w_out):
    B, T, _ = h.shape
    q, ckv, k_pe, rq, rk, rv, rg = _even_project(h, w_in, q_a_gain, kv_a_gain, w_q_b)
    cos, sin = rope_cs
    q = jnp.concatenate([q[..., :MLA_NOPE], _rope(q[..., MLA_NOPE:], cos[:, None, :], sin[:, None, :])], axis=-1)
    k_pe = _rope(k_pe, cos, sin)
    k_l, v_l = _mla_kv(ckv, k_pe, w_kv_b)
    k_c, v_c = _mla_kv(ckv_c, kpe_c, w_kv_b)
    attn = _attention(q, jnp.concatenate([k_c, k_l], axis=1), jnp.concatenate([v_c, v_l], axis=1))
    rcos, rsin = ret_cs
    rq = _rope(rq, rcos[:, None, :], rsin[:, None, :])
    rk = _rope(rk, rcos[:, None, :], rsin[:, None, :])
    ret, _, _ = _retention(rq, rk, rv, rg, lg_f, lg_b, sf0, sb0)
    return jnp.concatenate([attn.reshape(B, T, MLA_HEADS * MLA_V), ret], axis=-1) @ w_out

def _short_conv(h, w_in, conv_w, w_out):
    b_gate, c_gate, u = jnp.split(h @ w_in, 3, axis=-1)
    z = c_gate * u
    zp = jnp.pad(z, ((0, 0), (1, 1), (0, 0)))
    y = zp[:, :-2] * conv_w[0] + zp[:, 1:-1] * conv_w[1] + zp[:, 2:] * conv_w[2]
    return (b_gate * y) @ w_out

def _swiglu(h, w_gate, w_up, w_down):
    return (jax.nn.silu(h @ w_gate) * (h @ w_up)) @ w_down

def _moe(h, router_w, router_b, exp_gate, exp_up, exp_down):
    logits = (h @ router_w).astype(jnp.float32) + router_b.astype(jnp.float32)
    top_val, top_idx = lax.top_k(logits, TOP_K)
    wts = jax.nn.softmax(top_val, axis=-1)
    combine = jnp.sum(jax.nn.one_hot(top_idx, N_EXPERTS, dtype=jnp.float32) * wts[..., None], axis=-2)
    combine = combine.astype(h.dtype)
    y = jnp.zeros_like(h)
    for e in range(N_EXPERTS):
        y = y + combine[..., e:e + 1] * _swiglu(h, exp_gate[e], exp_up[e], exp_down[e])
    return y

def setup_inputs(seed: int = 0) -> dict:
    key = jax.random.key(seed)
    ks = jax.random.split(key, 32)
    f32 = jnp.float32
    D = D_MODEL

    def nrm(i, shape, scale):
        return jax.random.normal(ks[i], shape, f32) * scale

    heads = np.arange(RET_HEADS, dtype=np.float32)
    decay_logit = jnp.asarray(np.log(2.0 ** (5.0 + heads) - 1.0), dtype=f32)
    return {
        'x_prompt': nrm(0, (BATCH, SEQ, D), 1.0),
        'x_sample': nrm(1, (DEC_BATCH, DEC_SEQ, D), 1.0),
        'c': nrm(2, (DEC_BATCH, D), 1.0),
        'cache_ckv': nrm(3, (DEC_BATCH, N_MIX, PAST_LEN, KV_LORA), 1.0),
        'cache_kpe': nrm(4, (DEC_BATCH, N_MIX, PAST_LEN, MLA_ROPE), 1.0),
        'state_ret_fwd': nrm(5, (DEC_BATCH, N_MIX, RET_HEADS, RET_DK, RET_DV), 0.5),
        'state_ret_bwd': nrm(6, (DEC_BATCH, N_MIX, RET_HEADS, RET_DK, RET_DV), 0.5),
        'c_ctx': nrm(7, (D,), 1.0),
        'w_mod': nrm(8, (DEPTH, D, 6 * D), D ** -0.5),
        'b_mod': nrm(9, (DEPTH, 6 * D), 0.02),
        'ln_g': 1.0 + nrm(10, (DEPTH, 2, D), 0.02),
        'ln_b': nrm(11, (DEPTH, 2, D), 0.02),
        'w_in_mix': nrm(12, (N_MIX, D, IN_EVEN), D ** -0.5),
        'q_a_gain': 1.0 + nrm(13, (N_MIX, Q_LORA), 0.02),
        'kv_a_gain': 1.0 + nrm(14, (N_MIX, KV_LORA), 0.02),
        'w_q_b': nrm(15, (N_MIX, Q_LORA, MLA_HEADS * (MLA_NOPE + MLA_ROPE)), Q_LORA ** -0.5),
        'w_kv_b': nrm(16, (N_MIX, KV_LORA, MLA_HEADS * (MLA_NOPE + MLA_V)), KV_LORA ** -0.5),
        'ret_decay_fwd': decay_logit[None, :] + nrm(17, (N_MIX, RET_HEADS), 0.1),
        'ret_decay_bwd': decay_logit[None, :] + nrm(18, (N_MIX, RET_HEADS), 0.1),
        'w_out_mix': nrm(19, (N_MIX, MIX_WIDTH, D), BETA * MIX_WIDTH ** -0.5),
        'w_in_conv': nrm(20, (N_CONV, D, 3 * D), D ** -0.5),
        'conv_w': nrm(21, (N_CONV, CONV_W, D), CONV_W ** -0.5),
        'w_out_conv': nrm(22, (N_CONV, D, D), BETA * D ** -0.5),
        'ffn_gate': nrm(23, (N_MIX, D, D_FF), D ** -0.5),
        'ffn_up': nrm(24, (N_MIX, D, D_FF), D ** -0.5),
        'ffn_down': nrm(25, (N_MIX, D_FF, D), BETA * D_FF ** -0.5),
        'router_w': nrm(26, (N_CONV, D, N_EXPERTS), D ** -0.5),
        'router_b': nrm(27, (N_CONV, N_EXPERTS), 0.01),
        'exp_gate': nrm(28, (N_CONV, N_EXPERTS, D, D_FF_EXPERT), D ** -0.5),
        'exp_up': nrm(29, (N_CONV, N_EXPERTS, D, D_FF_EXPERT), D ** -0.5),
        'exp_down': nrm(30, (N_CONV, N_EXPERTS, D_FF_EXPERT, D), BETA * D_FF_EXPERT ** -0.5),
    }

def reference(x_prompt, x_sample, c, cache_ckv, cache_kpe, state_ret_fwd, state_ret_bwd,
              c_ctx, w_mod, b_mod, ln_g, ln_b,
              w_in_mix, q_a_gain, kv_a_gain, w_q_b, w_kv_b, ret_decay_fwd, ret_decay_bwd, w_out_mix,
              w_in_conv, conv_w, w_out_conv,
              ffn_gate, ffn_up, ffn_down,
              router_w, router_b, exp_gate, exp_up, exp_down):
    n_lat = x_sample.shape[1]
    rope_cs = _axial_angles(n_lat)
    ret_cs = _ret_angles(n_lat)
    xp, xs = x_prompt, x_sample
    ckv_new, kpe_new, sf_new, sb_new = [], [], [], []
    for layer in range(DEPTH):
        j = layer // 2
        mp = _modulation(c_ctx[None], w_mod[layer], b_mod[layer])
        ms = _modulation(c, w_mod[layer], b_mod[layer])
        hp = _modulate(xp, mp[0], mp[1])
        hs = _modulate(xs, ms[0], ms[1])
        if layer % 2 == 0:
            lg_f = jax.nn.log_sigmoid(ret_decay_fwd[j].astype(jnp.float32))
            lg_b = jax.nn.log_sigmoid(ret_decay_bwd[j].astype(jnp.float32))
            yp, ckv, kpe, sf, sb = _mix_context(hp, w_in_mix[j], q_a_gain[j], kv_a_gain[j], w_q_b[j],
                                                w_kv_b[j], lg_f, lg_b, w_out_mix[j])
            ys = _mix_latent(hs, cache_ckv[:, j], cache_kpe[:, j], state_ret_fwd[:, j], state_ret_bwd[:, j],
                             rope_cs, ret_cs, w_in_mix[j], q_a_gain[j], kv_a_gain[j], w_q_b[j], w_kv_b[j],
                             lg_f, lg_b, w_out_mix[j])
            ckv_new.append(ckv)
            kpe_new.append(kpe)
            sf_new.append(sf)
            sb_new.append(sb)
        else:
            yp = _short_conv(hp, w_in_conv[j], conv_w[j], w_out_conv[j])
            ys = _short_conv(hs, w_in_conv[j], conv_w[j], w_out_conv[j])
        xp = _layer_norm(ALPHA * xp + mp[2] * yp, ln_g[layer, 0], ln_b[layer, 0])
        xs = _layer_norm(ALPHA * xs + ms[2] * ys, ln_g[layer, 0], ln_b[layer, 0])
        hp = _modulate(xp, mp[3], mp[4])
        hs = _modulate(xs, ms[3], ms[4])
        if layer % 2 == 0:
            fp = _swiglu(hp, ffn_gate[j], ffn_up[j], ffn_down[j])
            fs = _swiglu(hs, ffn_gate[j], ffn_up[j], ffn_down[j])
        else:
            fp = _moe(hp, router_w[j], router_b[j], exp_gate[j], exp_up[j], exp_down[j])
            fs = _moe(hs, router_w[j], router_b[j], exp_gate[j], exp_up[j], exp_down[j])
        xp = _layer_norm(ALPHA * xp + mp[5] * fp, ln_g[layer, 1], ln_b[layer, 1])
        xs = _layer_norm(ALPHA * xs + ms[5] * fs, ln_g[layer, 1], ln_b[layer, 1])
    new_ckv = jnp.stack(ckv_new, axis=1)
    new_kpe = jnp.stack(kpe_new, axis=1)
    new_ret_fwd = jnp.stack(sf_new, axis=1)
    new_ret_bwd = jnp.stack(sb_new, axis=1)
    return (xp, xs, new_ckv, new_kpe, new_ret_fwd, new_ret_bwd)


_drawn_inputs = setup_inputs


def setup_inputs(seed=0):
    import zlib

    import numpy as np

    out = dict(_drawn_inputs(seed))
    spreads = {}
    factors = {'cache_ckv': 4.302,
     'cache_kpe': 6.37,
     'state_ret_fwd': 3.557,
     'state_ret_bwd': 3.571,
     'q_a_gain': 8.0,
     'kv_a_gain': 2.914,
     'router_b': 6.16}
    for name, (base, spread) in spreads.items():
        noise = np.random.default_rng([zlib.crc32(name.encode()), seed]).standard_normal(out[name].shape)
        drawn = base * np.exp(spread * noise) if base else spread * noise
        out[name] = __import__('jax').numpy.asarray(drawn.astype(out[name].dtype))
    for name, factor in factors.items():
        out[name] = (out[name] * factor).astype(out[name].dtype)
    return out
```

```python
from contextlib import ExitStack

import numpy as np
import concourse.bass as bass
from concourse import mybir
from concourse.bass import ds

F32 = mybir.dt.float32
F32R = mybir.dt.float32r
I32 = mybir.dt.int32
ALU = mybir.AluOpType
ACT = mybir.ActivationFunctionType
AX = mybir.AxisListType.X

P = 128
D = 1024
KD = D // P
TILES = 3
T_ALL = TILES * P
PAST = 128
Q_LORA, KV_LORA, ROPE, NOPE, HEADS, DV = 384, 256, 32, 64, 8, 64
HD = HEADS * DV
KQ, KKV = Q_LORA // P, KV_LORA // P
IN_EVEN = Q_LORA + KV_LORA + ROPE + 4 * HD
FF = 2816
N_EXP = 8
GRID_W = 64
ALPHA = (2.0 * 2) ** 0.25
ATT_SCALE = float(NOPE + ROPE) ** -0.5
RET_SCALE = float(DV) ** -0.5
LN_EPS, RMS_EPS = 1e-5, 1e-6

C_Q, C_KV, C_PE = 0, Q_LORA, Q_LORA + KV_LORA
C_RQ = C_PE + ROPE
C_RK, C_RV, C_RG = C_RQ + HD, C_RQ + 2 * HD, C_RQ + 3 * HD
PROJ_CHUNKS = [(0, 512), (512, C_RQ - 512), (C_RQ, 512), (C_RK, 512), (C_RV, 512), (C_RG, 512)]

UNIT = 2048
RAW = 3
SPLIT = 3
AHEAD = 2

PAIR = 256
PAIRS = FF // PAIR
PHASE_PAIRS = [range(0, 6), range(6, PAIRS)]
PHASE_DOWN = [[2, 2, 2, 2, 2, 1, 1], [2, 2, 2, 1, 1, 1, 1]]
FFN_UNITS = 2 * PAIRS + 14

U_MODA0 = 0
U_PROJ = U_MODA0 + 12
U_KV = U_PROJ + 11
U_QA, U_QB = U_KV + 1, U_KV + 2
U_OUT0 = U_QB + 1
U_MODB0 = U_OUT0 + 4
U_FFN0 = U_MODB0 + 12
U_MODA1 = U_FFN0 + FFN_UNITS
U_CONV = U_MODA1 + 12
U_OUT1 = U_CONV + 12
U_MODB1 = U_OUT1 + 4
U_MOE = U_MODB1 + 12
assert FFN_UNITS % RAW == 0 and FFN_UNITS % SPLIT == 0

R_COND, R_QG, R_CONVW, R_BMOD = 0, 16, 19, 43


def _constants():
    i = np.arange(P, dtype=np.float32)
    row, col = i[:, None], i[None, :]
    parts = {}
    parts["ident"] = np.eye(P, dtype=np.float32)
    parts["iota"] = np.broadcast_to(col, (P, P)).astype(np.float32)
    sel = np.zeros((P, 2, P), np.float32)
    sel[[0, 32], 0] = 1.0
    sel[[64, 96], 1] = 1.0
    parts["selrow"] = sel.reshape(P, -1)
    parts["selcol"] = np.ascontiguousarray(sel[:, :, 0])
    parts["decay_at"] = np.stack([i + 1, P - 1 - i, i, P - i], 1)
    parts["rank8"] = np.broadcast_to(100.0 - np.arange(8, dtype=np.float32), (P, 8)).astype(np.float32)
    parts["mhalf"] = np.full((P, 8), -0.5, np.float32)

    def tables(cos, sin):
        n = cos.shape[1]
        c = np.ones((TILES, P, 2 * n), np.float32)
        s = np.zeros((TILES, P, 2 * n), np.float32)
        c[1:] = np.repeat(cos, 2, axis=1).reshape(2, P, 2 * n)
        s[1:, :, 0::2] = -sin.reshape(2, P, n)
        s[1:, :, 1::2] = sin.reshape(2, P, n)
        return (a.transpose(1, 0, 2).reshape(P, -1) for a in (c, s))

    tok = np.arange(2 * P)
    n_freq = ROPE // 4
    freqs = (1.0 / (np.float32(10000.0) ** (np.arange(n_freq, dtype=np.float32) / n_freq))).astype(np.float32)
    r, c = (tok // GRID_W).astype(np.float32), (tok % GRID_W).astype(np.float32)
    ang = np.concatenate([r[:, None] * freqs, c[:, None] * freqs], -1)
    parts["cos_q"], parts["sin_q"] = tables(np.cos(ang), np.sin(ang))
    theta = (1.0 / (np.float32(10000.0) ** np.linspace(0.0, 1.0, DV // 2, dtype=np.float32))).astype(np.float32)
    ang = tok.astype(np.float32)[:, None] * theta
    ret_tables = np.concatenate(list(tables(np.cos(ang), np.sin(ang))), 1)
    ranks = np.concatenate([(row < col).astype(np.float32), np.ones((P, P), np.float32)], 1)
    at, cols = 0, {}
    for k, v in parts.items():
        cols[k] = (at, at + v.shape[1])
        at += v.shape[1]
    masks = np.concatenate([np.maximum(col - row, 0), np.maximum(row - col, 0),
                            (col >= row), (row >= col)], 1).astype(np.float32)
    return np.concatenate(list(parts.values()), 1).astype(np.float32), cols, masks, ret_tables, ranks


CONST, CONST_AT, MASKS, RET_TABLES, RANKS = _constants()


def weight_unit(w, n, expert=None):
    def chunk(mat, c0, width, k0, nk):
        half = (nk + 1) // 2
        src = mat.rearrange("(k p) n -> p k n", p=P)
        return nk * width, [((a * width, b * width), b - a, src[:, k0 + a:k0 + b, c0:c0 + width])
                            for a, b in ((0, half), (half, nk))]

    def rows(mat, k0, nk):
        src = mat.rearrange("(k p) n -> p k n", p=P)
        if nk == 2:
            return 2 * D, [((a * D, (a + 1) * D), 1, src[:, k0 + a:k0 + a + 1, :]) for a in (0, 1)]
        return D, [((a * 512, (a + 1) * 512), 1, src[:, k0:k0 + 1, a * 512:(a + 1) * 512]) for a in (0, 1)]

    def mod(layer, i):
        return chunk(w["w_mod"][layer], (i // 2) * 512, 512, 4 * (i % 2), 4)

    def ffn(gate, up, down, i):
        for phase in (0, 1):
            pairs, downs = PHASE_PAIRS[phase], PHASE_DOWN[phase]
            if i < 2 * len(pairs):
                c, k0 = pairs[i // 2] * PAIR, 4 * (i % 2)
                return UNIT, [(s, None, m.rearrange("(k p) n -> p k n", p=P)[:, k0:k0 + 4, c:c + PAIR])
                              for s, m in enumerate((gate, up))]
            i -= 2 * len(pairs)
            if i < len(downs):
                return rows(down, 2 * pairs[0] + sum(downs[:i]), downs[i])
            i -= len(downs)

    if n < U_PROJ:
        return mod(0, n)
    if n < U_KV:
        i = n - U_PROJ
        for c0, width in PROJ_CHUNKS:
            if width < 512:
                if i == 0:
                    return chunk(w["w_in_mix"][0], c0, width, 0, KD)
                i -= 1
            else:
                if i < 2:
                    return chunk(w["w_in_mix"][0], c0, width, 4 * i, 4)
                i -= 2
    if n == U_KV:
        return rows(w["w_kv_b"][0], 0, 2)
    if n == U_QA:
        return chunk(w["w_q_b"][0], 0, HD, 0, KQ)
    if n == U_QB:
        return chunk(w["w_q_b"][0], HD, HEADS * ROPE, 0, KQ)
    if n < U_MODB0:
        return rows(w["w_out_mix"][0], 2 * (n - U_OUT0), 2)
    if n < U_FFN0:
        return mod(0, 12 + n - U_MODB0)
    if n < U_MODA1:
        return ffn(w["ffn_gate"][0], w["ffn_up"][0], w["ffn_down"][0], n - U_FFN0)
    if n < U_CONV:
        return mod(1, n - U_MODA1)
    if n < U_OUT1:
        i = n - U_CONV
        third = (1, 2, 0)[i % 3]
        return chunk(w["w_in_conv"][0], third * D + (i // 3) * 256, 256, 0, KD)
    if n < U_MODB1:
        return rows(w["w_out_conv"][0], 2 * (n - U_OUT1), 2)
    if n < U_MOE:
        return mod(1, 12 + n - U_MODB1)
    return ffn(w["exp_gate"][0][expert], w["exp_up"][0][expert], w["exp_down"][0][expert], n - U_MOE)


def unit_words(n):
    if n >= U_MOE:
        n = U_FFN0 + n - U_MOE
    if n >= U_FFN0 and n < U_MODA1:
        i = n - U_FFN0
        for phase in (0, 1):
            if i < 2 * len(PHASE_PAIRS[phase]):
                return UNIT
            i -= 2 * len(PHASE_PAIRS[phase])
            if i < len(PHASE_DOWN[phase]):
                return PHASE_DOWN[phase][i] * D
            i -= len(PHASE_DOWN[phase])
    if n == U_PROJ + 2:
        return KD * PROJ_CHUNKS[1][1]
    return {U_QA: KQ * HD, U_QB: KQ * HEADS * ROPE}.get(n, UNIT)


MOD_CHUNKS = [(layer, v, h) for layer in (0, 1) for v in range(6) for h in (0, 1)]
MOD_POSTS = [0]
for _layer, _v, _h in MOD_CHUNKS:
    MOD_POSTS.append(MOD_POSTS[-1] + (2 if _v % 3 == 2 else 1))


def build(nc, t, outs):
    ctx = ExitStack()
    with ctx:
        sems = {}

        def sem(name):
            if name not in sems:
                sems[name] = ctx.enter_context(nc.semaphore(name))
            return sems[name]

        KB = 1024
        base = nc.sbuf_base
        base += (-base) % 64
        arena_bytes = nc.sbuf_usable_end - base - 256
        ctx.enter_context(nc.sbuf_tensor("arena", [P, (arena_bytes - 64) // 4], F32))
        at = [base + 64]

        def region(size):
            start = at[0]
            at[0] += size
            assert at[0] <= base + arena_bytes, (at[0] - base, arena_bytes)
            return start

        def place(name, shape, dtype, where, offset=0):
            return nc.alloc_sbuf_tensor_at(name, shape, dtype, offset=where + offset)

        def own(name, shape, dtype=F32):
            words = int(np.prod(shape[1:]))
            return place(name, shape, dtype, region((words * 4 + 31) // 32 * 32))

        raw = own("raw", [P, RAW, UNIT])
        w_hi = own("w_hi", [P, SPLIT, UNIT], F32R)
        w_lo = own("w_lo", [P, SPLIT, UNIT], F32R)
        X = own("X", [P, TILES, D])
        R_H, R_G, R_P, R_Y = region(24 * KB), region(24 * KB), region(36 * KB), region(12 * KB)
        R_S = region(9 * KB)
        const = own("const", [P, CONST.shape[1]])
        gate_bc = own("gate_bc", [P, 2, D])
        st_cond = own("st_cond", [P, KD, P], F32R)
        mod_col = own("mod_col", [P, 4, KD, 2])
        cols0 = own("cols0", [P, 96])
        cols1 = own("cols1", [P, 48])
        cond_f = own("cond_f", [P, 16])
        cond_hi = own("cond_hi", [P, 16], F32R)
        cond_lo = own("cond_lo", [P, 16], F32R)
        small = own("small", [P, 64])
        lg = own("lg", [P, 16])
        dec = own("dec", [P, 4, HEADS])
        cdec = own("cdec", [P, 2, 4])

        def cst(name):
            a, b = CONST_AT[name]
            return const[:, a:b]

        ident = cst("ident")

        hT = [place(f"hT_{x}", [P, KD, T_ALL], F32R, R_H, o * KB) for x, o in (("hi", 0), ("lo", 12))]
        qnT = [place(f"qnT_{x}", [P, KQ, T_ALL], F32R, R_H, o) for x, o in (("hi", 0), ("lo", 4608))]
        ckvT = [place(f"ckvT_{x}", [P, KKV, 4 * P], F32R, R_H, 9216 + o * KB) for x, o in (("hi", 0), ("lo", 4))]
        V23 = place("V23", [P, 2, HD], F32, R_H, 17408)
        mask = place("mask", [P, HEADS, P], F32, R_H, 0)
        mask_b = place("mask_b", [P, HEADS, P], F32, R_H, 4 * KB)
        k_dec = place("k_dec", [P, 4, HD], F32, R_H, 8 * KB)
        s0 = place("s0", [P, 2, 4, DV], F32, R_H, 16 * KB)
        s1 = place("s1", [P, 2, 4, DV], F32, R_H, 18 * KB)
        s_ctx = place("s_ctx", [P, 2, 4, DV], F32, R_H, 20 * KB)
        hn = place("hn", [P, HD], F32, R_H, 22 * KB)
        H_tok = [place(f"H_{x}", [P, TILES, D], F32R, R_H, o * KB) for x, o in (("hi", 0), ("lo", 12))]

        ln_rows = place("ln_rows", [P, 2, D], F32, R_G, 0)
        gate_bias = place("gate_bias", [P, D], F32, R_G, 8 * KB)
        m4 = place("m4", [P, 512], F32, R_G, 12 * KB)
        hf = place("hf", [P, 2, T_ALL], F32, R_G, 14 * KB)
        vec_rows = place("vec_rows", [P, 2, P], F32, R_G, 18 * KB)
        dec_rows = place("dec_rows", [P, 8, 16], F32, R_G, 20 * KB)
        qR = place("qR", [P, TILES, HEADS * ROPE], F32, R_G, 0)
        rope_tmp = place("rope_tmp", [P, TILES, HEADS * ROPE], F32, R_G, 3 * KB)
        qNT = place("qNT", [P, 4, T_ALL], F32, R_G, 6 * KB)
        qRT = place("qRT", [P, 2, T_ALL], F32, R_G, 12 * KB)
        kpe4 = place("kpe4", [P, 4, 4, ROPE], F32, R_G, 15 * KB)
        V01 = place("V01", [P, 2, HD], F32, R_G, 17 * KB)
        ret_tmp = place("ret_tmp", [P, HD], F32, R_G, 21 * KB)
        kpe_r = place("kpe_r", [P, 3, ROPE], F32, R_G, 23 * KB)
        rqT = place("rqT", [P, 4, T_ALL], F32, R_G, 0)
        rkT = place("rkT", [P, 4, T_ALL], F32, R_G, 6 * KB)
        qdT = place("qdT", [P, 2, 4, 2 * P], F32, R_G, 12 * KB)
        q_dec = place("q_dec", [P, 2, HD], F32, R_G, 20 * KB)
        gT = [place(f"gT_{x}", [P, KD, T_ALL], F32R, R_G, o * KB) for x, o in (("hi", 0), ("lo", 12))]

        proj = place("proj", [P, TILES, IN_EVEN], F32, R_P)
        kpeT = place("kpeT", [P, 4 * P], F32, R_P, 32640)
        mask_c = place("mask_c", [P, 4, P], F32, R_P, 34 * KB - 128)
        prodT = [place(f"prodT_{x}", [P, 12, T_ALL], F32R, R_P, o * KB) for x, o in (("hi", 0), ("lo", 18))]
        byT = [place(f"byT_{x}", [P, KD, T_ALL], F32R, R_P, o * KB) for x, o in (("hi", 0), ("lo", 12))]
        conv_c = place("conv_c", [P, 2, T_ALL], F32, R_P, 24 * KB)
        zpad = place("zpad", [P, 2, T_ALL + 4], F32, R_P, 27 * KB)
        conv_y = place("conv_y", [P, 2, T_ALL], F32, R_P, 31 * KB)
        hfT = place("hfT", [P, KD, T_ALL], F32, R_P, 0)
        rt = place("rt", [P, 12, TILES, N_EXP], F32, R_P, 24 * KB)
        mix = [place(f"mix_{x}", [P, TILES, HD], F32, R_Y, o * KB) for x, o in (("att", 0), ("ret", 6))]
        Y = place("Y", [P, TILES, D], F32, R_Y)
        mixT = [place(f"mixT_{x}", [P, KD, T_ALL], F32R, R_H, o * KB) for x, o in (("hi", 0), ("lo", 12))]
        kNT = place("kNT", [P, 4, 4 * P], F32, R_S)
        y_st = [place(f"y_{x}", [P, D], F32R, R_P, o * KB) for x, o in (("hi", 0), ("lo", 4))]
        E = place("E", [P, 2, 3 * P], F32, R_Y, 6 * KB)
        ET = place("ET", [P, 2, 3 * P], F32, R_Y, 9 * KB)
        ckv_c = place("ckv_c", [P, KV_LORA], F32, R_S, 0)
        kv_gain = place("kv_gain", [P, KV_LORA], F32, R_S, 1 * KB)
        junk = place("junk", [P, Q_LORA], F32, R_G, 3 * KB)
        prod = place("prod", [P, 3, PAIR], F32, R_S)
        sel = place("sel", [P, TILES, P], F32R, R_S, 3 * KB)
        ret_s = place("ret_s", [P, 2, 4, P], F32, R_S)
        selT = place("selT", [P, 3, T_ALL], F32R, R_S, 4608)
        rank_tab = place("rank_tab", [P, 2, P], F32, R_P, 28 * KB)
        ret_tab = place("ret_tab", [P, 2, TILES, DV], F32, R_Y)
        posm = own("posm", [P, TILES, N_EXP])
        comb = own("comb", [P, TILES, N_EXP])
        counts = own("counts", [P, 3, N_EXP], I32)
        rtr_w = own("rtr_w", [P, KD, N_EXP])
        rt_bias = own("rt_bias", [P, N_EXP])
        stats = own("stats", [P, TILES, 2, 6])
        mv = own("mv", [P, TILES, 4])
        den = own("den", [P, TILES, HEADS])
        mx = own("mx", [P, 2, 2])

        ps = ctx.enter_context(nc.psum_tensor("ps", [P, 8, 512], F32))

        block = ctx.enter_context(nc.Block())

        def val(k, per, e):
            return k if e is None else e * per + k

        def act_split(act, n, e=None):
            s = n % SPLIT
            act.wait_ge(sem(f"raw_landed{n % RAW}"), val(32 * (n // RAW + 1), 32 * FFN_UNITS // RAW, e))
            if n >= SPLIT:
                act.wait_ge(sem("w_used"), val(n - SPLIT + 1, FFN_UNITS, e))
            nc.scalar.copy(w_hi[:, s, 0:unit_words(n)], raw[:, n % RAW, 0:unit_words(n)]).then_inc(sem("w_hi_ready"), 1)

        def dve_split(dve, n, e=None):
            s, m = n % SPLIT, unit_words(n)
            dve.wait_ge(sem("w_hi_ready"), val(n + 1, FFN_UNITS, e))
            nc.vector.tensor_tensor(w_lo[:, s, 0:m], raw[:, n % RAW, 0:m], w_hi[:, s, 0:m].bitcast(F32),
                                    ALU.subtract).then_inc(sem("w_ready"), 1)

        def splitter(one):
            done = [0]

            def upto(n):
                while done[0] < min(n + AHEAD + 1, U_MOE + AHEAD):
                    one(done[0])
                    done[0] += 1
            return upto

        def split_in_loop(eng, one, u, e):
            v = u + AHEAD
            if v < FFN_UNITS:
                one(eng, U_MOE + v, e)

        class Weights:
            def __init__(self, pe, n, e=None):
                pe.wait_ge(sem("w_ready"), val(n + 1, FFN_UNITS, e))
                self.hi, self.lo = w_hi[:, n % SPLIT, :], w_lo[:, n % SPLIT, :]

            def used(self, ins):
                ins.then_inc(sem("w_used"), 1)

        def product3(out, a, b, start, stop, lanes=1):
            nc.tensor.matmul(out, a[0], b[0], start=start, stop=False)
            nc.tensor.matmul(out, a[0], b[1], start=False, stop=False)
            return nc.tensor.matmul(out, a[1], b[0], start=False, stop=stop)

        ckv_dst, kpe_dst = outs[2], outs[3]

        @block.sync
        def _(sp):
            def load(n, e=None):
                if n >= RAW:
                    sp.wait_ge(sem("w_ready"), val(n - RAW + 1, FFN_UNITS, e))
                _, parts = weight_unit(t, n, e)
                slot = raw[:, n % RAW, :]
                for where, nk, src in parts:
                    if nk is None:
                        dst = slot.rearrange("p (k s n) -> p k s n", k=4, s=2)[:, :, where, :]
                    else:
                        dst = slot[:, where[0]:where[1]].rearrange("p (k n) -> p k n", k=nk)
                    sp.dma_start(dst, src).then_inc(sem(f"raw_landed{n % RAW}"), 16)

            for n in range(U_MOE):
                load(n)
            with sp.Fori(0, N_EXP) as e:
                for u in range(FFN_UNITS):
                    load(U_MOE + u, e)
            for i in range(TILES):
                sp.wait_ge(sem("x_ready"), 3 * TILES + i + 1)
                dst = outs[0][0] if i == 0 else outs[1][0, (i - 1) * P:i * P, :]
                sp.dma_start(dst, X[:, i, :]).then_inc(sem("y_stored"), 16)
            sp.wait_ge(sem("y_stored"), 16 * TILES)

        def rope(tt, chain, dst, src, cos, sin, tmp):
            chain(tt(tmp[..., 0::2], src[..., 1::2], sin[..., 0::2], ALU.mult))
            chain(tt(tmp[..., 1::2], src[..., 0::2], sin[..., 1::2], ALU.mult))
            chain(tt(dst, src, cos, ALU.mult))
            return tt(dst, dst, tmp, ALU.add)

        @block.gpsimd
        def _(pool):
            step = [0]

            def chain(ins):
                step[0] += 1
                ins.then_inc(sem("pool_step"), 1)
                pool.wait_ge(sem("pool_step"), step[0])

            def get(dst, src, name):
                pool.dma_start(dst, src).then_inc(sem(name), 16)

            get(vec_rows[0:8, 0, :], t["c_ctx"].rearrange("(r n) -> r n", n=P), "rows_in")
            get(vec_rows[8:16, 0, :], t["c"].rearrange("b (r n) -> (b r) n", n=P), "rows_in")
            get(vec_rows[R_QG:R_QG + 3, 0, :], t["q_a_gain"].rearrange("b (r n) -> (b r) n", n=P), "rows_in")
            get(vec_rows[R_CONVW:R_CONVW + 24, 0, :], t["conv_w"].rearrange("a b (r n) -> (a b r) n", n=P), "rows_in")
            get(vec_rows[R_BMOD:R_BMOD + 48, 0, :], t["b_mod"][0].rearrange("(r n) -> r n", n=P), "rows_in")
            get(vec_rows[0:48, 1, :], t["b_mod"][1].rearrange("(r n) -> r n", n=P), "rows_in")
            get(const[:, :], t["const"], "const_in")
            get(X[:, 0, :], t["x_prompt"][0], "x_in")
            get(X[:, 1:3, :], t["x_sample"][0].rearrange("(t p) d -> p t d", p=P), "x_in")
            get(gate_bias[:, :], t["b_mod"][0][2 * D:3 * D].unsqueeze(0).broadcast_to([P, D]), "gbias_in")
            get(lg[:, 0:8], t["ret_decay_fwd"].broadcast_to([P, 8]), "dec_in")
            get(lg[:, 8:16], t["ret_decay_bwd"].broadcast_to([P, 8]), "dec_in")
            get(ckv_c[:, :], t["cache_ckv"][0, 0], "cache_in")
            get(kv_gain[:, :], t["kv_a_gain"].broadcast_to([P, KV_LORA]), "cache_in")
            get(ret_tab[:, :, :, :], t["ret_tables"].rearrange("p (a i d) -> p a i d", a=2, i=TILES), "ret_tab_in")
            get(rtr_w[:, :, :], t["router_w"][0].rearrange("(k p) n -> p k n", p=P), "rtr_in")
            get(rt_bias[:, :], t["router_b"].broadcast_to([P, N_EXP]), "rtr_in")
            get(mask_c[:, :, :], t["masks"].rearrange("p (a n) -> p a n", a=4), "mask_in")
            pool.wait_ge(sem("hT_ready"), KD)
            pool.wait_ge(sem("post_done"), MOD_POSTS[6])
            get(kpe4[:, 3, 0, :], t["cache_kpe"][0, 0], "kpe_in")

            pool.wait_ge(sem("rms_ms"), 1)
            pool.tensor_tensor(small[:, 8:14], small[:, 0:6], cst("mhalf")[:, 0:6], ALU.pow).then_inc(sem("rms_pow"), 1)
            pool.wait_ge(sem("ret_tab_in"), 16)
            for which, c0 in enumerate((C_RQ, C_RK)):
                pool.wait_ge(sem("proj_in"), 3 + which)
                for i in range(TILES):
                    v = proj[:, i, c0:c0 + HD].rearrange("p (h d) -> p h d", h=HEADS)
                    cs = ret_tab[:, 0, i:i + 1, :].broadcast_to([P, HEADS, DV])
                    sn = ret_tab[:, 1, i:i + 1, :].broadcast_to([P, HEADS, DV])
                    rope(pool.tensor_tensor, chain, v, v, cs, sn,
                         ret_tmp[:, :].rearrange("p (h d) -> p h d", h=HEADS)).then_inc(sem("ret_roped"), 1)
                    pool.wait_ge(sem("ret_roped"), which * TILES + i + 1)
            pool.wait_ge(sem("ckv_ready"), TILES)
            get(ckv_dst[0, 0], proj[:, 0, C_KV:C_KV + KV_LORA], "small_out")
            get(kpe_dst[0, 0], proj[:, 0, C_PE:C_PE + ROPE], "small_out")
            pool.wait_ge(sem("att_done"), TILES)
            for d_, name in enumerate(("state_ret_fwd", "state_ret_bwd")):
                for two in (0, 1):
                    get(s0[64 * two:64 * two + 64, d_, :, :],
                        t[name][0, 0].rearrange("(c two) d v -> two d c v", two=2)[two], "s0_in")
            for i in range(TILES):
                pool.wait_ge(sem("hn_var"), i + 1)
                pool.tensor_tensor(small[:, 24:32], small[:, 16:24], cst("mhalf"), ALU.pow).then_inc(sem("hn_pow"), 1)
            pool.wait_ge(sem("sctx_ready"), 2)
            for d_ in (0, 1):
                for two in (0, 1):
                    get(outs[4 + d_][0, 0].rearrange("(c two) d v -> two d c v", two=2)[two],
                        s_ctx[64 * two:64 * two + 64, d_, :, :], "small_out")
            for k in range(4):
                layer, sub = k // 2, k % 2
                if k == 3:
                    pool.wait_ge(sem("x_ready"), 3 * TILES)
                    get(rank_tab[:, :, :], t["ranks"].rearrange("p (a n) -> p a n", a=2), "ranks_in")
                if k == 0:
                    pool.wait_ge(sem("mix_ready"), TILES)
                elif k == 3:
                    pool.wait_ge(sem("moe_done"), 1)
                else:
                    pool.wait_ge(sem("x_ready"), TILES * k)
                for j, name in enumerate(("ln_g", "ln_b")):
                    get(ln_rows[:, j, :], t[name][layer, sub].unsqueeze(0).broadcast_to([P, D]), "ln_rows_in")
                if k < 3:
                    nl, nv = ((0, 5), (1, 2), (1, 5))[k]
                    pool.wait_ge(sem("post_done"), MOD_POSTS[6 * (k + 1)])
                    get(gate_bias[:, :], t["b_mod"][nl][nv * D:(nv + 1) * D].unsqueeze(0).broadcast_to([P, D]), "gbias_in")
                for i in range(TILES):
                    pool.wait_ge(sem("ln_var"), TILES * k + i + 1)
                    pool.tensor_tensor(mv[:, i, 3:4], mv[:, i, 2:3], cst("mhalf")[:, 0:1], ALU.pow).then_inc(sem("ln_pow"), 1)
            pool.wait_ge(sem("small_out"), 16 * 6)

        @block.tensor
        def _(pe):
            mm = nc.tensor.matmul

            def modulation(g, unit):
                if g >= 1:
                    pe.wait_ge(sem("m4_ready"), g)
                for half in (0, 1):
                    w = Weights(pe, unit + half)
                    for k in range(4):
                        kc, cols = 4 * half + k, slice(k * 512, (k + 1) * 512)
                        mm(ps[:, 6, :], st_cond[:, kc, :], w.hi[:, cols], start=kc == 0, stop=False)
                        last = mm(ps[:, 6, :], st_cond[:, kc, :], w.lo[:, cols], start=False, stop=kc == KD - 1)
                    if half == 0:
                        w.used(last)
                w.used(last)
                pe.wait_ge(sem("m4_ready"), g + 1)
                posts = MOD_POSTS[g]
                if posts >= 1:
                    pe.wait_ge(sem("post_done"), posts)
                if MOD_CHUNKS[g][1] % 3 == 2:
                    for cond in (0, 1):
                        if cond:
                            pe.wait_ge(sem("post_done"), posts + 1)
                        mm(ps[:, 7, :], cst("selrow")[:, cond * P:(cond + 1) * P], m4[:, :],
                           start=True, stop=True).then_inc(sem("post_ready"), 1)
                else:
                    for k in range(4):
                        last = mm(ps[:, 7, 2 * k:2 * k + 2], m4[:, k * P:(k + 1) * P], cst("selcol"),
                                  start=True, stop=True)
                    last.then_inc(sem("post_ready"), 1)

            def turn_x(first, count):
                for k in range(KD):
                    if k >= 2:
                        pe.wait_ge(sem("hf_ready"), first + k - 1)
                    for i in range(TILES):
                        if k == 0 and count:
                            pe.wait_ge(sem("x_ready"), count + i)
                        last = nc.tensor.transpose(ps[:, 4 + k % 2, i * P:(i + 1) * P], X[:, i, k * P:(k + 1) * P], ident)
                    last.then_inc(sem("xT_ready"), 1)

            pe.wait_ge(sem("rows_in"), 16 * 6)
            pe.wait_ge(sem("const_in"), 16)
            nc.tensor.transpose(ps[:, 0, 0:91], vec_rows[0:91, 0, :], ident[0:91, 0:91])
            nc.tensor.transpose(ps[:, 0, 96:144], vec_rows[0:48, 1, :], ident[0:48, 0:48]).then_inc(sem("cols_ready"), 1)
            pe.wait_ge(sem("cond_ready"), 4)
            for g in range(6):
                modulation(g, U_MODA0 + 2 * g)
            pe.wait_ge(sem("x_in"), 32)
            pe.wait_ge(sem("cols_done"), 2)
            turn_x(0, 0)

            n = U_PROJ
            for c, (_, width) in enumerate(PROJ_CHUNKS):
                if c >= 2:
                    pe.wait_ge(sem("proj_in"), c - 1)
                halves = [(0, KD)] if width < 512 else [(0, 4), (4, 8)]
                for a, b in halves:
                    w = Weights(pe, n)
                    if c == 0:
                        pe.wait_ge(sem("hT_ready"), b)
                    for i in range(TILES):
                        for k in range(a, b):
                            cols = slice((k - a) * width, (k - a + 1) * width)
                            last = product3(ps[:, (c % 2) * 3 + i, 0:width], [x[:, k, i * P:(i + 1) * P] for x in hT],
                                            (w.hi[:, cols], w.lo[:, cols]), k == 0, k == KD - 1)
                    w.used(last)
                    n += 1

            turned = 0

            def turn_bank():
                nonlocal turned
                if turned == 7:
                    pe.wait_ge(sem("lat_hi"), 6)
                elif turned >= 2:
                    pe.wait_ge(sem("lat_lo"), turned - 1)
                turned += 1
                return 6 + (turned - 1) % 2
            pe.wait_ge(sem("post_done"), MOD_POSTS[6])
            pe.wait_ge(sem("m4_ready"), 6)
            pe.wait_ge(sem("cache_in"), 32)
            pe.wait_ge(sem("ckv_ready"), TILES)
            for k in range(KKV):
                b = turn_bank()
                for i in range(4):
                    src = ckv_c[:, k * P:(k + 1) * P] if i == 3 else proj[:, i, C_KV + k * P:C_KV + (k + 1) * P]
                    last = nc.tensor.transpose(ps[:, b, i * P:(i + 1) * P], src, ident)
                last.then_inc(sem("lat_turned"), 1)
            for k in range(KQ):
                b = turn_bank()
                for i in range(TILES):
                    last = nc.tensor.transpose(ps[:, b, i * P:(i + 1) * P], proj[:, i, k * P:(k + 1) * P], ident)
                last.then_inc(sem("lat_turned"), 1)
            b = turn_bank()
            pe.wait_ge(sem("kpe4_ready"), 1)
            for i in range(4):
                last = nc.tensor.transpose(ps[:, b, i * P:(i + 1) * P],
                                           kpe4[:, i, :, :].rearrange("p r d -> p (r d)"), ident)
            last.then_inc(sem("lat_turned"), 1)

            outn = 0

            def mla_bank():
                nonlocal outn
                outn += 1
                if outn == 1:
                    pe.wait_ge(sem("proj_in"), 6)
                if outn > 6:
                    pe.wait_ge(sem("mla_in"), outn - 6)
                return (outn - 1) % 6
            w = Weights(pe, U_KV)
            pe.wait_ge(sem("lat_lo"), KKV)
            kv = [(w.hi[:, k * D:(k + 1) * D], w.lo[:, k * D:(k + 1) * D]) for k in range(KKV)]
            for i in range(4):
                b = mla_bank()
                for k in range(KKV):
                    last = product3(ps[:, b, :], [x[:, k, i * P:(i + 1) * P] for x in ckvT],
                                    [x[:, HD:2 * HD] for x in kv[k]], k == 0, k == KKV - 1)
                last.then_inc(sem("mla_out"), 1)
            for hp in range(4):
                b = mla_bank()
                for k in range(KKV):
                    last = product3(ps[:, b, :], [x[:, hp * P:(hp + 1) * P] for x in kv[k]],
                                    [x[:, k, :] for x in ckvT], k == 0, k == KKV - 1)
                if hp < 3:
                    last.then_inc(sem("mla_out"), 1)
            w.used(last)
            w = Weights(pe, U_QA)
            pe.wait_ge(sem("lat_lo"), KKV + KQ)
            for hp in range(4):
                b = mla_bank()
                for k in range(KQ):
                    cols = slice(k * HD + hp * P, k * HD + (hp + 1) * P)
                    last = product3(ps[:, b, 0:T_ALL], (w.hi[:, cols], w.lo[:, cols]),
                                    [x[:, k, :] for x in qnT], k == 0, k == KQ - 1)
                if hp < 3:
                    last.then_inc(sem("mla_out"), 1)
            w.used(last)
            w = Weights(pe, U_QB)
            for i in range(TILES):
                b = mla_bank()
                for k in range(KQ):
                    cols = slice(k * HEADS * ROPE, (k + 1) * HEADS * ROPE)
                    last = product3(ps[:, b, 0:HEADS * ROPE], [x[:, k, i * P:(i + 1) * P] for x in qnT],
                                    (w.hi[:, cols], w.lo[:, cols]), k == 0, k == KQ - 1)
                if i < TILES - 1:
                    last.then_inc(sem("mla_out"), 1)
            w.used(last)
            pe.wait_ge(sem("qR_ready"), TILES)
            for k in range(2):
                b = turn_bank()
                for i in range(TILES):
                    last = nc.tensor.transpose(ps[:, b, i * P:(i + 1) * P], qR[:, i, k * P:(k + 1) * P], ident)
                last.then_inc(sem("lat_turned"), 1)
            pe.wait_ge(sem("qRT_in"), 2)
            pe.wait_ge(sem("mla_in"), 15)

            items = [(i, h) for i in range(TILES) for h in range(HEADS)]

            def scores(m):
                i, h = items[m]
                keys = slice(0, P) if i == 0 else slice(P, 4 * P)
                nk = 1 if i == 0 else 3
                if m >= 2:
                    pe.wait_ge(sem("e_ready"), m - 1)
                rows, rr = slice(64 * (h % 2), 64 * (h % 2) + 64), slice(32 * (h % 4), 32 * (h % 4) + 32)
                mm(ps[:, m % 2, 0:nk * P], qNT[rows, h // 2, i * P:(i + 1) * P], kNT[rows, h // 2, keys],
                   start=True, stop=False)
                mm(ps[:, m % 2, 0:nk * P], qRT[rr, h // 4, i * P:(i + 1) * P], kpeT[rr, keys],
                   start=False, stop=True).then_inc(sem("s_ready"), 1)

            def turn_e(m):
                i, h = items[m]
                pe.wait_ge(sem("e_ready"), m + 1)
                if m >= 2:
                    pe.wait_ge(sem("eT_ready"), m - 1)
                for j in range(1 if i == 0 else 3):
                    last = nc.tensor.transpose(ps[:, 2 + m % 2, j * P:(j + 1) * P], E[:, m % 2, j * P:(j + 1) * P], ident)
                last.then_inc(sem("eT_turned"), 1)

            def values(m):
                i, h = items[m]
                pe.wait_ge(sem("eT_ready"), m + 1)
                tiles = [0] if i == 0 else [1, 2, 3]
                for j, kt in enumerate(tiles):
                    v = V01[:, kt, :] if kt < 2 else V23[:, kt - 2, :]
                    last = mm(ps[:, 4 + i, h * DV:(h + 1) * DV], ET[:, m % 2, j * P:(j + 1) * P],
                              v[:, h * DV:(h + 1) * DV], start=j == 0, stop=j == len(tiles) - 1)
                last.then_inc(sem("o_ready"), 1)

            for m in range(len(items) + 2):
                if m < len(items):
                    scores(m)
                if 0 <= m - 1 < len(items):
                    turn_e(m - 1)
                if m >= 2:
                    values(m - 2)

            pe.wait_ge(sem("ret_roped"), 2 * TILES)
            rturn = 0

            def ret_bank():
                nonlocal rturn
                if rturn >= 2:
                    pe.wait_ge(sem("ret_turned_in"), rturn - 1)
                rturn += 1
                return (rturn - 1) % 2
            for c0 in (C_RQ, C_RK):
                for k in range(4):
                    b = ret_bank()
                    for i in range(TILES):
                        last = nc.tensor.transpose(ps[:, b, i * P:(i + 1) * P], proj[:, i, c0 + k * P:c0 + (k + 1) * P], ident)
                    last.then_inc(sem("ret_turned"), 1)
            for i in (1, 2):
                for d_ in (0, 1):
                    b = ret_bank()
                    pe.wait_ge(sem("q_dec_ready"), 2 * (i - 1) + d_ + 1)
                    for k in range(4):
                        last = nc.tensor.transpose(ps[:, b, k * P:(k + 1) * P], q_dec[:, d_, k * P:(k + 1) * P], ident)
                    last.then_inc(sem("ret_turned"), 1)
            for j, i in enumerate((0, 0, 1, 2)):
                pe.wait_ge(sem("k_dec_ready"), j + 1)
                if j == 1 or j == 2:
                    pe.wait_ge(sem("sctx_ready"), j)
                elif j == 3:
                    pe.wait_ge(sem("state_in"), 1)
                for h in range(HEADS):
                    r = slice(64 * (h % 2), 64 * (h % 2) + 64)
                    last = mm(ps[r, 2, (h // 2) * DV:(h // 2 + 1) * DV], k_dec[:, j, h * DV:(h + 1) * DV],
                              proj[:, i, C_RV + h * DV:C_RV + (h + 1) * DV], start=True, stop=True)
                last.then_inc(sem("state_out"), 1)
            pe.wait_ge(sem("ret_turned_in"), 12)
            pe.wait_ge(sem("state_in"), 2)
            pe.wait_ge(sem("s0_in"), 16 * 4)
            pe.wait_ge(sem("att_done"), TILES)

            def ret_scores(m):
                i, parity = m // 2, m % 2
                if m >= 2:
                    pe.wait_ge(sem("rs_ready"), m - 1)
                for j in range(4):
                    h = 2 * j + parity
                    r = slice(64 * (h % 2), 64 * (h % 2) + 64)
                    last = mm(ps[:, m % 2, j * P:(j + 1) * P], rkT[r, h // 2, i * P:(i + 1) * P],
                              rqT[r, h // 2, i * P:(i + 1) * P], start=True, stop=True)
                last.then_inc(sem("rs_out"), 1)

            def ret_values(m):
                i, parity = m // 2, m % 2
                pe.wait_ge(sem("rs_ready"), m + 1)
                if parity:
                    pe.wait_ge(sem("ret_even"), i + 1)
                for j in range(4):
                    h = 2 * j + parity
                    r = slice(64 * (h % 2), 64 * (h % 2) + 64)
                    out = ps[:, 4 + i, h * DV:(h + 1) * DV]
                    last = mm(out, ret_s[:, m % 2, j, :], proj[:, i, C_RV + h * DV:C_RV + (h + 1) * DV],
                              start=True, stop=i == 0)
                    if i:
                        fwd, bwd = (s0, s1) if i == 1 else (s1, s0)
                        q = slice((i - 1) * P, i * P)
                        mm(out, qdT[r, 0, h // 2, q], fwd[r, 0, h // 2, :], start=False, stop=False)
                        last = mm(out, qdT[r, 1, h // 2, q], bwd[r, 1, h // 2, :], start=False, stop=True)
                last.then_inc(sem("ret_out" if parity else "ret_even"), 1)

            for m in range(7):
                if m < 6:
                    ret_scores(m)
                if m >= 1:
                    ret_values(m - 1)

            pe.wait_ge(sem("mix_ready"), TILES)
            for k in range(KD):
                if k >= 2:
                    pe.wait_ge(sem("mixT_ready"), k - 1)
                for i in range(TILES):
                    last = nc.tensor.transpose(ps[:, k % 2, i * P:(i + 1) * P], mix[k // 4][:, i, (k % 4) * P:(k % 4 + 1) * P], ident)
                last.then_inc(sem("mix_turned"), 1)

            def down(src, widths, unit, acc, tiles, first, last_phase, ready, e=None):
                k = 0
                for u, nk in enumerate(widths):
                    w = Weights(pe, unit + u, e)
                    for kk in range(nk):
                        ready(k)
                        for i in range(tiles):
                            for half in (0, 1):
                                cols = slice(kk * D + half * 512, kk * D + half * 512 + 512)
                                last = product3(ps[:, acc(i, half), :], [x[:, k, i * P:(i + 1) * P] for x in src],
                                                (w.hi[:, cols], w.lo[:, cols]), first and k == 0,
                                                last_phase and k == sum(widths) - 1)
                        k += 1
                    w.used(last)
                    yield u

            def all_banks(i, half):
                return 2 * i + half

            def ready_mix(k):
                if k == 0:
                    pe.wait_ge(sem("mixT_ready"), KD)

            for _ in down(mixT, [2] * 4, U_OUT0, all_banks, TILES, True, True, ready_mix):
                pass
            for g in range(6, 12):
                modulation(g, U_MODB0 + 2 * (g - 6))
            turn_x(KD, 1)

            def ffn(src, unit, tiles, e, before_down=None, after_phase=None):
                pairs0 = 0 if e is None else PAIRS
                per = None if e is None else PAIRS
                single = tiles == 1
                acc = (lambda i, half: 2 + half) if single else all_banks

                def turn_prod(c):
                    pe.wait_ge(sem("prod_ready"), val(pairs0 + c + 1, per, e))
                    prev = c - 1 if tiles == 3 else c - 2
                    if pairs0 + prev >= 0 and prev >= 0:
                        pe.wait_ge(sem("pT_lo"), val(pairs0 + prev + 1, per, e))
                    for i in range(tiles):
                        b = (7 if i == 2 else 6) if tiles == 3 else 6 + c % 2
                        o = (i % 2) * PAIR
                        for j in (0, 1):
                            last = nc.tensor.transpose(ps[:, b, o + j * P:o + (j + 1) * P], prod[:, i, j * P:(j + 1) * P], ident)
                    last.then_inc(sem("pT_turned"), 1)

                u = 0
                for phase in (0, 1):
                    pairs = PHASE_PAIRS[phase]
                    waiting = None
                    for c in pairs:
                        for half in (0, 1):
                            w = Weights(pe, unit + u, e)
                            for i in range(tiles):
                                b = (c + phase) % 2 * tiles + i
                                for k in range(4):
                                    cols = slice(k * 512, (k + 1) * 512)
                                    last = product3(ps[:, b, :], [x[:, 4 * half + k, i * P:(i + 1) * P] for x in src],
                                                    (w.hi[:, cols], w.lo[:, cols]), half == 0 and k == 0,
                                                    half == 1 and k == 3)
                            w.used(last)
                            u += 1
                            if half == 0 and waiting is not None:
                                turn_prod(waiting)
                        waiting = c
                    if not single:
                        pe.wait_ge(sem("prod_ready"), val(pairs0 + waiting + 1, per, e))
                    last_pair = waiting

                    def ready(k):
                        if k % 2 == 0:
                            pe.wait_ge(sem("pT_lo"), val(pairs0 + pairs[0] + k // 2 + 1, per, e))
                    for d_ in down(prodT, PHASE_DOWN[phase], unit + u, acc, tiles, phase == 0 or not single,
                                   phase == 1 or not single, ready, e):
                        if d_ == 0:
                            turn_prod(last_pair)
                    u += len(PHASE_DOWN[phase])
                    if after_phase:
                        after_phase(phase)

            def dense_phase(phase):
                if phase == 0:
                    pe.wait_ge(sem("dense_in"), 1)

            pe.wait_ge(sem("hT_ready"), 2 * KD)
            ffn(hT, U_FFN0, TILES, None, after_phase=dense_phase)

            for g in range(12, 18):
                modulation(g, U_MODA1 + 2 * (g - 12))
            turn_x(2 * KD, TILES + 1)
            pe.wait_ge(sem("hT_ready"), 3 * KD)
            m = 0
            for f in range(4):
                for third in range(3):
                    w = Weights(pe, U_CONV + 3 * f + third)
                    for j in (0, 1):
                        if f:
                            pe.wait_ge(sem(("conv_c_in", "z_ready", "by_ready")[third]), 2 * (f - 1) + j + 1)
                        for k in range(KD):
                            cols = slice(k * 256 + j * P, k * 256 + (j + 1) * P)
                            last = product3(ps[:, m % 6, 0:T_ALL], (w.hi[:, cols], w.lo[:, cols]),
                                            [x[:, k, :] for x in hT], k == 0, k == KD - 1)
                        m += 1
                        if j == 0:
                            last.then_inc(sem("conv_out"), 1)
                    w.used(last)
            def ready_conv(k):
                if k == 0:
                    pe.wait_ge(sem("by_lo"), KD)
            for _ in down(byT, [2] * 4, U_OUT1, all_banks, TILES, True, True, ready_conv):
                pass
            for g in range(18, 24):
                modulation(g, U_MODB1 + 2 * (g - 18))
            turn_x(3 * KD, 2 * TILES + 1)

            pe.wait_ge(sem("hf_ready"), 4 * KD)
            pe.wait_ge(sem("rtr_in"), 32)
            for i in range(TILES):
                for k in range(KD):
                    last = mm(ps[:, 2, i * N_EXP:(i + 1) * N_EXP], hfT[:, k, i * P:(i + 1) * P], rtr_w[:, k, :],
                              start=k == 0, stop=k == KD - 1)
            last.then_inc(sem("logits_out"), 1)
            n = 0
            for i in range(TILES):
                for q in (0, 1):
                    if n >= 2:
                        pe.wait_ge(sem("Ht_lo"), n - 1)
                    for k in range(4):
                        last = nc.tensor.transpose(ps[:, 4 + n % 2, k * P:(k + 1) * P],
                                                   hfT[:, 4 * q + k, i * P:(i + 1) * P], ident)
                    last.then_inc(sem("Ht_turned"), 1)
                    n += 1
            pe.wait_ge(sem("chosen"), 1)
            pe.wait_ge(sem("ranks_in"), 16)
            for i in range(TILES):
                for j in range(i + 1):
                    mm(ps[:, 3, i * N_EXP:(i + 1) * N_EXP], rank_tab[:, 0 if j == i else 1, :],
                       rt[:, 0, j, :], start=j == 0, stop=j == i)
            for j in range(TILES):
                last = mm(ps[:, 3, 3 * N_EXP:4 * N_EXP], rank_tab[:, 1, :], rt[:, 0, j, :], start=j == 0, stop=j == TILES - 1)
            last.then_inc(sem("ranks_out"), 1)

            pe.wait_ge(sem("counts_ready"), 2)
            pe.wait_ge(sem("post_done"), MOD_POSTS[24])
            pe.wait_ge(sem("Ht_hi"), 2 * TILES)
            pe.wait_ge(sem("Ht_lo"), 2 * TILES)
            pe.sem_inc(sem("g_out"), 1)
            pe.sem_inc(sem("y_out"), 1)
            with pe.Fori(0, N_EXP) as e:
                count = pe.value_load(counts[0:1, 0, ds(e, 1)], min_val=0, max_val=T_ALL)
                tiles0 = pe.value_load(counts[0:1, 1, ds(e, 1)], min_val=0, max_val=3 * N_EXP)
                scat0 = pe.value_load(counts[0:1, 2, ds(e, 1)], min_val=0, max_val=6 * N_EXP)

                def expert(tiles):
                    pe.wait_ge(sem("y_added"), scat0 * 6 + 6)
                    for s in range(tiles):
                        g = tiles0 + s
                        if s:
                            pe.wait_ge(sem("g_lo"), g * 2)
                            pe.wait_ge(sem("g_hi"), g * 2)
                        pe.wait_ge(sem("sel_ready"), g + 1)
                        for i in range(TILES):
                            last = nc.tensor.transpose(ps[:, 6, i * P:(i + 1) * P], sel[:, i, :].bitcast(F32), ident)
                        last.then_inc(sem("selT_out"), 1)
                        for q in (0, 1):
                            if q == 1:
                                pe.wait_ge(sem("selT_ready"), g + 1)
                            for x in (0, 1):
                                for k in range(4):
                                    kc = 4 * q + k
                                    for i in range(TILES):
                                        last = mm(ps[:, 4 + 2 * q + x, k * P:(k + 1) * P],
                                                  H_tok[x][:, i, kc * P:(kc + 1) * P], sel[:, i, :],
                                                  start=i == 0, stop=i == TILES - 1)
                            last.then_inc(sem("g_out"), 1)
                    pe.wait_ge(sem("g_lo"), tiles0 * 2 + 2 * tiles)
                    pe.wait_ge(sem("g_hi"), tiles0 * 2 + 2 * tiles)

                    def scatter(phase):
                        if tiles == 1 and phase == 0:
                            return
                        for s in range(tiles):
                            k = 0 if tiles == 1 else phase * tiles + s
                            q = scat0 + k
                            pe.wait_ge(sem("yst_lo"), q + 1)
                            for m in range(6):
                                i, half = m // 2, m % 2
                                pe.wait_ge(sem("y_added"), q * 6 + (m + 5))
                                b = (6 if tiles == 3 else 4) + m % 2
                                cols = slice(half * 512, half * 512 + 512)
                                mm(ps[:, b, :], selT[:, s, i * P:(i + 1) * P], y_st[0][:, cols], start=True, stop=False)
                                mm(ps[:, b, :], selT[:, s, i * P:(i + 1) * P], y_st[1][:, cols], start=False,
                                   stop=True).then_inc(sem("y_out"), 1)
                    ffn(gT, U_MOE, tiles, e, after_phase=scatter)

                with pe.If(count > P):
                    with pe.If(count > 2 * P):
                        expert(3)
                    with pe.Else():
                        expert(2)
                    pe.nop()
                with pe.Else():
                    expert(1)
                pe.nop()

        @block.scalar
        def _(act):
            split = splitter(lambda n: act_split(act, n))
            step = [0]

            def chain(ins):
                step[0] += 1
                ins.then_inc(sem("act_step"), 1)
                act.wait_ge(sem("act_step"), step[0])

            def modulation(g, unit):
                split(unit)
                split(unit + 1)
                act.wait_ge(sem("w_used"), unit + 2)
                nc.scalar.copy(m4[:, :], ps[:, 6, :]).then_inc(sem("m4_ready"), 1)

            def modulate(first, shift, scale, dst=None):
                for k in range(KD):
                    act.wait_ge(sem("xT_ready"), first + k + 1)
                    if dst is None:
                        if k >= 2:
                            act.wait_ge(sem("hT_ready"), first + k - 1)
                        out = hf[:, k % 2, :]
                    else:
                        out = dst[:, k, :]
                    for cond, cols in ((0, slice(0, P)), (1, slice(P, T_ALL))):
                        last = nc.scalar.activation(out[:, cols], ps[:, 4 + k % 2, cols], ACT.Identity,
                                                    bias=mod_col[:, shift, k, cond:cond + 1],
                                                    scale=mod_col[:, scale, k, cond:cond + 1])
                    last.then_inc(sem("hf_ready"), 1)

            act.wait_ge(sem("cols_ready"), 1)
            nc.scalar.copy(cols1[:, :], ps[:, 0, 96:144]).then_inc(sem("cols_done"), 1)
            nc.scalar.copy(cols0[:, 0:91], ps[:, 0, 0:91]).then_inc(sem("cols_done"), 1)
            act.wait_ge(sem("cols_done"), 2)
            chain(nc.scalar.activation(cond_f[:, :], cols0[:, 0:16], ACT.Silu))
            nc.scalar.copy(cond_hi[:, :], cond_f[:, :]).then_inc(sem("cond_hi"), 1)
            act.wait_ge(sem("lsig_in"), 1)
            nc.scalar.activation(small[:, 48:64], small[:, 32:48], ACT.Exp).then_inc(sem("lsig_exp"), 1)
            for g in range(6):
                modulation(g, U_MODA0 + 2 * g)
            act.wait_ge(sem("post_done"), MOD_POSTS[6])
            modulate(0, 0, 1)
            n = U_PROJ
            for c, (c0, width) in enumerate(PROJ_CHUNKS):
                n += 1 if width < 512 else 2
                for m in range(n - (1 if width < 512 else 2), n):
                    split(m)
                act.wait_ge(sem("w_used"), n)
                src = ps[:, (c % 2) * 3:(c % 2) * 3 + 3, 0:width]
                nc.scalar.activation(proj[:, :, c0:c0 + width], src, ACT.Copy,
                                     scale=RET_SCALE if c0 == C_RK else 1.0).then_inc(sem("proj_in"), 1)
                if c == 1:
                    act.wait_ge(sem("proj_in"), 2)
                    for i in range(TILES):
                        for j, (a, b) in enumerate(((C_Q, Q_LORA), (C_KV, KV_LORA))):
                            if i + j:
                                act.wait_ge(sem("rms_ss"), 2 * i + j)
                            nc.scalar.activation(junk[:, 0:b], proj[:, i, a:a + b], ACT.Square,
                                                 accum_out=small[:, 16 + 3 * j + i:17 + 3 * j + i]).then_inc(sem("rms_ss"), 1)
            act.wait_ge(sem("proj_in"), 6)
            for i in range(TILES):
                nc.scalar.activation(proj[:, i, C_RG:C_RG + HD], proj[:, i, C_RG:C_RG + HD], ACT.Silu).then_inc(sem("rg_ready"), 1)
            for m in range(KKV + KQ):
                act.wait_ge(sem("lat_turned"), m + 1)
                b = 6 + m % 2
                if m == 0:
                    act.wait_ge(sem("w_used"), U_KV)
                if m < KKV:
                    nc.scalar.copy(ckvT[0][:, m, :], ps[:, b, :]).then_inc(sem("lat_hi"), 1)
                else:
                    k = m - KKV
                    nc.scalar.activation(qnT[0][:, k, :], ps[:, b, 0:T_ALL], ACT.Copy,
                                         scale=cols0[:, R_QG + k:R_QG + k + 1]).then_inc(sem("lat_hi"), 1)
            act.wait_ge(sem("lat_turned"), 6)
            nc.scalar.copy(kpeT[:, :], ps[:, 7, :]).then_inc(sem("lat_hi"), 1)
            split(U_KV)
            for m in range(15):
                if m == 8:
                    split(U_QA)
                if m == 12:
                    split(U_QB)
                done = {7: U_KV, 11: U_QA, 14: U_QB}.get(m)
                if done is None:
                    act.wait_ge(sem("mla_out"), m + 1 - sum(m > x for x in (7, 11)))
                else:
                    act.wait_ge(sem("w_used"), done + 1)
                b = m % 6
                if m < 2:
                    nc.scalar.copy(V01[:, m, :], ps[:, b, :]).then_inc(sem("mla_in"), 1)
                elif m < 4:
                    nc.scalar.copy(V23[:, m - 2, :], ps[:, b, :]).then_inc(sem("mla_in"), 1)
                elif m < 8:
                    nc.scalar.copy(kNT[:, m - 4, :], ps[:, b, :]).then_inc(sem("mla_in"), 1)
                elif m < 12:
                    nc.scalar.copy(qNT[:, m - 8, :], ps[:, b, 0:T_ALL]).then_inc(sem("mla_in"), 1)
                else:
                    nc.scalar.copy(qR[:, m - 12, :], ps[:, b, 0:HEADS * ROPE]).then_inc(sem("mla_in"), 1)
            for k in range(2):
                act.wait_ge(sem("lat_turned"), 7 + k)
                nc.scalar.copy(qRT[:, k, :], ps[:, 6 + k % 2, 0:T_ALL]).then_inc(sem("qRT_in"), 1)
            for m in range(TILES * HEADS):
                i, h = m // HEADS, m % HEADS
                w_ = P if i == 0 else 3 * P
                act.wait_ge(sem("mx_ready"), m + 1)
                if m >= 2:
                    act.wait_ge(sem("eT_turned"), m - 1)
                nc.scalar.activation(E[:, m % 2, 0:w_], ps[:, m % 2, 0:w_], ACT.Exp, bias=mx[:, m % 2, 1:2],
                                     scale=ATT_SCALE, accum_out=den[:, i, h:h + 1]).then_inc(sem("e_ready"), 1)
            act.wait_ge(sem("att_done"), TILES)
            act.wait_ge(sem("lg_ready"), 1)
            act.wait_ge(sem("mask_in"), 16)
            for j, (a, d_) in enumerate(((0, 0), (1, 0), (2, 1), (3, 1))):
                nc.scalar.activation(dec[:, j, :], lg[:, 8 * d_:8 * d_ + 8], ACT.Exp, scale=cst("decay_at")[:, a:a + 1])
            for two in (0, 1):
                r = slice(64 * two, 64 * two + 64)
                last = nc.scalar.activation(cdec[r, :, :], lg[r, :].rearrange("p (d c two) -> p d c two", d=2, two=2)[:, :, :, two],
                                            ACT.Exp, scale=float(P))
            last.then_inc(sem("dec_ready"), 1)
            for h in range(HEADS):
                nc.scalar.activation(mask[:, h, :], mask_c[:, 0, :], ACT.Exp, scale=lg[:, h:h + 1])
                last = nc.scalar.activation(mask_b[:, h, :], mask_c[:, 1, :], ACT.Exp, scale=lg[:, 8 + h:9 + h])
            last.then_inc(sem("mask_exp"), 1)
            for m in range(12):
                act.wait_ge(sem("ret_turned"), m + 1)
                b = m % 2
                if m < 8:
                    dst = (rqT if m < 4 else rkT)[:, m % 4, :]
                    last = nc.scalar.copy(dst, ps[:, b, 0:T_ALL])
                else:
                    i, d_ = (m - 8) // 2, (m - 8) % 2
                    last = nc.scalar.copy(qdT[:, d_, :, i * P:(i + 1) * P], ps[:, b, :].rearrange("p (c n) -> p c n", c=4))
                last.then_inc(sem("ret_turned_in"), 1)
            for j in range(2):
                act.wait_ge(sem("state_out"), j + 1)
                nc.scalar.copy(s_ctx[:, j, :, :], ps[:, 2, 0:4 * DV].rearrange("p (c v) -> p c v", c=4)).then_inc(sem("sctx_ready"), 1)
            for k in range(KD):
                act.wait_ge(sem("mix_turned"), k + 1)
                if k == 0:
                    act.wait_ge(sem("small_out"), 16 * 6)
                nc.scalar.copy(mixT[0][:, k, :], ps[:, k % 2, 0:T_ALL]).then_inc(sem("mixT_hi"), 1)
            for u in range(4):
                split(U_OUT0 + u)
            for g in range(6, 12):
                modulation(g, U_MODB0 + 2 * (g - 6))
            act.wait_ge(sem("post_done"), MOD_POSTS[12])
            modulate(KD, 2, 3)

            def ffn(unit, tiles, e, splits, after_phase=None):
                pairs0 = 0 if e is None else PAIRS
                per = None if e is None else PAIRS

                def hidden_hi(c):
                    act.wait_ge(sem("pT_turned"), val(pairs0 + c + 1, per, e))
                    k = 2 * (c - PHASE_PAIRS[0 if c < 6 else 1][0])
                    for i in range(tiles):
                        b = (7 if i == 2 else 6) if tiles == 3 else 6 + c % 2
                        o = (i % 2) * PAIR
                        last = nc.scalar.copy(prodT[0][:, k:k + 2, i * P:(i + 1) * P],
                                              ps[:, b, o:o + PAIR].rearrange("p (j n) -> p j n", j=2))
                    last.then_inc(sem("pT_hi"), 1)
                u = 0
                for phase in (0, 1):
                    waiting = None
                    for c in PHASE_PAIRS[phase]:
                        for half in (0, 1):
                            splits(u)
                            u += 1
                            if half == 0 and waiting is not None:
                                hidden_hi(waiting)
                        waiting = c
                        act.wait_ge(sem("w_used"), val(unit + u, FFN_UNITS, e))
                        for i in range(tiles):
                            b = (c + phase) % 2 * tiles + i
                            last = nc.scalar.activation(prod[:, i, :], ps[:, b, 0:PAIR], ACT.Silu)
                        last.then_inc(sem("sg_ready"), 1)
                    for d_ in range(len(PHASE_DOWN[phase])):
                        splits(u)
                        u += 1
                        if d_ == 0:
                            hidden_hi(waiting)
                    if after_phase:
                        after_phase(phase, u)

            ffn(U_FFN0, TILES, None, lambda u: split(U_FFN0 + u))
            for g in range(12, 18):
                modulation(g, U_MODA1 + 2 * (g - 12))
            act.wait_ge(sem("post_done"), MOD_POSTS[18])
            modulate(2 * KD, 0, 1)
            for f in range(4):
                for third in range(3):
                    unit = U_CONV + 3 * f + third
                    split(unit)
                    for j in (0, 1):
                        m = 6 * f + 2 * third + j
                        if j == 0:
                            act.wait_ge(sem("conv_out"), 3 * f + third + 1)
                        else:
                            act.wait_ge(sem("w_used"), unit + 1)
                        if third == 0:
                            if f:
                                act.wait_ge(sem("z_ready"), 2 * (f - 1) + j + 1)
                            nc.scalar.copy(conv_c[:, j, :], ps[:, m % 6, 0:T_ALL]).then_inc(sem("conv_c_in"), 1)
                        if third == 2:
                            act.wait_ge(sem("by_ready"), 2 * f + j + 1)
                            nc.scalar.copy(byT[0][:, 2 * f + j, :], conv_y[:, j, :]).then_inc(sem("by_hi"), 1)
            for u in range(4):
                split(U_OUT1 + u)
            for g in range(18, 24):
                modulation(g, U_MODB1 + 2 * (g - 18))
            act.wait_ge(sem("post_done"), MOD_POSTS[24])
            modulate(3 * KD, 2, 3, dst=hfT)
            for n in range(2 * TILES):
                i, q = n // 2, n % 2
                act.wait_ge(sem("Ht_turned"), n + 1)
                nc.scalar.copy(H_tok[0][:, i, q * 512:(q + 1) * 512], ps[:, 4 + n % 2, :]).then_inc(sem("Ht_hi"), 1)
            act.wait_ge(sem("chosen_max"), 1)
            nc.scalar.activation(small[:, 8:8 + TILES], small[:, 0:TILES], ACT.Exp).then_inc(sem("gate_exp"), 1)
            act.wait_ge(sem("counts_ready"), 2)
            with act.Fori(0, N_EXP) as e:
                count = act.value_load(counts[0:1, 0, ds(e, 1)], min_val=0, max_val=T_ALL)
                tiles0 = act.value_load(counts[0:1, 1, ds(e, 1)], min_val=0, max_val=3 * N_EXP)
                scat0 = act.value_load(counts[0:1, 2, ds(e, 1)], min_val=0, max_val=6 * N_EXP)

                def expert(tiles):
                    for s in range(tiles):
                        g = tiles0 + s
                        act.wait_ge(sem("selT_out"), g + 1)
                        nc.scalar.copy(selT[:, s, :], ps[:, 6, 0:T_ALL]).then_inc(sem("selT_ready"), 1)
                        for q in (0, 1):
                            act.wait_ge(sem("g_out"), g * 2 + (q + 2))
                            nc.scalar.copy(gT[0][:, 4 * q:4 * q + 4, s * P:(s + 1) * P],
                                           ps[:, 4 + 2 * q, :].rearrange("p (k n) -> p k n", k=4)).then_inc(sem("g_hi"), 1)

                    def stage(phase, u):
                        if tiles == 1 and phase == 0:
                            return
                        act.wait_ge(sem("w_used"), val(U_MOE + u, FFN_UNITS, e))
                        for s in range(tiles):
                            k = 0 if tiles == 1 else phase * tiles + s
                            act.wait_ge(sem("y_out"), (scat0 + k) * 6 + 1)
                            b = 2 if tiles == 1 else 2 * s
                            nc.scalar.copy(y_st[0][:, :].rearrange("p (a n) -> p a n", a=2), ps[:, b:b + 2, :]).then_inc(sem("yst_hi"), 1)
                    ffn(U_MOE, tiles, e, lambda u: split_in_loop(act, act_split, u, e), after_phase=stage)

                with act.If(count > P):
                    with act.If(count > 2 * P):
                        expert(3)
                    with act.Else():
                        expert(2)
                    act.nop()
                with act.Else():
                    expert(1)
                with act.If(e < N_EXP - 1):
                    for v in range(AHEAD):
                        act_split(act, U_MOE + FFN_UNITS + v, e)
                act.nop()

        @block.vector
        def _(dve):
            split = splitter(lambda n: dve_split(dve, n))
            step = [0]
            tt, ts = nc.vector.tensor_tensor, nc.vector.tensor_scalar
            stt = nc.vector.scalar_tensor_tensor

            def chain(ins):
                step[0] += 1
                ins.then_inc(sem("dve_step"), 1)
                dve.wait_ge(sem("dve_step"), step[0])

            def modulation(g, unit):
                split(unit)
                split(unit + 1)
                layer, v, half = MOD_CHUNKS[g]
                bcol = (cols0[:, R_BMOD:R_BMOD + 48] if layer == 0 else cols1[:, :])
                if v % 3 == 2:
                    if half == 0:
                        dve.wait_ge(sem("gbias_in"), 16 * (g // 6 + 1))
                        if g > 6:
                            dve.wait_ge(sem("dve_step"), step[0])
                    for cond in (0, 1):
                        dve.wait_ge(sem("post_ready"), MOD_POSTS[g] + cond + 1)
                        cols = slice(half * 512, half * 512 + 512)
                        tt(gate_bc[:, cond, cols], ps[:, 7, :], gate_bias[:, cols], ALU.add).then_inc(sem("post_done"), 1)
                else:
                    dve.wait_ge(sem("post_ready"), MOD_POSTS[g] + 1)
                    b = bcol[:, v * KD + 4 * half:v * KD + 4 * half + 4].unsqueeze(2).broadcast_to([P, 4, 2])
                    src = ps[:, 7, 0:8].rearrange("p (k c) -> p k c", c=2)
                    slot = 2 * (v // 3) + v % 3
                    stt(mod_col[:, slot, 4 * half:4 * half + 4, :], src, float(v % 3), b, ALU.add, ALU.add).then_inc(sem("post_done"), 1)

            def split_h(first):
                for k in range(KD):
                    dve.wait_ge(sem("hf_ready"), first + k + 1)
                    nc.vector.tensor_copy(hT[0][:, k, :], hf[:, k % 2, :]).then_inc(sem("hT_hi"), 1)
                    dve.wait_ge(sem("hT_hi"), first + k + 1)
                    tt(hT[1][:, k, :], hf[:, k % 2, :], hT[0][:, k, :].bitcast(F32), ALU.subtract).then_inc(sem("hT_ready"), 1)

            def layer_norm(k, ready, src):
                for i in range(TILES):
                    ready(i)
                    cond = min(i, 1)
                    g = gate_bc[:, cond, :]
                    s = src(i)
                    y, g = (Y[:, i, :].rearrange("p (a n) -> p a n", a=2), g.rearrange("p (a n) -> p a n", a=2)) \
                        if len(s.shape) == 3 else (Y[:, i, :], g)
                    chain(tt(y, s, g, ALU.mult))
                    chain(stt(X[:, i, :], X[:, i, :], ALPHA, Y[:, i, :], ALU.mult, ALU.add))
                    for a in (0, 1):
                        chain(nc.vector.bn_stats(stats[:, i, a, :], X[:, i, a * 512:(a + 1) * 512]))
                    chain(nc.vector.bn_aggr(mv[:, i, 0:2], stats[:, i, :, :].rearrange("p a n -> p (a n)")))
                    ts(mv[:, i, 2:3], mv[:, i, 1:2], LN_EPS, None, ALU.add).then_inc(sem("ln_var"), 1)
                dve.wait_ge(sem("ln_rows_in"), 32 * (k + 1))
                for i in range(TILES):
                    dve.wait_ge(sem("ln_pow"), TILES * k + i + 1)
                    chain(ts(X[:, i, :], X[:, i, :], mv[:, i, 0:1], mv[:, i, 3:4], ALU.subtract, ALU.mult))
                    chain(tt(X[:, i, :], X[:, i, :], ln_rows[:, 0, :], ALU.mult))
                    tt(X[:, i, :], X[:, i, :], ln_rows[:, 1, :], ALU.add).then_inc(sem("x_ready"), 1)

            dve.wait_ge(sem("cond_hi"), 1)
            chain(tt(cond_lo[:, :], cond_f[:, :], cond_hi[:, :].bitcast(F32), ALU.subtract))
            for g, (src, o) in enumerate(((cond_hi, 0), (cond_lo, 0), (cond_hi, 8), (cond_lo, 8))):
                nc.vector.tensor_copy(st_cond[:, :, 32 * g:32 * g + 32],
                                      src[:, o:o + 8].bitcast(F32).unsqueeze(2).broadcast_to([P, KD, 32])).then_inc(sem("cond_ready"), 1)
            dve.wait_ge(sem("dec_in"), 32)
            chain(ts(small[:, 32:48], lg[:, :], -1.0, None, ALU.mult))
            chain(tt(small[:, 32:48], small[:, 32:48], lg[:, :], ALU.min))
            ts(small[:, 32:48], small[:, 32:48], 1.0, None, ALU.mult).then_inc(sem("lsig_in"), 1)
            dve.wait_ge(sem("lsig_exp"), 1)
            u_, s_ = small[:, 48:64], small[:, 32:48]
            chain(ts(s_, u_, 2.0, None, ALU.add))
            chain(nc.vector.reciprocal(s_, s_))
            chain(tt(u_, u_, s_, ALU.mult))
            chain(tt(s_, u_, u_, ALU.mult))
            pl = small[:, 0:16]
            chain(ts(pl, s_, 1.0 / 17, None, ALU.mult))
            for m in range(15, 1, -2):
                chain(stt(pl, pl, 1.0 / m, s_, ALU.add, ALU.mult))
            chain(stt(pl, pl, 1.0, u_, ALU.add, ALU.mult))
            chain(ts(lg[:, :], lg[:, :], 0.0, None, ALU.min))
            stt(lg[:, :], pl, -2.0, lg[:, :], ALU.mult, ALU.add).then_inc(sem("lg_ready"), 1)
            dve.wait_ge(sem("lg_ready"), 1)

            dve.wait_ge(sem("cols_done"), 2)
            for g in range(6):
                modulation(g, U_MODA0 + 2 * g)
            split_h(0)
            for m in range(U_PROJ, U_PROJ + 3):
                split(m)
            dve.wait_ge(sem("rms_ss"), 2 * TILES)
            chain(ts(small[:, 0:3], small[:, 16:19], 1.0 / Q_LORA, RMS_EPS, ALU.mult, ALU.add))
            ts(small[:, 3:6], small[:, 19:22], 1.0 / KV_LORA, RMS_EPS, ALU.mult, ALU.add).then_inc(sem("rms_ms"), 1)
            for m in range(U_PROJ + 3, U_KV):
                split(m)
            dve.wait_ge(sem("rms_pow"), 1)
            dve.wait_ge(sem("cache_in"), 32)
            cosq, sinq = (cst(x).rearrange("p (i d) -> p i d", i=TILES) for x in ("cos_q", "sin_q"))
            for i in range(TILES):
                stt(proj[:, i, C_KV:C_KV + KV_LORA], proj[:, i, C_KV:C_KV + KV_LORA], small[:, 11 + i:12 + i],
                    kv_gain[:, :], ALU.mult, ALU.mult)
                ts(proj[:, i, 0:Q_LORA], proj[:, i, 0:Q_LORA], small[:, 8 + i:9 + i], None, ALU.mult).then_inc(sem("ckv_ready"), 1)
            rope(tt, chain, kpe_r[:, :, :], proj[:, :, C_PE:C_PE + ROPE], cosq, sinq,
                 rope_tmp[:, :, 0:ROPE]).then_inc(sem("kpe_r"), 1)
            dve.wait_ge(sem("kpe_r"), 1)
            nc.vector.tensor_copy(kpe4[:, 0:3, :, :], kpe_r[:, :, :].unsqueeze(2).broadcast_to([P, 3, 4, ROPE]))
            dve.wait_ge(sem("kpe_in"), 16)
            nc.vector.tensor_copy(kpe4[:, 3, 1:4, :], kpe4[:, 3, 0:1, :].broadcast_to([P, 3, ROPE])).then_inc(sem("kpe4_ready"), 1)
            for m in range(KKV + KQ):
                dve.wait_ge(sem("lat_hi"), m + 1)
                b = 6 + m % 2
                if m < KKV:
                    tt(ckvT[1][:, m, :], ps[:, b, :], ckvT[0][:, m, :].bitcast(F32), ALU.subtract).then_inc(sem("lat_lo"), 1)
                else:
                    k = m - KKV
                    stt(qnT[1][:, k, :], ps[:, b, 0:T_ALL], cols0[:, R_QG + k:R_QG + k + 1],
                        qnT[0][:, k, :].bitcast(F32), ALU.mult, ALU.subtract).then_inc(sem("lat_lo"), 1)
            split(U_KV)
            split(U_QA)
            split(U_QB)
            for i in range(TILES):
                dve.wait_ge(sem("mla_in"), 13 + i)
                v = qR[:, i, :].rearrange("p (h d) -> p h d", h=HEADS)
                rope(tt, chain, v, v, cosq[:, i:i + 1, :].broadcast_to([P, HEADS, ROPE]),
                     sinq[:, i:i + 1, :].broadcast_to([P, HEADS, ROPE]),
                     rope_tmp[:, i, :].rearrange("p (h d) -> p h d", h=HEADS)).then_inc(sem("qR_ready"), 1)
            items = TILES * HEADS

            def maximum(m):
                w_ = P if m < HEADS else 3 * P
                dve.wait_ge(sem("s_ready"), m + 1)
                if m >= 2:
                    dve.wait_ge(sem("e_ready"), m - 1)
                nc.vector.tensor_reduce(mx[:, m % 2, 0:1], ps[:, m % 2, 0:w_], AX, ALU.max).then_inc(sem("mx_raw"), 1)
                dve.wait_ge(sem("mx_raw"), m + 1)
                ts(mx[:, m % 2, 1:2], mx[:, m % 2, 0:1], -ATT_SCALE, None, ALU.mult).then_inc(sem("mx_ready"), 1)

            def weights_in(m):
                w_ = P if m < HEADS else 3 * P
                dve.wait_ge(sem("eT_turned"), m + 1)
                if m >= 2:
                    dve.wait_ge(sem("o_ready"), m - 1)
                nc.vector.tensor_copy(ET[:, m % 2, 0:w_], ps[:, 2 + m % 2, 0:w_]).then_inc(sem("eT_ready"), 1)

            for m in range(items + 1):
                if m < items:
                    maximum(m)
                if m >= 1:
                    weights_in(m - 1)
            dve.wait_ge(sem("ret_roped"), 2 * TILES)
            for i in range(TILES):
                dve.wait_ge(sem("o_ready"), HEADS * (i + 1))
                dve.wait_ge(sem("e_ready"), HEADS * (i + 1))
                chain(nc.vector.reciprocal(den[:, i, :], den[:, i, :]))
                tt(mix[0][:, i, :].rearrange("p (h d) -> p h d", h=HEADS),
                   ps[:, 4 + i, :].rearrange("p (h d) -> p h d", h=HEADS),
                   den[:, i, :].unsqueeze(2).broadcast_to([P, HEADS, DV]), ALU.mult).then_inc(sem("att_done"), 1)

            heads = lambda ap: ap.rearrange("p (h d) -> p h d", h=HEADS)
            over = lambda j: dec[:, j, :].unsqueeze(2).broadcast_to([P, HEADS, DV])
            dve.wait_ge(sem("dec_ready"), 1)
            dve.wait_ge(sem("ret_roped"), 2 * TILES)
            dve.wait_ge(sem("att_done"), TILES)
            for j, (i, d_) in enumerate(((0, 1), (0, 2), (1, 1), (2, 2))):
                tt(heads(k_dec[:, j, :]), heads(proj[:, i, C_RK:C_RK + HD]), over(d_), ALU.mult).then_inc(sem("k_dec_ready"), 1)
            for i in (1, 2):
                for d_ in (0, 1):
                    if i == 2:
                        dve.wait_ge(sem("ret_turned"), 9 + d_)
                    tt(heads(q_dec[:, d_, :]), heads(proj[:, i, C_RQ:C_RQ + HD]), over(0 if d_ == 0 else 3),
                       ALU.mult).then_inc(sem("q_dec_ready"), 1)
            dve.wait_ge(sem("mask_exp"), 1)
            over_h = lambda j: mask_c[:, j:j + 1, :].broadcast_to([P, HEADS, P])
            chain(tt(mask[:, :, :], mask[:, :, :], over_h(2), ALU.mult))
            chain(tt(mask_b[:, :, :], mask_b[:, :, :], over_h(3), ALU.mult))
            chain(tt(mask[:, :, :], mask[:, :, :], mask_b[:, :, :], ALU.add))
            dve.wait_ge(sem("s0_in"), 16 * 4)
            for d_ in (0, 1):
                chain(tt(s1[:, d_, :, :], s0[:, d_, :, :], cdec[:, d_, :].unsqueeze(2).broadcast_to([P, 4, DV]), ALU.mult))
                dve.wait_ge(sem("state_out"), 3 + d_)
                tt(s1[:, d_, :, :], ps[:, 2, 0:4 * DV].rearrange("p (c v) -> p c v", c=4), s1[:, d_, :, :],
                   ALU.add).then_inc(sem("state_in"), 1)

            def masked(m):
                dve.wait_ge(sem("rs_out"), m + 1)
                tt(ret_s[:, m % 2, :, :], ps[:, m % 2, :].rearrange("p (j n) -> p j n", j=4),
                   mask[:, m % 2::2, :], ALU.mult).then_inc(sem("rs_ready"), 1)

            def head_norm(i):
                dve.wait_ge(sem("ret_out"), i + 1)
                sm = small[:, 16:24]
                chain(nc.vector.tensor_reduce(sm, heads(ps[:, 4 + i, :]), AX, ALU.add))
                chain(ts(sm, sm, 1.0 / DV, None, ALU.mult))
                y = heads(mix[1][:, i, :])
                chain(tt(y, heads(ps[:, 4 + i, :]), sm.unsqueeze(2).broadcast_to([P, HEADS, DV]), ALU.subtract))
                chain(tt(heads(hn[:, :]), y, y, ALU.mult))
                chain(nc.vector.tensor_reduce(sm, heads(hn[:, :]), AX, ALU.add))
                ts(sm, sm, 1.0 / DV, LN_EPS, ALU.mult, ALU.add).then_inc(sem("hn_var"), 1)
                chain(tt(y, y, heads(proj[:, i, C_RG:C_RG + HD]), ALU.mult))
                dve.wait_ge(sem("hn_pow"), i + 1)
                tt(y, y, small[:, 24:32].unsqueeze(2).broadcast_to([P, HEADS, DV]), ALU.mult).then_inc(sem("mix_ready"), 1)
                dve.wait_ge(sem("mix_ready"), i + 1)

            dve.wait_ge(sem("rg_ready"), TILES)
            for m in range(6):
                if m % 2 == 0 and m >= 2:
                    dve.wait_ge(sem("ret_out"), m // 2)
                masked(m)
                if m % 2 == 1 and m >= 3:
                    head_norm(m // 2 - 1)
            head_norm(2)
            for k in range(KD):
                dve.wait_ge(sem("mixT_hi"), k + 1)
                tt(mixT[1][:, k, :], ps[:, k % 2, 0:T_ALL], mixT[0][:, k, :].bitcast(F32), ALU.subtract).then_inc(sem("mixT_ready"), 1)
            for u in range(4):
                split(U_OUT0 + u)
            acc = lambda i: ps[:, 2 * i:2 * i + 2, :]
            layer_norm(0, lambda i: dve.wait_ge(sem("w_used"), U_MODB0), acc)
            for g in range(6, 12):
                modulation(g, U_MODB0 + 2 * (g - 6))
            split_h(KD)

            def ffn(unit, tiles, e, splits, after_phase):
                pairs0 = 0 if e is None else PAIRS
                per = None if e is None else PAIRS

                def hidden_lo(c):
                    dve.wait_ge(sem("pT_hi"), val(pairs0 + c + 1, per, e))
                    k = 2 * (c - PHASE_PAIRS[0 if c < 6 else 1][0])
                    for i in range(tiles):
                        b = (7 if i == 2 else 6) if tiles == 3 else 6 + c % 2
                        o = (i % 2) * PAIR
                        last = tt(prodT[1][:, k:k + 2, i * P:(i + 1) * P],
                                  ps[:, b, o:o + PAIR].rearrange("p (j n) -> p j n", j=2),
                                  prodT[0][:, k:k + 2, i * P:(i + 1) * P].bitcast(F32), ALU.subtract)
                    last.then_inc(sem("pT_lo"), 1)
                u = 0
                for phase in (0, 1):
                    waiting = None
                    for c in PHASE_PAIRS[phase]:
                        for half in (0, 1):
                            splits(u)
                            u += 1
                            if half == 0 and waiting is not None:
                                hidden_lo(waiting)
                        waiting = c
                        dve.wait_ge(sem("sg_ready"), val(pairs0 + c + 1, per, e))
                        for i in range(tiles):
                            b = (c + phase) % 2 * tiles + i
                            last = tt(prod[:, i, :], prod[:, i, :], ps[:, b, PAIR:2 * PAIR], ALU.mult)
                        last.then_inc(sem("prod_ready"), 1)
                    for d_ in range(len(PHASE_DOWN[phase])):
                        splits(u)
                        u += 1
                        if d_ == 0:
                            hidden_lo(waiting)
                    after_phase(phase, u)

            def dense_phase(phase, u):
                dve.wait_ge(sem("w_used"), U_FFN0 + u)
                for i in range(TILES):
                    y = Y[:, i, :].rearrange("p (a n) -> p a n", a=2)
                    last = nc.vector.tensor_copy(y, acc(i)) if phase == 0 else tt(y, acc(i), y, ALU.add)
                last.then_inc(sem("dense_in"), 1)
                dve.wait_ge(sem("dense_in"), phase + 1)
            ffn(U_FFN0, TILES, None, lambda u: split(U_FFN0 + u), dense_phase)
            layer_norm(1, lambda i: None, lambda i: Y[:, i, :])
            for g in range(12, 18):
                modulation(g, U_MODA1 + 2 * (g - 12))
            split_h(2 * KD)

            spans = ((0, 0, P), (P + 2, P, 2 * P))
            zz = zpad[:, :, :]
            for a in (0, P + 1, P + 2, T_ALL + 3):
                last = nc.vector.memset(zz[:, :, a:a + 1], 0.0)
                chain(last)
            cw = lambda tap, k: cols0[:, R_CONVW + tap * KD + k:R_CONVW + tap * KD + k + 1]
            for f in range(4):
                for third in range(3):
                    unit = U_CONV + 3 * f + third
                    split(unit)
                    for j in (0, 1):
                        m, k = 6 * f + 2 * third + j, 2 * f + j
                        bank = ps[:, m % 6, :]
                        if third == 1:
                            dve.wait_ge(sem("conv_c_in"), k + 1)
                            if j == 0:
                                dve.wait_ge(sem("conv_out"), 3 * f + third + 1)
                            else:
                                dve.wait_ge(sem("w_used"), unit + 1)
                            for z0, t0, nt in spans:
                                last = tt(zz[:, j, z0 + 1:z0 + 1 + nt], bank[:, t0:t0 + nt], conv_c[:, j, t0:t0 + nt], ALU.mult)
                            last.then_inc(sem("z_ready"), 1)
                            dve.wait_ge(sem("z_ready"), k + 1)
                            if f:
                                dve.wait_ge(sem("by_hi"), 2 * (f - 1) + j + 1)
                            for z0, t0, nt in spans:
                                y = conv_y[:, j, t0:t0 + nt]
                                chain(ts(y, zz[:, j, z0:z0 + nt], cw(0, k), None, ALU.mult))
                                chain(stt(y, zz[:, j, z0 + 1:z0 + 1 + nt], cw(1, k), y, ALU.mult, ALU.add))
                                chain(stt(y, zz[:, j, z0 + 2:z0 + 2 + nt], cw(2, k), y, ALU.mult, ALU.add))
                        elif third == 2:
                            if j == 0:
                                dve.wait_ge(sem("conv_out"), 3 * f + third + 1)
                            else:
                                dve.wait_ge(sem("w_used"), unit + 1)
                            tt(conv_y[:, j, :], bank[:, 0:T_ALL], conv_y[:, j, :], ALU.mult).then_inc(sem("by_ready"), 1)
                            dve.wait_ge(sem("by_hi"), k + 1)
                            tt(byT[1][:, k, :], conv_y[:, j, :], byT[0][:, k, :].bitcast(F32), ALU.subtract).then_inc(sem("by_lo"), 1)
            for u in range(4):
                split(U_OUT1 + u)
            layer_norm(2, lambda i: dve.wait_ge(sem("w_used"), U_MODB1), acc)
            for g in range(18, 24):
                modulation(g, U_MODB1 + 2 * (g - 18))

            for n in range(2 * TILES):
                i, q = n // 2, n % 2
                dve.wait_ge(sem("Ht_hi"), n + 1)
                tt(H_tok[1][:, i, q * 512:(q + 1) * 512], ps[:, 4 + n % 2, :],
                   H_tok[0][:, i, q * 512:(q + 1) * 512].bitcast(F32), ALU.subtract).then_inc(sem("Ht_lo"), 1)
            dve.wait_ge(sem("logits_out"), 1)
            R = lambda j: rt[:, j, :, :]
            per_tile = lambda ap: ap.unsqueeze(2).broadcast_to([P, TILES, N_EXP])
            b8 = lambda ap: ap.unsqueeze(1).broadcast_to([P, TILES, N_EXP])
            dve.wait_ge(sem("rtr_in"), 32)
            chain(tt(R(1), ps[:, 2, 0:24].rearrange("p (i n) -> p i n", i=TILES), b8(rt_bias[:, :]), ALU.add))
            m1, m2, ix = small[:, 32:35], small[:, 36:39], small[:, 40:43]

            def best(logits, top, eq, one):
                chain(nc.vector.tensor_reduce(top, logits, AX, ALU.max))
                chain(tt(eq, logits, per_tile(top), ALU.is_equal))
                chain(tt(eq, eq, b8(cst("rank8")), ALU.mult))
                chain(nc.vector.tensor_reduce(ix, eq, AX, ALU.max))
                chain(tt(one, eq, per_tile(ix), ALU.is_equal))
            best(R(1), m1, R(2), R(3))
            chain(stt(R(4), R(3), -1e30, R(1), ALU.mult, ALU.add))
            best(R(4), m2, R(2), R(5))
            tt(R(0), R(3), R(5), ALU.add).then_inc(sem("chosen"), 1)
            dve.wait_ge(sem("chosen"), 1)
            tt(small[:, 0:TILES], m2, m1, ALU.subtract).then_inc(sem("chosen_max"), 1)
            dve.wait_ge(sem("gate_exp"), 1)
            ex, w1 = small[:, 8:11], small[:, 16:19]
            chain(ts(w1, ex, 1.0, None, ALU.add))
            chain(nc.vector.reciprocal(w1, w1))
            chain(tt(ex, ex, w1, ALU.mult))
            chain(tt(R(3), R(3), per_tile(w1), ALU.mult))
            chain(tt(R(5), R(5), per_tile(ex), ALU.mult))
            chain(tt(comb[:, :, :], R(3), R(5), ALU.add))
            dve.wait_ge(sem("ranks_out"), 1)
            chain(stt(posm[:, :, :], ps[:, 3, 0:24].rearrange("p (i n) -> p i n", i=TILES), 1.0, R(0), ALU.add, ALU.mult))
            chain(ts(posm[:, :, :], posm[:, :, :], -1.0, None, ALU.add))
            cnt, big, huge, run = (rt[:, 6 + j, 0, :] for j in range(4))
            chain(nc.vector.tensor_copy(cnt, ps[:, 3, 24:32]))
            chain(ts(big, cnt, float(P), None, ALU.is_gt))
            chain(ts(huge, cnt, float(2 * P), None, ALU.is_gt))
            chain(nc.vector.tensor_copy(counts[:, 0, :], cnt))
            for row, (w_big, w_huge) in ((1, (1.0, 1.0)), (2, (3.0, 2.0))):
                chain(ts(run, huge, w_huge, 1.0, ALU.mult, ALU.add))
                chain(stt(run, big, w_big, run, ALU.mult, ALU.add))
                before = rt[:, 10 + row - 1, 0, :]
                chain(nc.vector.memset(before, 0.0))
                for e_ in range(1, N_EXP):
                    chain(tt(before[:, e_:e_ + 1], before[:, e_ - 1:e_], run[:, e_ - 1:e_], ALU.add))
                nc.vector.tensor_copy(counts[:, row, :], before).then_inc(sem("counts_ready"), 1)
            dve.wait_ge(sem("counts_ready"), 2)
            for m in range(6):
                nc.vector.memset(Y[:, m // 2, (m % 2) * 512:(m % 2) * 512 + 512], 0.0).then_inc(sem("y_added"), 1)

            with dve.Fori(0, N_EXP) as e:
                count = dve.value_load(counts[0:1, 0, ds(e, 1)], min_val=0, max_val=T_ALL)
                tiles0 = dve.value_load(counts[0:1, 1, ds(e, 1)], min_val=0, max_val=3 * N_EXP)
                scat0 = dve.value_load(counts[0:1, 2, ds(e, 1)], min_val=0, max_val=6 * N_EXP)

                def expert(tiles):
                    for s in range(tiles):
                        g = tiles0 + s
                        dve.wait_ge(sem("g_out"), g * 2 + 1)
                        for i in range(TILES):
                            last = ts(sel[:, i, :], cst("iota"), float(s * P), posm[:, i, ds(e, 1)], ALU.add, ALU.is_equal)
                        last.then_inc(sem("sel_ready"), 1)
                        for q in (0, 1):
                            dve.wait_ge(sem("g_out"), g * 2 + (q + 2))
                            nc.vector.tensor_copy(gT[1][:, 4 * q:4 * q + 4, s * P:(s + 1) * P],
                                                  ps[:, 5 + 2 * q, :].rearrange("p (k n) -> p k n", k=4)).then_inc(sem("g_lo"), 1)

                    def gather_back(phase, u):
                        if tiles == 1 and phase == 0:
                            return
                        for s in range(tiles):
                            k = 0 if tiles == 1 else phase * tiles + s
                            q = scat0 + k
                            b = 2 if tiles == 1 else 2 * s
                            dve.wait_ge(sem("yst_hi"), q + 1)
                            tt(y_st[1][:, :].rearrange("p (a n) -> p a n", a=2), ps[:, b:b + 2, :],
                               y_st[0][:, :].rearrange("p (a n) -> p a n", a=2).bitcast(F32), ALU.subtract).then_inc(sem("yst_lo"), 1)
                            for m in range(6):
                                i, half = m // 2, m % 2
                                bk = (6 if tiles == 3 else 4) + m % 2
                                y = Y[:, i, half * 512:half * 512 + 512]
                                dve.wait_ge(sem("y_added"), q * 6 + (m + 1))
                                dve.wait_ge(sem("y_out"), q * 6 + (m + 2))
                                stt(y, ps[:, bk, :], comb[:, i, ds(e, 1)], y, ALU.mult, ALU.add).then_inc(sem("y_added"), 1)
                    ffn(U_MOE, tiles, e, lambda u: split_in_loop(dve, dve_split, u, e), gather_back)

                with dve.If(count > P):
                    with dve.If(count > 2 * P):
                        expert(3)
                    with dve.Else():
                        expert(2)
                    dve.nop()
                with dve.Else():
                    expert(1)
                with dve.If(e < N_EXP - 1):
                    for v in range(AHEAD):
                        dve_split(dve, U_MOE + FFN_UNITS + v, e)
                dve.nop()
            dve.drain().then_inc(sem("moe_done"), 1)
            dve.wait_ge(sem("moe_done"), 1)
            layer_norm(3, lambda i: None, lambda i: Y[:, i, :])


_OUTS = [((1, 128, 1024), "float32"), ((1, 256, 1024), "float32"), ((1, 1, 128, 256), "float32"),
         ((1, 1, 128, 32), "float32"), ((1, 1, 8, 64, 64), "float32"), ((1, 1, 8, 64, 64), "float32")]


def kernel(**inputs):
    import concourse.bacc as bacc
    from concourse.bass_utils import run_bass_kernel_spmd

    nc = bacc.Bacc("TRN2", target_bir_lowering=False, num_devices=1)
    arrays = {k: np.ascontiguousarray(v) for k, v in inputs.items()}
    q = arrays["w_q_b"].reshape(1, Q_LORA, HEADS, NOPE + ROPE)
    arrays["w_q_b"] = np.concatenate([q[..., :NOPE].reshape(1, Q_LORA, -1), q[..., NOPE:].reshape(1, Q_LORA, -1)], -1)
    kv = arrays["w_kv_b"].reshape(1, KV_LORA, HEADS, NOPE + DV)
    arrays["w_kv_b"] = np.concatenate([kv[..., :NOPE].reshape(1, KV_LORA, -1), kv[..., NOPE:].reshape(1, KV_LORA, -1)], -1)
    arrays |= {"const": CONST, "masks": MASKS, "ret_tables": RET_TABLES, "ranks": RANKS}
    feed, t = {}, {}
    for name, a in arrays.items():
        feed[f"in_{name}"] = a
        t[name] = nc.dram_tensor(f"in_{name}", a.shape, mybir.dt.from_np(a.dtype), kind="ExternalInput").ap()
    outs = [nc.dram_tensor(f"out_{i}", s, mybir.dt.from_np(np.dtype(d)), kind="ExternalOutput").ap()
            for i, (s, d) in enumerate(_OUTS)]
    build(nc, t, outs)
    r = run_bass_kernel_spmd(nc, [feed], core_ids=[0])
    return tuple(r.results[0][f"out_{i}"] for i in range(len(_OUTS)))
```

```python
from contextlib import ExitStack

import numpy as np
import concourse.bass as bass
from concourse import mybir
from concourse.bass import ds

F32 = mybir.dt.float32
F32R = mybir.dt.float32r
I32 = mybir.dt.int32
ALU = mybir.AluOpType
ACT = mybir.ActivationFunctionType
AX = mybir.AxisListType.X

P = 128
D = 1024
KD = D // P
TILES = 3
T_ALL = TILES * P
PAST = 128
Q_LORA, KV_LORA, ROPE, NOPE, HEADS, DV = 384, 256, 32, 64, 8, 64
HD = HEADS * DV
KQ, KKV = Q_LORA // P, KV_LORA // P
IN_EVEN = Q_LORA + KV_LORA + ROPE + 4 * HD
FF = 2816
N_EXP = 8
GRID_W = 64
ALPHA = (2.0 * 2) ** 0.25
ATT_SCALE = float(NOPE + ROPE) ** -0.5
RET_SCALE = float(DV) ** -0.5
LN_EPS, RMS_EPS = 1e-5, 1e-6

C_Q, C_KV, C_PE = 0, Q_LORA, Q_LORA + KV_LORA
C_RQ = C_PE + ROPE
C_RK, C_RV, C_RG = C_RQ + HD, C_RQ + 2 * HD, C_RQ + 3 * HD
PROJ_CHUNKS = [(0, 512), (512, C_RQ - 512), (C_RQ, 512), (C_RK, 512), (C_RV, 512), (C_RG, 512)]

UNIT = 2048
RAW = 3
SPLIT = 3
AHEAD = 2

PAIR = 256
PAIRS = FF // PAIR
PHASE_PAIRS = [range(0, 6), range(6, PAIRS)]
PHASE_DOWN = [[2] * len(p) for p in PHASE_PAIRS]
FFN_UNITS = 3 * PAIRS
GATHER_AT = FFN_UNITS - 5

MOD_CHUNKS = [(layer, v, h) for layer in (0, 1) for v in range(6) for h in (0, 1)]
MOD_FIRST = [0, 1, 2, 3]
MOD_AFTER_PROJ = [[4, 5], [6], [7, 8], [9, 12], [13, 14], [15]]
MOD_IN_FFN = [10, 11]
MOD_AFTER_CONV = [[16, 17], [18, 19], [20], [21]]
MOD_LAST = [22, 23]
MOD_ORDER = (MOD_FIRST + sum(MOD_AFTER_PROJ, []) + MOD_IN_FFN + sum(MOD_AFTER_CONV, []) + MOD_LAST)
MOD_POSTS = [sum(2 if MOD_CHUNKS[g][1] % 3 == 2 else 1 for g in MOD_ORDER[:i]) for i in range(len(MOD_ORDER) + 1)]
GATE_PLACE = [MOD_ORDER.index(g) for g in (4, 10, 16, 22)]
FFN_PHASE0 = 2 * len(PHASE_PAIRS[0]) + len(PHASE_DOWN[0])


def _stream():
    out, at = [], {}

    def add(name, n, key=None):
        at[name if key is None else (name, key)] = len(out)
        out.extend((name, key, i) for i in range(n))

    def mods(chunks):
        for g in chunks:
            add("mod", 2, g)
    mods(MOD_FIRST)
    for c, (_, width) in enumerate(PROJ_CHUNKS):
        add("proj", 2 if width == 512 else 1, c)
        mods(MOD_AFTER_PROJ[c])
    add("kv", 1), add("qa", 1), add("qb", 1), add("out0", 4)
    add("ffn", FFN_PHASE0, 0)
    mods(MOD_IN_FFN)
    add("ffn", FFN_UNITS - FFN_PHASE0, 1)
    for f in range(4):
        add("conv", 3, f)
        mods(MOD_AFTER_CONV[f])
    add("out1", 4)
    mods(MOD_LAST)
    return out, at


STREAM, AT = _stream()
U_MOE = len(STREAM)
U_KV, U_QA, U_QB, U_OUT0, U_OUT1 = (AT[x] for x in ("kv", "qa", "qb", "out0", "out1"))
assert FFN_UNITS % RAW == 0 and FFN_UNITS % SPLIT == 0


def dense_unit(u):
    return AT["ffn", 0] + u if u < FFN_PHASE0 else AT["ffn", 1] + u - FFN_PHASE0


def expert_unit(u):
    return U_MOE + u


R_COND, R_QG, R_CONVW, R_BMOD = 0, 16, 19, 43


def _constants():
    i = np.arange(P, dtype=np.float32)
    row, col = i[:, None], i[None, :]
    parts = {}
    parts["ident"] = np.eye(P, dtype=np.float32)
    parts["iota"] = np.broadcast_to(col, (P, P)).astype(np.float32)
    sel = np.zeros((P, 2, P), np.float32)
    sel[[0, 32], 0] = 1.0
    sel[[64, 96], 1] = 1.0
    parts["selrow"] = sel.reshape(P, -1)
    parts["selcol"] = np.ascontiguousarray(sel[:, :, 0])
    parts["decay_at"] = np.stack([i + 1, P - 1 - i, i, P - i], 1)
    parts["rank8"] = np.broadcast_to(100.0 - np.arange(8, dtype=np.float32), (P, 8)).astype(np.float32)
    parts["mhalf"] = np.full((P, 8), -0.5, np.float32)

    def tables(cos, sin):
        n = cos.shape[1]
        c = np.ones((TILES, P, 2 * n), np.float32)
        s = np.zeros((TILES, P, 2 * n), np.float32)
        c[1:] = np.repeat(cos, 2, axis=1).reshape(2, P, 2 * n)
        s[1:, :, 0::2] = -sin.reshape(2, P, n)
        s[1:, :, 1::2] = sin.reshape(2, P, n)
        return (a.transpose(1, 0, 2).reshape(P, -1) for a in (c, s))

    tok = np.arange(2 * P)
    n_freq = ROPE // 4
    freqs = (1.0 / (np.float32(10000.0) ** (np.arange(n_freq, dtype=np.float32) / n_freq))).astype(np.float32)
    r, c = (tok // GRID_W).astype(np.float32), (tok % GRID_W).astype(np.float32)
    ang = np.concatenate([r[:, None] * freqs, c[:, None] * freqs], -1)
    parts["cos_q"], parts["sin_q"] = tables(np.cos(ang), np.sin(ang))
    theta = (1.0 / (np.float32(10000.0) ** np.linspace(0.0, 1.0, DV // 2, dtype=np.float32))).astype(np.float32)
    ang = tok.astype(np.float32)[:, None] * theta
    ret_tables = np.concatenate(list(tables(np.cos(ang), np.sin(ang))), 1)
    ranks = np.concatenate([(row < col).astype(np.float32), np.ones((P, P), np.float32)], 1)
    at, cols = 0, {}
    for k, v in parts.items():
        cols[k] = (at, at + v.shape[1])
        at += v.shape[1]
    masks = np.concatenate([np.maximum(col - row, 0), np.maximum(row - col, 0),
                            (col >= row), (row >= col)], 1).astype(np.float32)
    return np.concatenate(list(parts.values()), 1).astype(np.float32), cols, masks, ret_tables, ranks


CONST, CONST_AT, MASKS, RET_TABLES, RANKS = _constants()


def weight_unit(w, n, expert=None):
    def chunk(mat, c0, width, k0, nk):
        half = (nk + 1) // 2
        src = mat.rearrange("(k p) n -> p k n", p=P)
        return nk * width, [((a * width, b * width), b - a, src[:, k0 + a:k0 + b, c0:c0 + width])
                            for a, b in ((0, half), (half, nk))]

    def rows(mat, k0, nk):
        src = mat.rearrange("(k p) n -> p k n", p=P)
        if nk == 2:
            return 2 * D, [((a * D, (a + 1) * D), 1, src[:, k0 + a:k0 + a + 1, :]) for a in (0, 1)]
        return D, [((a * 512, (a + 1) * 512), 1, src[:, k0:k0 + 1, a * 512:(a + 1) * 512]) for a in (0, 1)]

    def mod(layer, i):
        return chunk(w["w_mod"][layer], (i // 2) * 512, 512, 4 * (i % 2), 4)

    def ffn(gate, up, down, i):
        for phase in (0, 1):
            pairs, downs = PHASE_PAIRS[phase], PHASE_DOWN[phase]
            if i < 2 * len(pairs):
                c, k0 = pairs[i // 2] * PAIR, 4 * (i % 2)
                return UNIT, [(s, None, m.rearrange("(k p) n -> p k n", p=P)[:, k0:k0 + 4, c:c + PAIR])
                              for s, m in enumerate((gate, up))]
            i -= 2 * len(pairs)
            if i < len(downs):
                return rows(down, 2 * pairs[0] + sum(downs[:i]), downs[i])
            i -= len(downs)

    if n >= U_MOE:
        return ffn(w["exp_gate"][0][expert], w["exp_up"][0][expert], w["exp_down"][0][expert], n - U_MOE)
    name, key, i = STREAM[n]
    if name == "mod":
        layer, v, half = MOD_CHUNKS[key]
        return chunk(w["w_mod"][layer], (2 * v + half) * 512, 512, 4 * i, 4)
    if name == "proj":
        c0, width = PROJ_CHUNKS[key]
        return chunk(w["w_in_mix"][0], c0, width, 4 * i, 4 if width == 512 else KD)
    if name == "kv":
        return rows(w["w_kv_b"][0], 0, 2)
    if name == "qa":
        return chunk(w["w_q_b"][0], 0, HD, 0, KQ)
    if name == "qb":
        return chunk(w["w_q_b"][0], HD, HEADS * ROPE, 0, KQ)
    if name == "ffn":
        return ffn(w["ffn_gate"][0], w["ffn_up"][0], w["ffn_down"][0], i + FFN_PHASE0 * key)
    if name == "conv":
        return chunk(w["w_in_conv"][0], (1, 2, 0)[i] * D + key * 256, 256, 0, KD)
    return rows(w["w_out_mix" if name == "out0" else "w_out_conv"][0], 2 * i, 2)


def unit_words(n):
    name, key, i = STREAM[n] if n < U_MOE else ("moe", None, n - U_MOE)
    if name in ("ffn", "moe"):
        i += FFN_PHASE0 if key == 1 else 0
        for phase in (0, 1):
            if i < 2 * len(PHASE_PAIRS[phase]):
                return UNIT
            i -= 2 * len(PHASE_PAIRS[phase])
            if i < len(PHASE_DOWN[phase]):
                return PHASE_DOWN[phase][i] * D
            i -= len(PHASE_DOWN[phase])
        return UNIT
    if name == "proj" and PROJ_CHUNKS[key][1] < 512:
        return KD * PROJ_CHUNKS[key][1]
    return {"qa": KQ * HD, "qb": KQ * HEADS * ROPE}.get(name, UNIT)


def build(nc, t, outs):
    ctx = ExitStack()
    with ctx:
        sems = {}

        def sem(name):
            if name not in sems:
                sems[name] = ctx.enter_context(nc.semaphore(name))
            return sems[name]

        KB = 1024
        base = nc.sbuf_base
        base += (-base) % 64
        arena_bytes = nc.sbuf_usable_end - base - 256
        ctx.enter_context(nc.sbuf_tensor("arena", [P, (arena_bytes - 64) // 4], F32))
        at = [base + 64]

        def region(size):
            start = at[0]
            at[0] += size
            assert at[0] <= base + arena_bytes, (at[0] - base, arena_bytes)
            return start

        def place(name, shape, dtype, where, offset=0):
            return nc.alloc_sbuf_tensor_at(name, shape, dtype, offset=where + offset)

        def own(name, shape, dtype=F32):
            words = int(np.prod(shape[1:]))
            return place(name, shape, dtype, region((words * 4 + 31) // 32 * 32))

        raw = own("raw", [P, RAW, UNIT])
        w_hi = own("w_hi", [P, SPLIT, UNIT], F32R)
        w_lo = own("w_lo", [P, SPLIT, UNIT], F32R)
        X = own("X", [P, TILES, D])
        R_H, R_G, R_P, R_Y = region(24 * KB), region(24 * KB), region(36 * KB), region(12 * KB)
        R_S = region(9 * KB)
        const = own("const", [P, CONST.shape[1]])
        gate_bc = own("gate_bc", [P, 2, D])
        st_cond = own("st_cond", [P, KD, P], F32R)
        mod_col = own("mod_col", [P, 8, KD, 2])
        cols0 = own("cols0", [P, 96])
        cols1 = own("cols1", [P, 96])
        cond_f = own("cond_f", [P, 16])
        cond_hi = own("cond_hi", [P, 16], F32R)
        cond_lo = own("cond_lo", [P, 16], F32R)
        small = own("small", [P, 64])
        lg = own("lg", [P, 16])
        dec = own("dec", [P, 4, HEADS])
        cdec = own("cdec", [P, 2, 4])

        def cst(name):
            a, b = CONST_AT[name]
            return const[:, a:b]

        ident = cst("ident")

        hT = [place(f"hT_{x}", [P, KD, T_ALL], F32R, R_H, o * KB) for x, o in (("hi", 0), ("lo", 12))]
        qnT = [place(f"qnT_{x}", [P, KQ, T_ALL], F32R, R_H, o) for x, o in (("hi", 0), ("lo", 4608))]
        ckvT = [place(f"ckvT_{x}", [P, KKV, 4 * P], F32R, R_H, 9216 + o * KB) for x, o in (("hi", 0), ("lo", 4))]
        V23 = place("V23", [P, 2, HD], F32, R_H, 17408)
        mask = place("mask", [P, HEADS, P], F32, R_H, 0)
        mask_b = place("mask_b", [P, HEADS, P], F32, R_H, 4 * KB)
        k_dec = place("k_dec", [P, 4, HD], F32, R_H, 8 * KB)
        s0 = place("s0", [P, 2, 4, DV], F32, R_H, 16 * KB)
        s1 = place("s1", [P, 2, 4, DV], F32, R_H, 18 * KB)
        s_ctx = place("s_ctx", [P, 2, 4, DV], F32, R_H, 20 * KB)
        hn = place("hn", [P, HD], F32, R_H, 22 * KB)
        H_tok = [place(f"H_{x}", [P, TILES, D], F32R, R_H, o * KB) for x, o in (("hi", 0), ("lo", 12))]

        last_rows = place("last_rows", [P, 2, D], F32, R_H, 0)

        ln_rows = place("ln_rows", [P, 2, D], F32, R_G, 0)
        gate_bias = place("gate_bias", [P, D], F32, R_G, 8 * KB)
        m4 = place("m4", [P, 512], F32, R_G, 12 * KB)
        hf = place("hf", [P, 2, T_ALL], F32, R_G, 14 * KB)
        vec_rows = place("vec_rows", [P, 2, P], F32, R_G, 18 * KB)
        dec_rows = place("dec_rows", [P, 8, 16], F32, R_G, 20 * KB)
        qR = place("qR", [P, TILES, HEADS * ROPE], F32, R_G, 0)
        rope_tmp = place("rope_tmp", [P, TILES, HEADS * ROPE], F32, R_G, 3 * KB)
        qNT = place("qNT", [P, 4, T_ALL], F32, R_G, 6 * KB)
        qRT = place("qRT", [P, 2, T_ALL], F32, R_G, 12 * KB)
        kpe4 = place("kpe4", [P, 4, 4, ROPE], F32, R_G, 15 * KB)
        V01 = place("V01", [P, 2, HD], F32, R_G, 17 * KB)
        ret_tmp = place("ret_tmp", [P, HD], F32, R_G, 21 * KB)
        kpe_r = place("kpe_r", [P, 3, ROPE], F32, R_G, 23 * KB)
        rqT = place("rqT", [P, 4, T_ALL], F32, R_G, 0)
        rkT = place("rkT", [P, 4, T_ALL], F32, R_G, 6 * KB)
        qdT = place("qdT", [P, 2, 4, 2 * P], F32, R_G, 12 * KB)
        q_dec = place("q_dec", [P, 2, HD], F32, R_G, 20 * KB)
        gT = [place(f"gT_{x}", [P, KD, T_ALL], F32R, R_G, o * KB) for x, o in (("hi", 0), ("lo", 12))]

        proj = place("proj", [P, TILES, IN_EVEN], F32, R_P)
        kpeT = place("kpeT", [P, 4 * P], F32, R_P, 32640)
        mask_c = place("mask_c", [P, 4, P], F32, R_P, 34 * KB - 128)
        prodT = [place(f"prodT_{x}", [P, 12, T_ALL], F32R, R_P, o * KB) for x, o in (("hi", 0), ("lo", 18))]
        byT = [place(f"byT_{x}", [P, KD, T_ALL], F32R, R_P, o * KB) for x, o in (("hi", 0), ("lo", 12))]
        conv_c = place("conv_c", [P, 2, T_ALL], F32, R_P, 24 * KB)
        zpad = place("zpad", [P, 2, T_ALL + 4], F32, R_P, 27 * KB)
        conv_y = place("conv_y", [P, 2, T_ALL], F32, R_P, 31 * KB)
        hfT = place("hfT", [P, KD, T_ALL], F32, R_P, 0)
        rt = place("rt", [P, 12, TILES, N_EXP], F32, R_P, 24 * KB)
        mix = [place(f"mix_{x}", [P, TILES, HD], F32, R_Y, o * KB) for x, o in (("att", 0), ("ret", 6))]
        Y = place("Y", [P, TILES, D], F32, R_Y)
        mixT = [place(f"mixT_{x}", [P, KD, T_ALL], F32R, R_H, o * KB) for x, o in (("hi", 0), ("lo", 12))]
        kNT = place("kNT", [P, 4, 4 * P], F32, R_S)
        y_st = [place(f"y_{x}", [P, 4, PAIR], F32R, R_P, o * KB) for x, o in (("hi", 0), ("lo", 4))]
        y_last = [gT[0][:, 4 * x:4 * x + 4, P:T_ALL] for x in (0, 1)]
        g_rows = place("g_rows", [P, KD, T_ALL], F32, R_G, 12 * KB)[:, 0:4, P:T_ALL]
        g_rows_more = place("g_rows_more", [P, 4, PAIR], F32, R_P, 8 * KB)
        E = place("E", [P, 2, 3 * P], F32, R_Y, 6 * KB)
        ET = place("ET", [P, 2, 3 * P], F32, R_Y, 9 * KB)
        ckv_c = place("ckv_c", [P, KV_LORA], F32, R_S, 0)
        kv_gain = place("kv_gain", [P, KV_LORA], F32, R_S, 1 * KB)
        junk = place("junk", [P, Q_LORA], F32, R_G, 3 * KB)
        prod = place("prod", [P, 3, PAIR], F32, R_S)
        sel = place("sel", [P, TILES, P], F32R, R_S, 3 * KB)
        ret_s = place("ret_s", [P, 2, 4, P], F32, R_S)
        selT = place("selT", [P, 3, T_ALL], F32R, R_S, 4608)
        rank_tab = place("rank_tab", [P, 2, P], F32, R_P, 28 * KB)
        ret_tab = place("ret_tab", [P, 2, TILES, DV], F32, R_Y)
        posm = own("posm", [P, TILES, N_EXP + 1])
        comb = own("comb", [P, TILES, N_EXP + 1])
        counts = own("counts", [P, 3, N_EXP + 1], I32)
        rtr_w = own("rtr_w", [P, KD, N_EXP])
        rt_bias = own("rt_bias", [P, N_EXP])
        stats = own("stats", [P, TILES, 2, 6])
        mv = own("mv", [P, TILES, 4])
        den = own("den", [P, TILES, HEADS])
        mx = own("mx", [P, 2, 2])

        ps = ctx.enter_context(nc.psum_tensor("ps", [P, 8, 512], F32))

        block = ctx.enter_context(nc.Block())

        def val(k, per, e):
            return k if e is None else e * per + k

        def act_split(act, n, e=None):
            s = n % SPLIT
            act.wait_ge(sem(f"raw_landed{n % RAW}"), val(32 * (n // RAW + 1), 32 * FFN_UNITS // RAW, e))
            if n >= SPLIT:
                act.wait_ge(sem("w_used"), val(n - SPLIT + 1, FFN_UNITS, e))
            nc.scalar.copy(w_hi[:, s, 0:unit_words(n)], raw[:, n % RAW, 0:unit_words(n)]).then_inc(sem("w_hi_ready"), 1)

        def dve_split(dve, n, e=None):
            s, m = n % SPLIT, unit_words(n)
            dve.wait_ge(sem("w_hi_ready"), val(n + 1, FFN_UNITS, e))
            nc.vector.tensor_tensor(w_lo[:, s, 0:m], raw[:, n % RAW, 0:m], w_hi[:, s, 0:m].bitcast(F32),
                                    ALU.subtract).then_inc(sem("w_ready"), 1)

        def splitter(one):
            done = [0]

            def upto(n):
                while done[0] < min(n + AHEAD + 1, U_MOE + AHEAD):
                    one(done[0])
                    done[0] += 1
            return upto

        def split_in_loop(eng, one, u, e):
            if u + AHEAD < FFN_UNITS:
                one(eng, U_MOE + u + AHEAD, e)
            else:
                with eng.If(e < N_EXP - 1):
                    one(eng, U_MOE + u + AHEAD, e)
                eng.nop()

        class Weights:
            def __init__(self, pe, n, e=None):
                pe.wait_ge(sem("w_ready"), val(n + 1, FFN_UNITS, e))
                self.hi, self.lo = w_hi[:, n % SPLIT, :], w_lo[:, n % SPLIT, :]

            def used(self, ins):
                ins.then_inc(sem("w_used"), 1)

        def product3(out, a, b, start, stop, lanes=1):
            nc.tensor.matmul(out, a[0], b[0], start=start, stop=False)
            nc.tensor.matmul(out, a[0], b[1], start=False, stop=False)
            return nc.tensor.matmul(out, a[1], b[0], start=False, stop=stop)

        ckv_dst, kpe_dst = outs[2], outs[3]

        @block.sync
        def _(sp):
            def load(n, e=None):
                if n >= RAW:
                    sp.wait_ge(sem("w_ready"), val(n - RAW + 1, FFN_UNITS, e))
                _, parts = weight_unit(t, n, e)
                slot = raw[:, n % RAW, :]
                for where, nk, src in parts:
                    if nk is None:
                        dst = slot.rearrange("p (k s n) -> p k s n", k=4, s=2)[:, :, where, :]
                    else:
                        dst = slot[:, where[0]:where[1]].rearrange("p (k n) -> p k n", k=nk)
                    sp.dma_start(dst, src).then_inc(sem(f"raw_landed{n % RAW}"), 16)

            for n in range(U_MOE):
                load(n)
            with sp.Fori(0, N_EXP) as e:
                for u in range(FFN_UNITS):
                    load(U_MOE + u, e)
            for i in range(TILES):
                sp.wait_ge(sem("x_ready"), 3 * TILES + i + 1)
                dst = outs[0][0] if i == 0 else outs[1][0, (i - 1) * P:i * P, :]
                sp.dma_start(dst, X[:, i, :]).then_inc(sem("y_stored"), 16)
            sp.wait_ge(sem("y_stored"), 16 * TILES)

        def rope(tt, chain, dst, src, cos, sin, tmp):
            chain(tt(tmp[..., 0::2], src[..., 1::2], sin[..., 0::2], ALU.mult))
            chain(tt(tmp[..., 1::2], src[..., 0::2], sin[..., 1::2], ALU.mult))
            chain(tt(dst, src, cos, ALU.mult))
            return tt(dst, dst, tmp, ALU.add)

        @block.gpsimd
        def _(pool):
            step = [0]

            def chain(ins):
                step[0] += 1
                ins.then_inc(sem("pool_step"), 1)
                pool.wait_ge(sem("pool_step"), step[0])

            def get(dst, src, name):
                pool.dma_start(dst, src).then_inc(sem(name), 16)

            get(vec_rows[0:8, 0, :], t["c_ctx"].rearrange("(r n) -> r n", n=P), "rows_in")
            get(vec_rows[8:16, 0, :], t["c"].rearrange("b (r n) -> (b r) n", n=P), "rows_in")
            get(vec_rows[R_QG:R_QG + 3, 0, :], t["q_a_gain"].rearrange("b (r n) -> (b r) n", n=P), "rows_in")
            get(vec_rows[R_CONVW:R_CONVW + 24, 0, :], t["conv_w"].rearrange("a b (r n) -> (a b r) n", n=P), "rows_in")
            get(vec_rows[R_BMOD:R_BMOD + 48, 0, :], t["b_mod"][0].rearrange("(r n) -> r n", n=P), "rows_in")
            get(vec_rows[0:48, 1, :], t["b_mod"][1].rearrange("(r n) -> r n", n=P), "rows_in")
            for j in range(3):
                for v, name in enumerate(("ln_g", "ln_b")):
                    a = 48 + 16 * j + 8 * v
                    get(vec_rows[a:a + 8, 1, :], t[name][j // 2, j % 2].rearrange("(r n) -> r n", n=P), "rows_in")
            get(const[:, :], t["const"], "const_in")
            get(X[:, 0, :], t["x_prompt"][0], "x_in")
            get(X[:, 1:3, :], t["x_sample"][0].rearrange("(t p) d -> p t d", p=P), "x_in")
            get(gate_bias[:, :], t["b_mod"][0][2 * D:3 * D].unsqueeze(0).broadcast_to([P, D]), "gbias_in")
            get(lg[:, 0:8], t["ret_decay_fwd"].broadcast_to([P, 8]), "dec_in")
            get(lg[:, 8:16], t["ret_decay_bwd"].broadcast_to([P, 8]), "dec_in")
            get(ckv_c[:, :], t["cache_ckv"][0, 0], "cache_in")
            get(kv_gain[:, :], t["kv_a_gain"].broadcast_to([P, KV_LORA]), "cache_in")
            get(ret_tab[:, :, :, :], t["ret_tables"].rearrange("p (a i d) -> p a i d", a=2, i=TILES), "ret_tab_in")
            get(rtr_w[:, :, :], t["router_w"][0].rearrange("(k p) n -> p k n", p=P), "rtr_in")
            get(rt_bias[:, :], t["router_b"].broadcast_to([P, N_EXP]), "rtr_in")
            get(mask_c[:, :, :], t["masks"].rearrange("p (a n) -> p a n", a=4), "mask_in")
            pool.wait_ge(sem("hT_ready"), KD)
            get(kpe4[:, 3, 0, :], t["cache_kpe"][0, 0], "kpe_in")

            pool.wait_ge(sem("rms_ms"), 1)
            pool.tensor_tensor(small[:, 8:14], small[:, 0:6], cst("mhalf")[:, 0:6], ALU.pow).then_inc(sem("rms_pow"), 1)
            pool.wait_ge(sem("ret_tab_in"), 16)
            for which, c0 in enumerate((C_RQ, C_RK)):
                pool.wait_ge(sem("proj_in"), 3 + which)
                for i in range(TILES):
                    v = proj[:, i, c0:c0 + HD].rearrange("p (h d) -> p h d", h=HEADS)
                    cs = ret_tab[:, 0, i:i + 1, :].broadcast_to([P, HEADS, DV])
                    sn = ret_tab[:, 1, i:i + 1, :].broadcast_to([P, HEADS, DV])
                    rope(pool.tensor_tensor, chain, v, v, cs, sn,
                         ret_tmp[:, :].rearrange("p (h d) -> p h d", h=HEADS)).then_inc(sem("ret_roped"), 1)
                    pool.wait_ge(sem("ret_roped"), which * TILES + i + 1)
            pool.wait_ge(sem("ckv_ready"), TILES)
            get(ckv_dst[0, 0], proj[:, 0, C_KV:C_KV + KV_LORA], "small_out")
            get(kpe_dst[0, 0], proj[:, 0, C_PE:C_PE + ROPE], "small_out")
            pool.wait_ge(sem("att_done"), TILES)
            for d_, name in enumerate(("state_ret_fwd", "state_ret_bwd")):
                for two in (0, 1):
                    get(s0[64 * two:64 * two + 64, d_, :, :],
                        t[name][0, 0].rearrange("(c two) d v -> two d c v", two=2)[two], "s0_in")
            for i in range(TILES):
                pool.wait_ge(sem("hn_var"), i + 1)
                pool.tensor_tensor(small[:, 24:32], small[:, 16:24], cst("mhalf"), ALU.pow).then_inc(sem("hn_pow"), 1)
            pool.wait_ge(sem("sctx_ready"), 2)
            for d_ in (0, 1):
                for two in (0, 1):
                    get(outs[4 + d_][0, 0].rearrange("(c two) d v -> two d c v", two=2)[two],
                        s_ctx[64 * two:64 * two + 64, d_, :, :], "small_out")
            for k in range(4):
                layer, sub = k // 2, k % 2
                if k == 0:
                    pool.wait_ge(sem("mix_ready"), TILES)
                elif k == 3:
                    pool.wait_ge(sem("x_full"), 3 * TILES)
                    get(rank_tab[:, :, :], t["ranks"].rearrange("p (a n) -> p a n", a=2), "ranks_in")
                    pool.wait_ge(sem("gathers_done"), 1)
                else:
                    pool.wait_ge(sem("x_full"), TILES * k)
                for j, name in enumerate(("ln_g", "ln_b")):
                    get((last_rows if k == 3 else ln_rows)[:, j, :], t[name][layer, sub].unsqueeze(0).broadcast_to([P, D]), "ln_rows_in")
                if k < 3:
                    nl, nv = ((0, 5), (1, 2), (1, 5))[k]
                    pool.wait_ge(sem("post_done"), MOD_POSTS[GATE_PLACE[k] + 2])
                    get(gate_bias[:, :], t["b_mod"][nl][nv * D:(nv + 1) * D].unsqueeze(0).broadcast_to([P, D]), "gbias_in")
                for i in range(TILES):
                    pool.wait_ge(sem("ln_var"), TILES * k + i + 1)
                    pool.tensor_tensor(mv[:, i, 3:4], mv[:, i, 2:3], cst("mhalf")[:, 0:1], ALU.pow).then_inc(sem("ln_pow"), 1)
                if k < 3:
                    pool.wait_ge(sem("xT_ready"), KD * (k + 2))
                    pool.wait_ge(sem("ln_rows_in"), 32 * (k + 1))
                    for i in range(TILES):
                        chain(pool.tensor_tensor(X[:, i, :], X[:, i, :], ln_rows[:, 0, :], ALU.mult))
                        pool.tensor_tensor(X[:, i, :], X[:, i, :], ln_rows[:, 1, :], ALU.add).then_inc(sem("x_full"), 1)
            pool.wait_ge(sem("small_out"), 16 * 6)

        @block.tensor
        def _(pe):
            mm = nc.tensor.matmul

            pending = []

            def mod_products(g):
                place_ = MOD_ORDER.index(g)
                if place_ >= 1:
                    pe.wait_ge(sem("m4_ready"), place_)
                for half in (0, 1):
                    w = Weights(pe, AT["mod", g] + half)
                    for k in range(4):
                        kc, cols = 4 * half + k, slice(k * 512, (k + 1) * 512)
                        mm(ps[:, 6, :], st_cond[:, kc, :], w.hi[:, cols], start=kc == 0, stop=False)
                        last = mm(ps[:, 6, :], st_cond[:, kc, :], w.lo[:, cols], start=False, stop=kc == KD - 1)
                    w.used(last)

            def mod_post(g):
                place_ = MOD_ORDER.index(g)
                pe.wait_ge(sem("m4_ready"), place_ + 1)
                posts = MOD_POSTS[place_]
                if posts >= 1:
                    pe.wait_ge(sem("post_done"), posts)
                if MOD_CHUNKS[g][1] % 3 == 2:
                    for cond in (0, 1):
                        if cond:
                            pe.wait_ge(sem("post_done"), posts + 1)
                        mm(ps[:, 7, :], cst("selrow")[:, cond * P:(cond + 1) * P], m4[:, :],
                           start=True, stop=True).then_inc(sem("post_ready"), 1)
                else:
                    for k in range(4):
                        last = mm(ps[:, 7, 2 * k:2 * k + 2], m4[:, k * P:(k + 1) * P], cst("selcol"),
                                  start=True, stop=True)
                    last.then_inc(sem("post_ready"), 1)

            def modulations(chunks, flush=False):
                for g in chunks:
                    if pending:
                        mod_post(pending.pop())
                    mod_products(g)
                    pending.append(g)
                if flush and pending:
                    mod_post(pending.pop())

            def turn_x(first, count):
                for k in range(KD):
                    if k >= 2:
                        pe.wait_ge(sem("hf_ready"), first + k - 1)
                    for i in range(TILES):
                        if k == 0 and count:
                            pe.wait_ge(sem("x_ready"), count + i)
                        last = nc.tensor.transpose(ps[:, 4 + k % 2, i * P:(i + 1) * P], X[:, i, k * P:(k + 1) * P], ident)
                    last.then_inc(sem("xT_ready"), 1)

            pe.wait_ge(sem("rows_in"), 16 * 12)
            pe.wait_ge(sem("const_in"), 16)
            nc.tensor.transpose(ps[:, 0, 0:91], vec_rows[0:91, 0, :], ident[0:91, 0:91])
            nc.tensor.transpose(ps[:, 0, 96:192], vec_rows[0:96, 1, :], ident[0:96, 0:96]).then_inc(sem("cols_ready"), 1)
            pe.wait_ge(sem("cond_ready"), 4)
            modulations(MOD_FIRST, flush=True)
            pe.wait_ge(sem("x_in"), 32)
            pe.wait_ge(sem("cols_done"), 2)
            turn_x(0, 0)

            for c, (_, width) in enumerate(PROJ_CHUNKS):
                n = AT["proj", c]
                if c >= 2:
                    pe.wait_ge(sem("proj_in"), c - 1)
                halves = [(0, KD)] if width < 512 else [(0, 4), (4, 8)]
                for a, b in halves:
                    w = Weights(pe, n)
                    if c == 0:
                        pe.wait_ge(sem("hT_ready"), b)
                    for i in range(TILES):
                        for k in range(a, b):
                            cols = slice((k - a) * width, (k - a + 1) * width)
                            last = product3(ps[:, (c % 2) * 3 + i, 0:width], [x[:, k, i * P:(i + 1) * P] for x in hT],
                                            (w.hi[:, cols], w.lo[:, cols]), k == 0, k == KD - 1)
                    w.used(last)
                    n += 1
                modulations(MOD_AFTER_PROJ[c])
            modulations([], flush=True)

            turned = 0

            def turn_bank():
                nonlocal turned
                if turned == 7:
                    pe.wait_ge(sem("lat_hi"), 6)
                elif turned >= 2:
                    pe.wait_ge(sem("lat_lo"), turned - 1)
                turned += 1
                return 6 + (turned - 1) % 2
            pe.wait_ge(sem("post_done"), MOD_POSTS[MOD_ORDER.index(10)])
            pe.wait_ge(sem("cache_in"), 32)
            pe.wait_ge(sem("ckv_ready"), TILES)
            for k in range(KKV):
                b = turn_bank()
                for i in range(4):
                    src = ckv_c[:, k * P:(k + 1) * P] if i == 3 else proj[:, i, C_KV + k * P:C_KV + (k + 1) * P]
                    last = nc.tensor.transpose(ps[:, b, i * P:(i + 1) * P], src, ident)
                last.then_inc(sem("lat_turned"), 1)
            for k in range(KQ):
                b = turn_bank()
                for i in range(TILES):
                    last = nc.tensor.transpose(ps[:, b, i * P:(i + 1) * P], proj[:, i, k * P:(k + 1) * P], ident)
                last.then_inc(sem("lat_turned"), 1)
            b = turn_bank()
            pe.wait_ge(sem("kpe4_ready"), 1)
            for i in range(4):
                last = nc.tensor.transpose(ps[:, b, i * P:(i + 1) * P],
                                           kpe4[:, i, :, :].rearrange("p r d -> p (r d)"), ident)
            last.then_inc(sem("lat_turned"), 1)

            outn = 0

            def mla_bank():
                nonlocal outn
                outn += 1
                if outn == 1:
                    pe.wait_ge(sem("proj_in"), 6)
                if outn > 6:
                    pe.wait_ge(sem("mla_in"), outn - 6)
                return (outn - 1) % 6
            w = Weights(pe, U_KV)
            pe.wait_ge(sem("lat_lo"), KKV)
            kv = [(w.hi[:, k * D:(k + 1) * D], w.lo[:, k * D:(k + 1) * D]) for k in range(KKV)]
            for i in range(4):
                b = mla_bank()
                for k in range(KKV):
                    last = product3(ps[:, b, :], [x[:, k, i * P:(i + 1) * P] for x in ckvT],
                                    [x[:, HD:2 * HD] for x in kv[k]], k == 0, k == KKV - 1)
                last.then_inc(sem("mla_out"), 1)
            for hp in range(4):
                b = mla_bank()
                for k in range(KKV):
                    last = product3(ps[:, b, :], [x[:, hp * P:(hp + 1) * P] for x in kv[k]],
                                    [x[:, k, :] for x in ckvT], k == 0, k == KKV - 1)
                if hp < 3:
                    last.then_inc(sem("mla_out"), 1)
            w.used(last)
            w = Weights(pe, U_QA)
            pe.wait_ge(sem("lat_lo"), KKV + KQ)
            for hp in range(4):
                b = mla_bank()
                for k in range(KQ):
                    cols = slice(k * HD + hp * P, k * HD + (hp + 1) * P)
                    last = product3(ps[:, b, 0:T_ALL], (w.hi[:, cols], w.lo[:, cols]),
                                    [x[:, k, :] for x in qnT], k == 0, k == KQ - 1)
                if hp < 3:
                    last.then_inc(sem("mla_out"), 1)
            w.used(last)
            w = Weights(pe, U_QB)
            for i in range(TILES):
                b = mla_bank()
                for k in range(KQ):
                    cols = slice(k * HEADS * ROPE, (k + 1) * HEADS * ROPE)
                    last = product3(ps[:, b, 0:HEADS * ROPE], [x[:, k, i * P:(i + 1) * P] for x in qnT],
                                    (w.hi[:, cols], w.lo[:, cols]), k == 0, k == KQ - 1)
                if i < TILES - 1:
                    last.then_inc(sem("mla_out"), 1)
            w.used(last)
            pe.wait_ge(sem("qR_ready"), TILES)
            for k in range(2):
                b = turn_bank()
                for i in range(TILES):
                    last = nc.tensor.transpose(ps[:, b, i * P:(i + 1) * P], qR[:, i, k * P:(k + 1) * P], ident)
                last.then_inc(sem("lat_turned"), 1)
            pe.wait_ge(sem("qRT_in"), 2)
            pe.wait_ge(sem("mla_in"), 15)

            items = [(i, h) for i in range(TILES) for h in range(HEADS)]

            def scores(m):
                i, h = items[m]
                keys = slice(0, P) if i == 0 else slice(P, 4 * P)
                nk = 1 if i == 0 else 3
                if m >= 2:
                    pe.wait_ge(sem("e_ready"), m - 1)
                rows, rr = slice(64 * (h % 2), 64 * (h % 2) + 64), slice(32 * (h % 4), 32 * (h % 4) + 32)
                mm(ps[:, m % 2, 0:nk * P], qNT[rows, h // 2, i * P:(i + 1) * P], kNT[rows, h // 2, keys],
                   start=True, stop=False)
                mm(ps[:, m % 2, 0:nk * P], qRT[rr, h // 4, i * P:(i + 1) * P], kpeT[rr, keys],
                   start=False, stop=True).then_inc(sem("s_ready"), 1)

            def turn_e(m):
                i, h = items[m]
                pe.wait_ge(sem("e_ready"), m + 1)
                if m >= 2:
                    pe.wait_ge(sem("eT_ready"), m - 1)
                for j in range(1 if i == 0 else 3):
                    last = nc.tensor.transpose(ps[:, 2 + m % 2, j * P:(j + 1) * P], E[:, m % 2, j * P:(j + 1) * P], ident)
                last.then_inc(sem("eT_turned"), 1)

            def values(m):
                i, h = items[m]
                pe.wait_ge(sem("eT_ready"), m + 1)
                tiles = [0] if i == 0 else [1, 2, 3]
                for j, kt in enumerate(tiles):
                    v = V01[:, kt, :] if kt < 2 else V23[:, kt - 2, :]
                    last = mm(ps[:, 4 + i, h * DV:(h + 1) * DV], ET[:, m % 2, j * P:(j + 1) * P],
                              v[:, h * DV:(h + 1) * DV], start=j == 0, stop=j == len(tiles) - 1)
                last.then_inc(sem("o_ready"), 1)

            for m in range(len(items) + 2):
                if m < len(items):
                    scores(m)
                if 0 <= m - 1 < len(items):
                    turn_e(m - 1)
                if m >= 2:
                    values(m - 2)

            pe.wait_ge(sem("ret_roped"), 2 * TILES)
            rturn = 0

            def ret_bank():
                nonlocal rturn
                if rturn >= 2:
                    pe.wait_ge(sem("ret_turned_in"), rturn - 1)
                rturn += 1
                return (rturn - 1) % 2
            for c0 in (C_RQ, C_RK):
                for k in range(4):
                    b = ret_bank()
                    for i in range(TILES):
                        last = nc.tensor.transpose(ps[:, b, i * P:(i + 1) * P], proj[:, i, c0 + k * P:c0 + (k + 1) * P], ident)
                    last.then_inc(sem("ret_turned"), 1)
            for i in (1, 2):
                for d_ in (0, 1):
                    b = ret_bank()
                    pe.wait_ge(sem("q_dec_ready"), 2 * (i - 1) + d_ + 1)
                    for k in range(4):
                        last = nc.tensor.transpose(ps[:, b, k * P:(k + 1) * P], q_dec[:, d_, k * P:(k + 1) * P], ident)
                    last.then_inc(sem("ret_turned"), 1)
            for j, i in enumerate((0, 0, 1, 2)):
                pe.wait_ge(sem("k_dec_ready"), j + 1)
                if j == 1 or j == 2:
                    pe.wait_ge(sem("sctx_ready"), j)
                elif j == 3:
                    pe.wait_ge(sem("state_in"), 1)
                for h in range(HEADS):
                    r = slice(64 * (h % 2), 64 * (h % 2) + 64)
                    last = mm(ps[r, 2, (h // 2) * DV:(h // 2 + 1) * DV], k_dec[:, j, h * DV:(h + 1) * DV],
                              proj[:, i, C_RV + h * DV:C_RV + (h + 1) * DV], start=True, stop=True)
                last.then_inc(sem("state_out"), 1)
            pe.wait_ge(sem("ret_turned_in"), 12)
            pe.wait_ge(sem("state_in"), 2)
            pe.wait_ge(sem("s0_in"), 16 * 4)
            pe.wait_ge(sem("att_done"), TILES)

            def ret_scores(m):
                i, parity = m // 2, m % 2
                if m >= 2:
                    pe.wait_ge(sem("rs_ready"), m - 1)
                for j in range(4):
                    h = 2 * j + parity
                    r = slice(64 * (h % 2), 64 * (h % 2) + 64)
                    last = mm(ps[:, m % 2, j * P:(j + 1) * P], rkT[r, h // 2, i * P:(i + 1) * P],
                              rqT[r, h // 2, i * P:(i + 1) * P], start=True, stop=True)
                last.then_inc(sem("rs_out"), 1)

            def ret_values(m):
                i, parity = m // 2, m % 2
                pe.wait_ge(sem("rs_ready"), m + 1)
                if parity:
                    pe.wait_ge(sem("ret_even"), i + 1)
                for j in range(4):
                    h = 2 * j + parity
                    r = slice(64 * (h % 2), 64 * (h % 2) + 64)
                    out = ps[:, 4 + i, h * DV:(h + 1) * DV]
                    last = mm(out, ret_s[:, m % 2, j, :], proj[:, i, C_RV + h * DV:C_RV + (h + 1) * DV],
                              start=True, stop=i == 0)
                    if i:
                        fwd, bwd = (s0, s1) if i == 1 else (s1, s0)
                        q = slice((i - 1) * P, i * P)
                        mm(out, qdT[r, 0, h // 2, q], fwd[r, 0, h // 2, :], start=False, stop=False)
                        last = mm(out, qdT[r, 1, h // 2, q], bwd[r, 1, h // 2, :], start=False, stop=True)
                last.then_inc(sem("ret_out" if parity else "ret_even"), 1)

            for m in range(7):
                if m < 6:
                    ret_scores(m)
                if m >= 1:
                    ret_values(m - 1)

            pe.wait_ge(sem("mix_ready"), TILES)
            for k in range(KD):
                if k >= 2:
                    pe.wait_ge(sem("mixT_ready"), k - 1)
                for i in range(TILES):
                    last = nc.tensor.transpose(ps[:, k % 2, i * P:(i + 1) * P], mix[k // 4][:, i, (k % 4) * P:(k % 4 + 1) * P], ident)
                last.then_inc(sem("mix_turned"), 1)

            def down(src, widths, unit, acc, tiles, first, last_phase, ready, e=None):
                k = 0
                for u, nk in enumerate(widths):
                    w = Weights(pe, unit + u, e)
                    for kk in range(nk):
                        ready(k)
                        for i in range(tiles):
                            for half in (0, 1):
                                cols = slice(kk * D + half * 512, kk * D + half * 512 + 512)
                                last = product3(ps[:, acc(i, half), :], [x[:, k, i * P:(i + 1) * P] for x in src],
                                                (w.hi[:, cols], w.lo[:, cols]), first and k == 0,
                                                last_phase and k == sum(widths) - 1)
                        k += 1
                    w.used(last)
                    yield u

            def all_banks(i, half):
                return 2 * i + half

            def ready_mix(k):
                if k == 0:
                    pe.wait_ge(sem("mixT_ready"), KD)

            for _ in down(mixT, [2] * 4, U_OUT0, all_banks, TILES, True, True, ready_mix):
                pass
            turn_x(KD, 1)

            def ffn(src, unit, tiles, e, after_unit=lambda u: None, after_phase=lambda phase: None):
                pairs0 = 0 if e is None else PAIRS
                per = None if e is None else PAIRS
                single = tiles == 1
                acc = (lambda i, half: 2 + half) if single else all_banks

                def turn_prod(c):
                    pe.wait_ge(sem("prod_ready"), val(pairs0 + c + 1, per, e))
                    prev = c - 1 if tiles == 3 else c - 2
                    if pairs0 + prev >= 0 and prev >= 0:
                        pe.wait_ge(sem("pT_lo"), val(pairs0 + prev + 1, per, e))
                    for i in range(tiles):
                        b = (7 if i == 2 else 6) if tiles == 3 else 6 + c % 2
                        o = (i % 2) * PAIR
                        for j in (0, 1):
                            last = nc.tensor.transpose(ps[:, b, o + j * P:o + (j + 1) * P], prod[:, i, j * P:(j + 1) * P], ident)
                    last.then_inc(sem("pT_turned"), 1)

                u = 0
                for phase in (0, 1):
                    pairs = PHASE_PAIRS[phase]
                    waiting = None
                    for c in pairs:
                        for half in (0, 1):
                            w = Weights(pe, unit(u), e)
                            for i in range(tiles):
                                b = (c + phase) % 2 * tiles + i
                                for k in range(4):
                                    cols = slice(k * 512, (k + 1) * 512)
                                    last = product3(ps[:, b, :], [x[:, 4 * half + k, i * P:(i + 1) * P] for x in src],
                                                    (w.hi[:, cols], w.lo[:, cols]), half == 0 and k == 0,
                                                    half == 1 and k == 3)
                            w.used(last)
                            if half == 0 and waiting is not None:
                                turn_prod(waiting)
                            after_unit(u)
                            u += 1
                        waiting = c
                    if not single:
                        pe.wait_ge(sem("prod_ready"), val(pairs0 + waiting + 1, per, e))
                    last_pair = waiting

                    def ready(k):
                        if k % 2 == 0:
                            pe.wait_ge(sem("pT_lo"), val(pairs0 + pairs[0] + k // 2 + 1, per, e))
                    for d_ in down(prodT, PHASE_DOWN[phase], unit(u), acc, tiles, phase == 0 or not single,
                                   phase == 1 or not single, ready, e):
                        if d_ == 0:
                            turn_prod(last_pair)
                        after_unit(u + d_)
                    u += len(PHASE_DOWN[phase])
                    after_phase(phase)

            def dense_phase(phase):
                if phase == 0:
                    modulations(MOD_IN_FFN, flush=True)
                    pe.wait_ge(sem("post_done"), MOD_POSTS[MOD_ORDER.index(16)])
                    pe.wait_ge(sem("dense_in"), 1)

            pe.wait_ge(sem("hT_ready"), 2 * KD)
            ffn(hT, dense_unit, TILES, None, after_phase=dense_phase)

            turn_x(2 * KD, TILES + 1)
            pe.wait_ge(sem("hT_ready"), 3 * KD)
            m = 0
            for f in range(4):
                for third in range(3):
                    w = Weights(pe, AT["conv", f] + third)
                    for j in (0, 1):
                        if f:
                            pe.wait_ge(sem(("conv_c_in", "z_ready", "by_ready")[third]), 2 * (f - 1) + j + 1)
                        for k in range(KD):
                            cols = slice(k * 256 + j * P, k * 256 + (j + 1) * P)
                            last = product3(ps[:, m % 6, 0:T_ALL], (w.hi[:, cols], w.lo[:, cols]),
                                            [x[:, k, :] for x in hT], k == 0, k == KD - 1)
                        m += 1
                        if j == 0:
                            last.then_inc(sem("conv_out"), 1)
                    w.used(last)
                modulations(MOD_AFTER_CONV[f])
            modulations([], flush=True)

            def ready_conv(k):
                if k == 0:
                    pe.wait_ge(sem("by_lo"), KD)
            for _ in down(byT, [2] * 4, U_OUT1, all_banks, TILES, True, True, ready_conv):
                pass
            modulations(MOD_LAST, flush=True)
            turn_x(3 * KD, 2 * TILES + 1)

            pe.wait_ge(sem("hf_ready"), 4 * KD)
            pe.wait_ge(sem("rtr_in"), 32)
            for i in range(TILES):
                for k in range(KD):
                    last = mm(ps[:, 2, i * N_EXP:(i + 1) * N_EXP], hfT[:, k, i * P:(i + 1) * P], rtr_w[:, k, :],
                              start=k == 0, stop=k == KD - 1)
            last.then_inc(sem("logits_out"), 1)
            n = 0
            for i in range(TILES):
                for q in (0, 1):
                    if n >= 2:
                        pe.wait_ge(sem("Ht_lo"), n - 1)
                    for k in range(4):
                        last = nc.tensor.transpose(ps[:, 4 + n % 2, k * P:(k + 1) * P],
                                                   hfT[:, 4 * q + k, i * P:(i + 1) * P], ident)
                    last.then_inc(sem("Ht_turned"), 1)
                    n += 1
            pe.wait_ge(sem("chosen"), 1)
            pe.wait_ge(sem("ranks_in"), 16)
            for i in range(TILES):
                for j in range(i + 1):
                    mm(ps[:, 3, i * N_EXP:(i + 1) * N_EXP], rank_tab[:, 0 if j == i else 1, :],
                       rt[:, 0, j, :], start=j == 0, stop=j == i)
            for j in range(TILES):
                last = mm(ps[:, 3, 3 * N_EXP:4 * N_EXP], rank_tab[:, 1, :], rt[:, 0, j, :], start=j == 0, stop=j == TILES - 1)
            last.then_inc(sem("ranks_out"), 1)

            pe.wait_ge(sem("counts_ready"), 2)
            pe.wait_ge(sem("post_done"), MOD_POSTS[-1])
            pe.wait_ge(sem("Ht_hi"), 2 * TILES)
            pe.wait_ge(sem("Ht_lo"), 2 * TILES)

            def gather(g, bank):
                pe.wait_ge(sem("sel_ready"), g + 1)
                for half in (0, 1):
                    cols = slice(half * 512, half * 512 + 512)
                    for x in (0, 1):
                        for i in range(TILES):
                            last = mm(ps[:, bank + half, :], sel[:, i, :], H_tok[x][:, i, cols],
                                      start=x + i == 0, stop=x == 1 and i == TILES - 1)
                    last.then_inc(sem("g_out"), 1)

            def turn_rows(g, bank, rows):
                for half in (0, 1):
                    pe.wait_ge(sem("g_in"), g * 2 + 2)
                    for k in range(4):
                        kc = 4 * half + k
                        last = nc.tensor.transpose(ps[:, bank + half, k * P:(k + 1) * P],
                                                   rows[:, kc // 2, kc % 2 * P:(kc % 2 + 1) * P], ident)
                    last.then_inc(sem("g_turned"), 1)

            def turn_selection(bank):
                for i in range(TILES):
                    last = nc.tensor.transpose(ps[:, bank, i * P:(i + 1) * P], sel[:, i, :].bitcast(F32), ident)
                last.then_inc(sem("selT_out"), 1)

            def scatter(q, bank, slot, y, steps):
                if 0 in steps:
                    pe.wait_ge(sem("yst_lo"), q + 1)
                for m in steps:
                    i, half = m // 2, m % 2
                    pe.wait_ge(sem("y_added"), q * 6 + (m + 5))
                    out = ps[:, bank + m % 2, :].rearrange("p (a n) -> p a n", a=2)
                    for x in (0, 1):
                        last = mm(out, selT[:, slot, i * P:(i + 1) * P], y[x][:, 2 * half:2 * half + 2, :],
                                  start=x == 0, stop=x == 1)
                    last.then_inc(sem("y_out"), 1)

            gather(0, 4)
            turn_rows(0, 4, g_rows)
            with pe.Fori(0, N_EXP) as e:
                count = pe.value_load(counts[0:1, 0, ds(e, 1)], min_val=0, max_val=T_ALL)
                tiles0 = pe.value_load(counts[0:1, 1, ds(e, 1)], min_val=0, max_val=3 * N_EXP)
                scat0 = pe.value_load(counts[0:1, 2, ds(e, 1)], min_val=0, max_val=6 * N_EXP)

                def expert(tiles):
                    bank = 6 if tiles == 3 else 4
                    pe.wait_ge(sem("y_added"), scat0 * 6 + 6)
                    pe.wait_ge(sem("g_hi"), tiles0 * 2 + 2)
                    pe.wait_ge(sem("g_lo"), tiles0 * 2 + 2)
                    if tiles > 1:
                        scatter(scat0, bank, 0, y_last, range(6))
                        pe.wait_ge(sem("y_added"), scat0 * 6 + 12)
                        turn_selection(bank)
                        for s in range(1, tiles):
                            g = tiles0 + s
                            pe.wait_ge(sem("selT_ready"), g)
                            gather(g, bank)
                            turn_rows(g, bank, g_rows_more)
                            pe.wait_ge(sem("g_hi"), g * 2 + 2)
                            pe.wait_ge(sem("g_lo"), g * 2 + 2)
                            turn_selection(bank)

                    def between(u):
                        if tiles == 1 and u < 3:
                            scatter(scat0, bank, 0, y_last, range(2 * u, 2 * u + 2))
                        elif tiles == 1 and u == 4:
                            pe.wait_ge(sem("y_added"), scat0 * 6 + 12)
                            turn_selection(bank)
                        elif u == GATHER_AT:
                            pe.wait_ge(sem("selT_ready"), tiles0 + tiles)
                            if tiles == 3:
                                pe.wait_ge(sem("pT_lo"), val(PAIRS + PAIRS, PAIRS, e))
                            else:
                                pe.wait_ge(sem("y_added"), scat0 * 6 + (6 * (tiles if tiles > 1 else 0) + 12))
                            gather(tiles0 + tiles, bank)
                        elif u == GATHER_AT + 2:
                            turn_rows(tiles0 + tiles, bank, g_rows)

                    def scatters(phase):
                        if tiles == 1:
                            return
                        if phase == 0:
                            pe.wait_ge(sem("selT_ready"), tiles0 + tiles)
                        else:
                            pe.wait_ge(sem("g_hi"), (tiles0 + tiles) * 2 + 2)
                            pe.wait_ge(sem("g_lo"), (tiles0 + tiles) * 2 + 2)
                        for s in range(tiles - phase):
                            scatter(scat0 + (1 + phase * tiles + s), bank, tiles - 1 - s, y_st, range(6))
                    ffn(gT, expert_unit, tiles, e, after_unit=between, after_phase=scatters)

                with pe.If(count > P):
                    with pe.If(count > 2 * P):
                        expert(3)
                    with pe.Else():
                        expert(2)
                    pe.nop()
                with pe.Else():
                    expert(1)
                pe.nop()
            total = pe.value_load(counts[0:1, 2, N_EXP:N_EXP + 1], min_val=0, max_val=6 * N_EXP)
            pe.wait_ge(sem("y_added"), total * 6 + 6)
            pe.wait_ge(sem("g_hi"), 2)
            pe.nop().then_inc(sem("gathers_done"), 1)
            scatter(total, 4, 0, y_last, range(6))

        @block.scalar
        def _(act):
            split = splitter(lambda n: act_split(act, n))
            step = [0]

            def chain(ins):
                step[0] += 1
                ins.then_inc(sem("act_step"), 1)
                act.wait_ge(sem("act_step"), step[0])

            def modulations(chunks):
                for g in chunks:
                    split(AT["mod", g])
                    split(AT["mod", g] + 1)
                    act.wait_ge(sem("w_used"), AT["mod", g] + 2)
                    nc.scalar.copy(m4[:, :], ps[:, 6, :]).then_inc(sem("m4_ready"), 1)

            def modulate(first, shift, scale, dst=None):
                for k in range(KD):
                    act.wait_ge(sem("xT_ready"), first + k + 1)
                    if dst is None:
                        if k >= 2:
                            act.wait_ge(sem("hT_ready"), first + k - 1)
                        out = hf[:, k % 2, :]
                    else:
                        out = dst[:, k, :]
                    for cond, cols in ((0, slice(0, P)), (1, slice(P, T_ALL))):
                        last = nc.scalar.activation(out[:, cols], ps[:, 4 + k % 2, cols], ACT.Identity,
                                                    bias=mod_col[:, shift, k, cond:cond + 1],
                                                    scale=mod_col[:, scale, k, cond:cond + 1])
                    last.then_inc(sem("hf_ready"), 1)

            act.wait_ge(sem("cols_ready"), 1)
            nc.scalar.copy(cols1[:, :], ps[:, 0, 96:192]).then_inc(sem("cols_done"), 1)
            nc.scalar.copy(cols0[:, 0:91], ps[:, 0, 0:91]).then_inc(sem("cols_done"), 1)
            act.wait_ge(sem("cols_done"), 2)
            chain(nc.scalar.activation(cond_f[:, :], cols0[:, 0:16], ACT.Silu))
            nc.scalar.copy(cond_hi[:, :], cond_f[:, :]).then_inc(sem("cond_hi"), 1)
            act.wait_ge(sem("lsig_in"), 1)
            nc.scalar.activation(small[:, 48:64], small[:, 32:48], ACT.Exp).then_inc(sem("lsig_exp"), 1)
            modulations(MOD_FIRST)
            act.wait_ge(sem("post_done"), MOD_POSTS[len(MOD_FIRST)])
            modulate(0, 0, 1)
            for c, (c0, width) in enumerate(PROJ_CHUNKS):
                n = AT["proj", c]
                for _ in range(1 if width < 512 else 2):
                    split(n)
                    n += 1
                act.wait_ge(sem("w_used"), n)
                src = ps[:, (c % 2) * 3:(c % 2) * 3 + 3, 0:width]
                nc.scalar.activation(proj[:, :, c0:c0 + width], src, ACT.Copy,
                                     scale=RET_SCALE if c0 == C_RK else 1.0).then_inc(sem("proj_in"), 1)
                if c == 1:
                    act.wait_ge(sem("proj_in"), 2)
                    for i in range(TILES):
                        for j, (a, b) in enumerate(((C_Q, Q_LORA), (C_KV, KV_LORA))):
                            if i + j:
                                act.wait_ge(sem("rms_ss"), 2 * i + j)
                            nc.scalar.activation(junk[:, 0:b], proj[:, i, a:a + b], ACT.Square,
                                                 accum_out=small[:, 16 + 3 * j + i:17 + 3 * j + i]).then_inc(sem("rms_ss"), 1)
                modulations(MOD_AFTER_PROJ[c])
            act.wait_ge(sem("proj_in"), 6)
            for i in range(TILES):
                nc.scalar.activation(proj[:, i, C_RG:C_RG + HD], proj[:, i, C_RG:C_RG + HD], ACT.Silu).then_inc(sem("rg_ready"), 1)
            for m in range(KKV + KQ):
                act.wait_ge(sem("lat_turned"), m + 1)
                b = 6 + m % 2
                if m == 0:
                    act.wait_ge(sem("w_used"), U_KV)
                if m < KKV:
                    nc.scalar.copy(ckvT[0][:, m, :], ps[:, b, :]).then_inc(sem("lat_hi"), 1)
                else:
                    k = m - KKV
                    nc.scalar.activation(qnT[0][:, k, :], ps[:, b, 0:T_ALL], ACT.Copy,
                                         scale=cols0[:, R_QG + k:R_QG + k + 1]).then_inc(sem("lat_hi"), 1)
            act.wait_ge(sem("lat_turned"), 6)
            nc.scalar.copy(kpeT[:, :], ps[:, 7, :]).then_inc(sem("lat_hi"), 1)
            split(U_KV)
            for m in range(15):
                if m == 8:
                    split(U_QA)
                if m == 12:
                    split(U_QB)
                done = {7: U_KV, 11: U_QA, 14: U_QB}.get(m)
                if done is None:
                    act.wait_ge(sem("mla_out"), m + 1 - sum(m > x for x in (7, 11)))
                else:
                    act.wait_ge(sem("w_used"), done + 1)
                b = m % 6
                if m < 2:
                    nc.scalar.copy(V01[:, m, :], ps[:, b, :]).then_inc(sem("mla_in"), 1)
                elif m < 4:
                    nc.scalar.copy(V23[:, m - 2, :], ps[:, b, :]).then_inc(sem("mla_in"), 1)
                elif m < 8:
                    nc.scalar.copy(kNT[:, m - 4, :], ps[:, b, :]).then_inc(sem("mla_in"), 1)
                elif m < 12:
                    nc.scalar.copy(qNT[:, m - 8, :], ps[:, b, 0:T_ALL]).then_inc(sem("mla_in"), 1)
                else:
                    nc.scalar.copy(qR[:, m - 12, :], ps[:, b, 0:HEADS * ROPE]).then_inc(sem("mla_in"), 1)
            for k in range(2):
                act.wait_ge(sem("lat_turned"), 7 + k)
                nc.scalar.copy(qRT[:, k, :], ps[:, 6 + k % 2, 0:T_ALL]).then_inc(sem("qRT_in"), 1)
            for m in range(TILES * HEADS):
                i, h = m // HEADS, m % HEADS
                w_ = P if i == 0 else 3 * P
                act.wait_ge(sem("mx_ready"), m + 1)
                if m >= 2:
                    act.wait_ge(sem("eT_turned"), m - 1)
                nc.scalar.activation(E[:, m % 2, 0:w_], ps[:, m % 2, 0:w_], ACT.Exp, bias=mx[:, m % 2, 1:2],
                                     scale=ATT_SCALE, accum_out=den[:, i, h:h + 1]).then_inc(sem("e_ready"), 1)
            act.wait_ge(sem("att_done"), TILES)
            act.wait_ge(sem("lg_ready"), 1)
            act.wait_ge(sem("mask_in"), 16)
            for j, (a, d_) in enumerate(((0, 0), (1, 0), (2, 1), (3, 1))):
                nc.scalar.activation(dec[:, j, :], lg[:, 8 * d_:8 * d_ + 8], ACT.Exp, scale=cst("decay_at")[:, a:a + 1])
            for two in (0, 1):
                r = slice(64 * two, 64 * two + 64)
                last = nc.scalar.activation(cdec[r, :, :], lg[r, :].rearrange("p (d c two) -> p d c two", d=2, two=2)[:, :, :, two],
                                            ACT.Exp, scale=float(P))
            last.then_inc(sem("dec_ready"), 1)
            for h in range(HEADS):
                nc.scalar.activation(mask[:, h, :], mask_c[:, 0, :], ACT.Exp, scale=lg[:, h:h + 1])
                last = nc.scalar.activation(mask_b[:, h, :], mask_c[:, 1, :], ACT.Exp, scale=lg[:, 8 + h:9 + h])
            last.then_inc(sem("mask_exp"), 1)
            for m in range(12):
                act.wait_ge(sem("ret_turned"), m + 1)
                b = m % 2
                if m < 8:
                    dst = (rqT if m < 4 else rkT)[:, m % 4, :]
                    last = nc.scalar.copy(dst, ps[:, b, 0:T_ALL])
                else:
                    i, d_ = (m - 8) // 2, (m - 8) % 2
                    last = nc.scalar.copy(qdT[:, d_, :, i * P:(i + 1) * P], ps[:, b, :].rearrange("p (c n) -> p c n", c=4))
                last.then_inc(sem("ret_turned_in"), 1)
            for j in range(2):
                act.wait_ge(sem("state_out"), j + 1)
                nc.scalar.copy(s_ctx[:, j, :, :], ps[:, 2, 0:4 * DV].rearrange("p (c v) -> p c v", c=4)).then_inc(sem("sctx_ready"), 1)
            for k in range(KD):
                act.wait_ge(sem("mix_turned"), k + 1)
                if k == 0:
                    act.wait_ge(sem("small_out"), 16 * 6)
                nc.scalar.copy(mixT[0][:, k, :], ps[:, k % 2, 0:T_ALL]).then_inc(sem("mixT_hi"), 1)
            for u in range(4):
                split(U_OUT0 + u)
            act.wait_ge(sem("folded"), 1)
            modulate(KD, 2, 3)

            def ffn(unit, tiles, e, splits, after_phase):
                pairs0 = 0 if e is None else PAIRS
                per = None if e is None else PAIRS

                def hidden_hi(c):
                    act.wait_ge(sem("pT_turned"), val(pairs0 + c + 1, per, e))
                    k = 2 * (c - PHASE_PAIRS[0 if c < 6 else 1][0])
                    for i in range(tiles):
                        b = (7 if i == 2 else 6) if tiles == 3 else 6 + c % 2
                        o = (i % 2) * PAIR
                        last = nc.scalar.copy(prodT[0][:, k:k + 2, i * P:(i + 1) * P],
                                              ps[:, b, o:o + PAIR].rearrange("p (j n) -> p j n", j=2))
                    last.then_inc(sem("pT_hi"), 1)
                u = 0
                for phase in (0, 1):
                    waiting = None
                    for c in PHASE_PAIRS[phase]:
                        for half in (0, 1):
                            splits(u)
                            u += 1
                            if half == 0 and waiting is not None:
                                hidden_hi(waiting)
                        waiting = c
                        act.wait_ge(sem("w_used"), val(unit(u - 1) + 1, FFN_UNITS, e))
                        for i in range(tiles):
                            b = (c + phase) % 2 * tiles + i
                            last = nc.scalar.activation(prod[:, i, :], ps[:, b, 0:PAIR], ACT.Silu)
                        last.then_inc(sem("sg_ready"), 1)
                    for d_ in range(len(PHASE_DOWN[phase])):
                        splits(u)
                        u += 1
                        if d_ == 0:
                            hidden_hi(waiting)
                    after_phase(phase, u)

            ffn(dense_unit, TILES, None, lambda u: split(dense_unit(u)),
                lambda phase, u: modulations(MOD_IN_FFN if phase == 0 else []))
            act.wait_ge(sem("folded"), 2)
            modulate(2 * KD, 4, 5)
            for f in range(4):
                for third in range(3):
                    unit = AT["conv", f] + third
                    split(unit)
                    for j in (0, 1):
                        m = 6 * f + 2 * third + j
                        if j == 0:
                            act.wait_ge(sem("conv_out"), 3 * f + third + 1)
                        else:
                            act.wait_ge(sem("w_used"), unit + 1)
                        if third == 0:
                            if f:
                                act.wait_ge(sem("z_ready"), 2 * (f - 1) + j + 1)
                            nc.scalar.copy(conv_c[:, j, :], ps[:, m % 6, 0:T_ALL]).then_inc(sem("conv_c_in"), 1)
                        if third == 2:
                            act.wait_ge(sem("by_ready"), 2 * f + j + 1)
                            nc.scalar.copy(byT[0][:, 2 * f + j, :], conv_y[:, j, :]).then_inc(sem("by_hi"), 1)
                modulations(MOD_AFTER_CONV[f])
            for u in range(4):
                split(U_OUT1 + u)
            modulations(MOD_LAST)
            act.wait_ge(sem("folded"), 3)
            modulate(3 * KD, 6, 7, dst=hfT)
            for n in range(2 * TILES):
                i, q = n // 2, n % 2
                act.wait_ge(sem("Ht_turned"), n + 1)
                nc.scalar.copy(H_tok[0][:, i, q * 512:(q + 1) * 512], ps[:, 4 + n % 2, :]).then_inc(sem("Ht_hi"), 1)
            act.wait_ge(sem("chosen_max"), 1)
            nc.scalar.activation(small[:, 8:8 + TILES], small[:, 0:TILES], ACT.Exp).then_inc(sem("gate_exp"), 1)
            act.wait_ge(sem("counts_ready"), 2)

            def rows_in(g, bank, rows):
                for half in (0, 1):
                    act.wait_ge(sem("g_out"), g * 2 + (half + 1))
                    nc.scalar.copy(rows[:, 2 * half:2 * half + 2, :],
                                   ps[:, bank + half, :].rearrange("p (a n) -> p a n", a=2)).then_inc(sem("g_in"), 1)

            def gathered_hi(g, bank, s):
                for half in (0, 1):
                    act.wait_ge(sem("g_turned"), g * 2 + (half + 1))
                    nc.scalar.copy(gT[0][:, 4 * half:4 * half + 4, s * P:(s + 1) * P],
                                   ps[:, bank + half, :].rearrange("p (k n) -> p k n", k=4)).then_inc(sem("g_hi"), 1)

            def selection_in(g, bank, slot):
                act.wait_ge(sem("selT_out"), g + 1)
                nc.scalar.copy(selT[:, slot, :], ps[:, bank, 0:T_ALL]).then_inc(sem("selT_ready"), 1)

            rows_in(0, 4, g_rows)
            gathered_hi(0, 4, 0)
            with act.Fori(0, N_EXP) as e:
                count = act.value_load(counts[0:1, 0, ds(e, 1)], min_val=0, max_val=T_ALL)
                tiles0 = act.value_load(counts[0:1, 1, ds(e, 1)], min_val=0, max_val=3 * N_EXP)
                scat0 = act.value_load(counts[0:1, 2, ds(e, 1)], min_val=0, max_val=6 * N_EXP)

                def expert(tiles):
                    bank = 6 if tiles == 3 else 4
                    if tiles > 1:
                        selection_in(tiles0, bank, tiles - 1)
                        for s in range(1, tiles):
                            g = tiles0 + s
                            rows_in(g, bank, g_rows_more)
                            gathered_hi(g, bank, s)
                            selection_in(g, bank, tiles - 1 - s)

                    def splits(u):
                        split_in_loop(act, act_split, u, e)
                        if tiles == 1 and u == 5:
                            selection_in(tiles0, bank, 0)
                        elif u == GATHER_AT + 1:
                            rows_in(tiles0 + tiles, bank, g_rows)
                        elif u == GATHER_AT + 3:
                            gathered_hi(tiles0 + tiles, bank, 0)

                    def stage(phase, u):
                        if tiles == 1 and phase == 0:
                            return
                        act.wait_ge(sem("w_used"), val(expert_unit(u), FFN_UNITS, e))
                        for s in range(tiles):
                            last = phase == 1 and s == tiles - 1
                            if not last:
                                act.wait_ge(sem("y_out"), (scat0 + (1 + phase * tiles + s)) * 6)
                            b = 2 if tiles == 1 else 2 * s
                            nc.scalar.copy((y_last if last else y_st)[0][:, :, :],
                                           ps[:, b:b + 2, :].rearrange("p h (a n) -> p (h a) n", a=2)).then_inc(sem("yst_hi"), 1)
                    ffn(expert_unit, tiles, e, splits, stage)

                with act.If(count > P):
                    with act.If(count > 2 * P):
                        expert(3)
                    with act.Else():
                        expert(2)
                    act.nop()
                with act.Else():
                    expert(1)
                act.nop()

        @block.vector
        def _(dve):
            split = splitter(lambda n: dve_split(dve, n))
            step = [0]
            tt, ts = nc.vector.tensor_tensor, nc.vector.tensor_scalar
            stt = nc.vector.scalar_tensor_tensor

            def chain(ins):
                step[0] += 1
                ins.then_inc(sem("dve_step"), 1)
                dve.wait_ge(sem("dve_step"), step[0])

            def mod_out(g):
                layer, v, half = MOD_CHUNKS[g]
                posts = MOD_POSTS[MOD_ORDER.index(g)]
                if v % 3 == 2:
                    if half == 0:
                        dve.wait_ge(sem("gbias_in"), 16 * (2 * layer + v // 3 + 1))
                    for cond in (0, 1):
                        dve.wait_ge(sem("post_ready"), posts + cond + 1)
                        cols = slice(half * 512, half * 512 + 512)
                        tt(gate_bc[:, cond, cols], ps[:, 7, :], gate_bias[:, cols], ALU.add).then_inc(sem("post_done"), 1)
                else:
                    dve.wait_ge(sem("post_ready"), posts + 1)
                    bcol = (cols0[:, R_BMOD:R_BMOD + 48] if layer == 0 else cols1[:, 0:48])
                    b = bcol[:, v * KD + 4 * half:v * KD + 4 * half + 4].unsqueeze(2).broadcast_to([P, 4, 2])
                    src = ps[:, 7, 0:8].rearrange("p (k c) -> p k c", c=2)
                    slot = 4 * layer + 2 * (v // 3) + v % 3
                    stt(mod_col[:, slot, 4 * half:4 * half + 4, :], src, float(v % 3), b, ALU.add, ALU.add).then_inc(sem("post_done"), 1)

            pending = []

            def modulations(chunks, flush=False):
                for g in chunks:
                    split(AT["mod", g])
                    if pending:
                        mod_out(pending.pop())
                    split(AT["mod", g] + 1)
                    pending.append(g)
                if flush and pending:
                    mod_out(pending.pop())

            def fold(k, posts):
                shift, scale = mod_col[:, 2 * (k + 1), :, :], mod_col[:, 2 * (k + 1) + 1, :, :]
                g, b = (cols1[:, 48 + 16 * k + 8 * v:56 + 16 * k + 8 * v].unsqueeze(2).broadcast_to([P, KD, 2]) for v in (0, 1))
                dve.wait_ge(sem("post_done"), posts)
                tmp = small[:, 16:32].rearrange("p (k c) -> p k c", c=2)
                chain(tt(tmp, scale, b, ALU.mult))
                chain(tt(shift, shift, tmp, ALU.add))
                tt(scale, scale, g, ALU.mult).then_inc(sem("folded"), 1)

            def split_h(first):
                for k in range(KD):
                    dve.wait_ge(sem("hf_ready"), first + k + 1)
                    nc.vector.tensor_copy(hT[0][:, k, :], hf[:, k % 2, :]).then_inc(sem("hT_hi"), 1)
                    dve.wait_ge(sem("hT_hi"), first + k + 1)
                    tt(hT[1][:, k, :], hf[:, k % 2, :], hT[0][:, k, :].bitcast(F32), ALU.subtract).then_inc(sem("hT_ready"), 1)

            def layer_norm(k, ready, src):
                for i in range(TILES):
                    ready(i)
                    if k:
                        dve.wait_ge(sem("x_full"), TILES * (k - 1) + i + 1)
                    cond = min(i, 1)
                    g = gate_bc[:, cond, :]
                    s = src(i)
                    y, g = (Y[:, i, :].rearrange("p (a n) -> p a n", a=2), g.rearrange("p (a n) -> p a n", a=2)) \
                        if len(s.shape) == 3 else (Y[:, i, :], g)
                    chain(tt(y, s, g, ALU.mult))
                    chain(stt(X[:, i, :], X[:, i, :], ALPHA, Y[:, i, :], ALU.mult, ALU.add))
                    for a in (0, 1):
                        chain(nc.vector.bn_stats(stats[:, i, a, :], X[:, i, a * 512:(a + 1) * 512]))
                    chain(nc.vector.bn_aggr(mv[:, i, 0:2], stats[:, i, :, :].rearrange("p a n -> p (a n)")))
                    ts(mv[:, i, 2:3], mv[:, i, 1:2], LN_EPS, None, ALU.add).then_inc(sem("ln_var"), 1)
                for i in range(TILES):
                    dve.wait_ge(sem("ln_pow"), TILES * k + i + 1)
                    if k < 3:
                        ts(X[:, i, :], X[:, i, :], mv[:, i, 0:1], mv[:, i, 3:4], ALU.subtract, ALU.mult).then_inc(sem("x_ready"), 1)
                        continue
                    dve.wait_ge(sem("ln_rows_in"), 32 * (k + 1))
                    chain(ts(X[:, i, :], X[:, i, :], mv[:, i, 0:1], mv[:, i, 3:4], ALU.subtract, ALU.mult))
                    chain(tt(X[:, i, :], X[:, i, :], last_rows[:, 0, :], ALU.mult))
                    tt(X[:, i, :], X[:, i, :], last_rows[:, 1, :], ALU.add).then_inc(sem("x_ready"), 1)

            dve.wait_ge(sem("cond_hi"), 1)
            chain(tt(cond_lo[:, :], cond_f[:, :], cond_hi[:, :].bitcast(F32), ALU.subtract))
            for g, (src, o) in enumerate(((cond_hi, 0), (cond_lo, 0), (cond_hi, 8), (cond_lo, 8))):
                nc.vector.tensor_copy(st_cond[:, :, 32 * g:32 * g + 32],
                                      src[:, o:o + 8].bitcast(F32).unsqueeze(2).broadcast_to([P, KD, 32])).then_inc(sem("cond_ready"), 1)
            dve.wait_ge(sem("dec_in"), 32)
            chain(ts(small[:, 32:48], lg[:, :], -1.0, None, ALU.mult))
            chain(tt(small[:, 32:48], small[:, 32:48], lg[:, :], ALU.min))
            ts(small[:, 32:48], small[:, 32:48], 1.0, None, ALU.mult).then_inc(sem("lsig_in"), 1)
            dve.wait_ge(sem("lsig_exp"), 1)
            u_, s_ = small[:, 48:64], small[:, 32:48]
            chain(ts(s_, u_, 2.0, None, ALU.add))
            chain(nc.vector.reciprocal(s_, s_))
            chain(tt(u_, u_, s_, ALU.mult))
            chain(tt(s_, u_, u_, ALU.mult))
            pl = small[:, 0:16]
            chain(ts(pl, s_, 1.0 / 17, None, ALU.mult))
            for m in range(15, 1, -2):
                chain(stt(pl, pl, 1.0 / m, s_, ALU.add, ALU.mult))
            chain(stt(pl, pl, 1.0, u_, ALU.add, ALU.mult))
            chain(ts(lg[:, :], lg[:, :], 0.0, None, ALU.min))
            stt(lg[:, :], pl, -2.0, lg[:, :], ALU.mult, ALU.add).then_inc(sem("lg_ready"), 1)
            dve.wait_ge(sem("lg_ready"), 1)

            dve.wait_ge(sem("cols_done"), 2)
            modulations(MOD_FIRST, flush=True)
            split_h(0)
            for c in (0, 1):
                for m in range(2 - c):
                    split(AT["proj", c] + m)
                modulations(MOD_AFTER_PROJ[c])
            dve.wait_ge(sem("rms_ss"), 2 * TILES)
            chain(ts(small[:, 0:3], small[:, 16:19], 1.0 / Q_LORA, RMS_EPS, ALU.mult, ALU.add))
            ts(small[:, 3:6], small[:, 19:22], 1.0 / KV_LORA, RMS_EPS, ALU.mult, ALU.add).then_inc(sem("rms_ms"), 1)
            for c in range(2, 6):
                for m in range(2):
                    split(AT["proj", c] + m)
                modulations(MOD_AFTER_PROJ[c])
            modulations([], flush=True)
            fold(0, MOD_POSTS[MOD_ORDER.index(10)])
            fold(1, MOD_POSTS[MOD_ORDER.index(10)])
            dve.wait_ge(sem("rms_pow"), 1)
            dve.wait_ge(sem("cache_in"), 32)
            cosq, sinq = (cst(x).rearrange("p (i d) -> p i d", i=TILES) for x in ("cos_q", "sin_q"))
            for i in range(TILES):
                stt(proj[:, i, C_KV:C_KV + KV_LORA], proj[:, i, C_KV:C_KV + KV_LORA], small[:, 11 + i:12 + i],
                    kv_gain[:, :], ALU.mult, ALU.mult)
                ts(proj[:, i, 0:Q_LORA], proj[:, i, 0:Q_LORA], small[:, 8 + i:9 + i], None, ALU.mult).then_inc(sem("ckv_ready"), 1)
            rope(tt, chain, kpe_r[:, :, :], proj[:, :, C_PE:C_PE + ROPE], cosq, sinq,
                 rope_tmp[:, :, 0:ROPE]).then_inc(sem("kpe_r"), 1)
            dve.wait_ge(sem("kpe_r"), 1)
            nc.vector.tensor_copy(kpe4[:, 0:3, :, :], kpe_r[:, :, :].unsqueeze(2).broadcast_to([P, 3, 4, ROPE]))
            dve.wait_ge(sem("kpe_in"), 16)
            nc.vector.tensor_copy(kpe4[:, 3, 1:4, :], kpe4[:, 3, 0:1, :].broadcast_to([P, 3, ROPE])).then_inc(sem("kpe4_ready"), 1)
            for m in range(KKV + KQ):
                dve.wait_ge(sem("lat_hi"), m + 1)
                b = 6 + m % 2
                if m < KKV:
                    tt(ckvT[1][:, m, :], ps[:, b, :], ckvT[0][:, m, :].bitcast(F32), ALU.subtract).then_inc(sem("lat_lo"), 1)
                else:
                    k = m - KKV
                    stt(qnT[1][:, k, :], ps[:, b, 0:T_ALL], cols0[:, R_QG + k:R_QG + k + 1],
                        qnT[0][:, k, :].bitcast(F32), ALU.mult, ALU.subtract).then_inc(sem("lat_lo"), 1)
            split(U_KV)
            split(U_QA)
            split(U_QB)
            for i in range(TILES):
                dve.wait_ge(sem("mla_in"), 13 + i)
                v = qR[:, i, :].rearrange("p (h d) -> p h d", h=HEADS)
                rope(tt, chain, v, v, cosq[:, i:i + 1, :].broadcast_to([P, HEADS, ROPE]),
                     sinq[:, i:i + 1, :].broadcast_to([P, HEADS, ROPE]),
                     rope_tmp[:, i, :].rearrange("p (h d) -> p h d", h=HEADS)).then_inc(sem("qR_ready"), 1)
            items = TILES * HEADS

            def maximum(m):
                w_ = P if m < HEADS else 3 * P
                dve.wait_ge(sem("s_ready"), m + 1)
                if m >= 2:
                    dve.wait_ge(sem("e_ready"), m - 1)
                nc.vector.tensor_reduce(mx[:, m % 2, 0:1], ps[:, m % 2, 0:w_], AX, ALU.max).then_inc(sem("mx_raw"), 1)
                dve.wait_ge(sem("mx_raw"), m + 1)
                ts(mx[:, m % 2, 1:2], mx[:, m % 2, 0:1], -ATT_SCALE, None, ALU.mult).then_inc(sem("mx_ready"), 1)

            def weights_in(m):
                w_ = P if m < HEADS else 3 * P
                dve.wait_ge(sem("eT_turned"), m + 1)
                if m >= 2:
                    dve.wait_ge(sem("o_ready"), m - 1)
                nc.vector.tensor_copy(ET[:, m % 2, 0:w_], ps[:, 2 + m % 2, 0:w_]).then_inc(sem("eT_ready"), 1)

            for m in range(items + 1):
                if m < items:
                    maximum(m)
                if m >= 1:
                    weights_in(m - 1)
            dve.wait_ge(sem("ret_roped"), 2 * TILES)
            for i in range(TILES):
                dve.wait_ge(sem("o_ready"), HEADS * (i + 1))
                dve.wait_ge(sem("e_ready"), HEADS * (i + 1))
                chain(nc.vector.reciprocal(den[:, i, :], den[:, i, :]))
                tt(mix[0][:, i, :].rearrange("p (h d) -> p h d", h=HEADS),
                   ps[:, 4 + i, :].rearrange("p (h d) -> p h d", h=HEADS),
                   den[:, i, :].unsqueeze(2).broadcast_to([P, HEADS, DV]), ALU.mult).then_inc(sem("att_done"), 1)

            heads = lambda ap: ap.rearrange("p (h d) -> p h d", h=HEADS)
            over = lambda j: dec[:, j, :].unsqueeze(2).broadcast_to([P, HEADS, DV])
            dve.wait_ge(sem("dec_ready"), 1)
            dve.wait_ge(sem("ret_roped"), 2 * TILES)
            dve.wait_ge(sem("att_done"), TILES)
            for j, (i, d_) in enumerate(((0, 1), (0, 2), (1, 1), (2, 2))):
                tt(heads(k_dec[:, j, :]), heads(proj[:, i, C_RK:C_RK + HD]), over(d_), ALU.mult).then_inc(sem("k_dec_ready"), 1)
            for i in (1, 2):
                for d_ in (0, 1):
                    if i == 2:
                        dve.wait_ge(sem("ret_turned"), 9 + d_)
                    tt(heads(q_dec[:, d_, :]), heads(proj[:, i, C_RQ:C_RQ + HD]), over(0 if d_ == 0 else 3),
                       ALU.mult).then_inc(sem("q_dec_ready"), 1)
            dve.wait_ge(sem("mask_exp"), 1)
            over_h = lambda j: mask_c[:, j:j + 1, :].broadcast_to([P, HEADS, P])
            chain(tt(mask[:, :, :], mask[:, :, :], over_h(2), ALU.mult))
            chain(tt(mask_b[:, :, :], mask_b[:, :, :], over_h(3), ALU.mult))
            chain(tt(mask[:, :, :], mask[:, :, :], mask_b[:, :, :], ALU.add))
            dve.wait_ge(sem("s0_in"), 16 * 4)
            for d_ in (0, 1):
                chain(tt(s1[:, d_, :, :], s0[:, d_, :, :], cdec[:, d_, :].unsqueeze(2).broadcast_to([P, 4, DV]), ALU.mult))
                dve.wait_ge(sem("state_out"), 3 + d_)
                tt(s1[:, d_, :, :], ps[:, 2, 0:4 * DV].rearrange("p (c v) -> p c v", c=4), s1[:, d_, :, :],
                   ALU.add).then_inc(sem("state_in"), 1)

            def masked(m):
                dve.wait_ge(sem("rs_out"), m + 1)
                tt(ret_s[:, m % 2, :, :], ps[:, m % 2, :].rearrange("p (j n) -> p j n", j=4),
                   mask[:, m % 2::2, :], ALU.mult).then_inc(sem("rs_ready"), 1)

            def head_norm(i):
                dve.wait_ge(sem("ret_out"), i + 1)
                sm = small[:, 16:24]
                chain(nc.vector.tensor_reduce(sm, heads(ps[:, 4 + i, :]), AX, ALU.add))
                chain(ts(sm, sm, 1.0 / DV, None, ALU.mult))
                y = heads(mix[1][:, i, :])
                chain(tt(y, heads(ps[:, 4 + i, :]), sm.unsqueeze(2).broadcast_to([P, HEADS, DV]), ALU.subtract))
                chain(tt(heads(hn[:, :]), y, y, ALU.mult))
                chain(nc.vector.tensor_reduce(sm, heads(hn[:, :]), AX, ALU.add))
                ts(sm, sm, 1.0 / DV, LN_EPS, ALU.mult, ALU.add).then_inc(sem("hn_var"), 1)
                chain(tt(y, y, heads(proj[:, i, C_RG:C_RG + HD]), ALU.mult))
                dve.wait_ge(sem("hn_pow"), i + 1)
                tt(y, y, small[:, 24:32].unsqueeze(2).broadcast_to([P, HEADS, DV]), ALU.mult).then_inc(sem("mix_ready"), 1)
                dve.wait_ge(sem("mix_ready"), i + 1)

            dve.wait_ge(sem("rg_ready"), TILES)
            for m in range(6):
                if m % 2 == 0 and m >= 2:
                    dve.wait_ge(sem("ret_out"), m // 2)
                masked(m)
                if m % 2 == 1 and m >= 3:
                    head_norm(m // 2 - 1)
            head_norm(2)
            for k in range(KD):
                dve.wait_ge(sem("mixT_hi"), k + 1)
                tt(mixT[1][:, k, :], ps[:, k % 2, 0:T_ALL], mixT[0][:, k, :].bitcast(F32), ALU.subtract).then_inc(sem("mixT_ready"), 1)
            for u in range(4):
                split(U_OUT0 + u)
            acc = lambda i: ps[:, 2 * i:2 * i + 2, :]
            layer_norm(0, lambda i: dve.wait_ge(sem("w_used"), U_OUT0 + 4), acc)
            split_h(KD)

            def ffn(unit, tiles, e, splits, after_phase):
                pairs0 = 0 if e is None else PAIRS
                per = None if e is None else PAIRS

                def hidden_lo(c):
                    dve.wait_ge(sem("pT_hi"), val(pairs0 + c + 1, per, e))
                    k = 2 * (c - PHASE_PAIRS[0 if c < 6 else 1][0])
                    for i in range(tiles):
                        b = (7 if i == 2 else 6) if tiles == 3 else 6 + c % 2
                        o = (i % 2) * PAIR
                        last = tt(prodT[1][:, k:k + 2, i * P:(i + 1) * P],
                                  ps[:, b, o:o + PAIR].rearrange("p (j n) -> p j n", j=2),
                                  prodT[0][:, k:k + 2, i * P:(i + 1) * P].bitcast(F32), ALU.subtract)
                    last.then_inc(sem("pT_lo"), 1)
                u = 0
                for phase in (0, 1):
                    waiting = None
                    for c in PHASE_PAIRS[phase]:
                        for half in (0, 1):
                            splits(u)
                            u += 1
                            if half == 0 and waiting is not None:
                                hidden_lo(waiting)
                        waiting = c
                        dve.wait_ge(sem("sg_ready"), val(pairs0 + c + 1, per, e))
                        for i in range(tiles):
                            b = (c + phase) % 2 * tiles + i
                            last = tt(prod[:, i, :], prod[:, i, :], ps[:, b, PAIR:2 * PAIR], ALU.mult)
                        last.then_inc(sem("prod_ready"), 1)
                    for d_ in range(len(PHASE_DOWN[phase])):
                        splits(u)
                        u += 1
                        if d_ == 0:
                            hidden_lo(waiting)
                    after_phase(phase, u)

            def dense_phase(phase, u):
                dve.wait_ge(sem("w_used"), dense_unit(u - 1) + 1)
                for i in range(TILES):
                    y = Y[:, i, :].rearrange("p (a n) -> p a n", a=2)
                    last = nc.vector.tensor_copy(y, acc(i)) if phase == 0 else tt(y, acc(i), y, ALU.add)
                last.then_inc(sem("dense_in"), 1)
                dve.wait_ge(sem("dense_in"), phase + 1)
                if phase == 0:
                    modulations(MOD_IN_FFN, flush=True)
            ffn(dense_unit, TILES, None, lambda u: split(dense_unit(u)), dense_phase)
            layer_norm(1, lambda i: None, lambda i: Y[:, i, :])
            split_h(2 * KD)

            spans = ((0, 0, P), (P + 2, P, 2 * P))
            zz = zpad[:, :, :]
            for a in (0, P + 1, P + 2, T_ALL + 3):
                last = nc.vector.memset(zz[:, :, a:a + 1], 0.0)
                chain(last)
            cw = lambda tap, k: cols0[:, R_CONVW + tap * KD + k:R_CONVW + tap * KD + k + 1]
            for f in range(4):
                for third in range(3):
                    unit = AT["conv", f] + third
                    split(unit)
                    for j in (0, 1):
                        m, k = 6 * f + 2 * third + j, 2 * f + j
                        bank = ps[:, m % 6, :]
                        if third == 1:
                            dve.wait_ge(sem("conv_c_in"), k + 1)
                            if j == 0:
                                dve.wait_ge(sem("conv_out"), 3 * f + third + 1)
                            else:
                                dve.wait_ge(sem("w_used"), unit + 1)
                            for z0, t0, nt in spans:
                                last = tt(zz[:, j, z0 + 1:z0 + 1 + nt], bank[:, t0:t0 + nt], conv_c[:, j, t0:t0 + nt], ALU.mult)
                            last.then_inc(sem("z_ready"), 1)
                            dve.wait_ge(sem("z_ready"), k + 1)
                            if f:
                                dve.wait_ge(sem("by_hi"), 2 * (f - 1) + j + 1)
                            for z0, t0, nt in spans:
                                y = conv_y[:, j, t0:t0 + nt]
                                chain(ts(y, zz[:, j, z0:z0 + nt], cw(0, k), None, ALU.mult))
                                chain(stt(y, zz[:, j, z0 + 1:z0 + 1 + nt], cw(1, k), y, ALU.mult, ALU.add))
                                chain(stt(y, zz[:, j, z0 + 2:z0 + 2 + nt], cw(2, k), y, ALU.mult, ALU.add))
                        elif third == 2:
                            if j == 0:
                                dve.wait_ge(sem("conv_out"), 3 * f + third + 1)
                            else:
                                dve.wait_ge(sem("w_used"), unit + 1)
                            tt(conv_y[:, j, :], bank[:, 0:T_ALL], conv_y[:, j, :], ALU.mult).then_inc(sem("by_ready"), 1)
                            dve.wait_ge(sem("by_hi"), k + 1)
                            tt(byT[1][:, k, :], conv_y[:, j, :], byT[0][:, k, :].bitcast(F32), ALU.subtract).then_inc(sem("by_lo"), 1)
                modulations(MOD_AFTER_CONV[f])
            modulations([], flush=True)
            fold(2, MOD_POSTS[MOD_ORDER.index(22)])
            for u in range(4):
                split(U_OUT1 + u)
            layer_norm(2, lambda i: dve.wait_ge(sem("w_used"), U_OUT1 + 4), acc)
            modulations(MOD_LAST, flush=True)

            for n in range(2 * TILES):
                i, q = n // 2, n % 2
                dve.wait_ge(sem("Ht_hi"), n + 1)
                tt(H_tok[1][:, i, q * 512:(q + 1) * 512], ps[:, 4 + n % 2, :],
                   H_tok[0][:, i, q * 512:(q + 1) * 512].bitcast(F32), ALU.subtract).then_inc(sem("Ht_lo"), 1)
            dve.wait_ge(sem("logits_out"), 1)
            R = lambda j: rt[:, j, :, :]
            per_tile = lambda ap: ap.unsqueeze(2).broadcast_to([P, TILES, N_EXP])
            b8 = lambda ap: ap.unsqueeze(1).broadcast_to([P, TILES, N_EXP])
            dve.wait_ge(sem("rtr_in"), 32)
            chain(tt(R(1), ps[:, 2, 0:24].rearrange("p (i n) -> p i n", i=TILES), b8(rt_bias[:, :]), ALU.add))
            m1, m2, ix = small[:, 32:35], small[:, 36:39], small[:, 40:43]

            def best(logits, top, eq, one):
                chain(nc.vector.tensor_reduce(top, logits, AX, ALU.max))
                chain(tt(eq, logits, per_tile(top), ALU.is_equal))
                chain(tt(eq, eq, b8(cst("rank8")), ALU.mult))
                chain(nc.vector.tensor_reduce(ix, eq, AX, ALU.max))
                chain(tt(one, eq, per_tile(ix), ALU.is_equal))
            best(R(1), m1, R(2), R(3))
            chain(stt(R(4), R(3), -1e30, R(1), ALU.mult, ALU.add))
            best(R(4), m2, R(2), R(5))
            tt(R(0), R(3), R(5), ALU.add).then_inc(sem("chosen"), 1)
            dve.wait_ge(sem("chosen"), 1)
            tt(small[:, 0:TILES], m2, m1, ALU.subtract).then_inc(sem("chosen_max"), 1)
            dve.wait_ge(sem("gate_exp"), 1)
            ex, w1 = small[:, 8:11], small[:, 16:19]
            chain(ts(w1, ex, 1.0, None, ALU.add))
            chain(nc.vector.reciprocal(w1, w1))
            chain(tt(ex, ex, w1, ALU.mult))
            chain(tt(R(3), R(3), per_tile(w1), ALU.mult))
            chain(tt(R(5), R(5), per_tile(ex), ALU.mult))
            chain(nc.vector.memset(comb[:, :, 0:1], 0.0))
            chain(tt(comb[:, :, 1:N_EXP + 1], R(3), R(5), ALU.add))
            dve.wait_ge(sem("ranks_out"), 1)
            chain(nc.vector.memset(posm[:, :, N_EXP:], -1.0))
            pm = posm[:, :, 0:N_EXP]
            chain(stt(pm, ps[:, 3, 0:24].rearrange("p (i n) -> p i n", i=TILES), 1.0, R(0), ALU.add, ALU.mult))
            chain(ts(pm, pm, -1.0, None, ALU.add))
            cnt, big, huge, run = (rt[:, 6 + j, 0, :] for j in range(4))
            chain(nc.vector.tensor_copy(cnt, ps[:, 3, 24:32]))
            chain(ts(big, cnt, float(P), None, ALU.is_gt))
            chain(ts(huge, cnt, float(2 * P), None, ALU.is_gt))
            chain(nc.vector.tensor_copy(counts[:, 0, 0:N_EXP], cnt))
            for row, (w_big, w_huge) in ((1, (1.0, 1.0)), (2, (3.0, 2.0))):
                chain(ts(run, huge, w_huge, 1.0, ALU.mult, ALU.add))
                chain(stt(run, big, w_big, run, ALU.mult, ALU.add))
                before = rt[:, 10 + row - 1, :, :].rearrange("p i n -> p (i n)")[:, 0:N_EXP + 1]
                chain(nc.vector.memset(before, 0.0))
                for e_ in range(1, N_EXP + 1):
                    chain(tt(before[:, e_:e_ + 1], before[:, e_ - 1:e_], run[:, e_ - 1:e_], ALU.add))
                nc.vector.tensor_copy(counts[:, row, :], before).then_inc(sem("counts_ready"), 1)
            dve.wait_ge(sem("counts_ready"), 2)
            for m in range(6):
                nc.vector.memset(Y[:, m // 2, (m % 2) * 512:(m % 2) * 512 + 512], 0.0).then_inc(sem("y_added"), 1)

            for x in (0, 1):
                nc.vector.memset(y_last[x].bitcast(F32), 0.0)
            chain(nc.vector.memset(selT[:, 0, :].bitcast(F32), 0.0))
            dve.nop().then_inc(sem("yst_lo"), 1)

            def select(g, s, column):
                for i in range(TILES):
                    last = ts(sel[:, i, :], cst("iota"), float(s * P), posm[:, i, column], ALU.add, ALU.is_equal)
                last.then_inc(sem("sel_ready"), 1)

            def gathered_lo(g, bank, s):
                for half in (0, 1):
                    cols = slice(s * P, (s + 1) * P)
                    dve.wait_ge(sem("g_hi"), g * 2 + (half + 1))
                    tt(gT[1][:, 4 * half:4 * half + 4, cols], ps[:, bank + half, :].rearrange("p (k n) -> p k n", k=4),
                       gT[0][:, 4 * half:4 * half + 4, cols].bitcast(F32), ALU.subtract).then_inc(sem("g_lo"), 1)

            def add_scatter(q, bank, column, steps):
                for m in steps:
                    i, half = m // 2, m % 2
                    y = Y[:, i, half * 512:half * 512 + 512]
                    dve.wait_ge(sem("y_added"), q * 6 + (m + 1))
                    dve.wait_ge(sem("y_out"), q * 6 + (m + 1))
                    stt(y, ps[:, bank + m % 2, :], comb[:, i, column], y, ALU.mult, ALU.add).then_inc(sem("y_added"), 1)

            select(0, 0, slice(0, 1))
            gathered_lo(0, 4, 0)
            with dve.Fori(0, N_EXP) as e:
                count = dve.value_load(counts[0:1, 0, ds(e, 1)], min_val=0, max_val=T_ALL)
                tiles0 = dve.value_load(counts[0:1, 1, ds(e, 1)], min_val=0, max_val=3 * N_EXP)
                scat0 = dve.value_load(counts[0:1, 2, ds(e, 1)], min_val=0, max_val=6 * N_EXP)

                def expert(tiles):
                    bank = 6 if tiles == 3 else 4
                    if tiles > 1:
                        add_scatter(scat0, bank, ds(e, 1), range(6))
                        for s in range(1, tiles):
                            g = tiles0 + s
                            dve.wait_ge(sem("selT_out"), g)
                            select(g, s, ds(e, 1))
                            gathered_lo(g, bank, s)

                    def splits(u):
                        split_in_loop(dve, dve_split, u, e)
                        if tiles == 1 and 1 <= u < 4:
                            add_scatter(scat0, bank, ds(e, 1), range(2 * u - 2, 2 * u))
                        elif u == GATHER_AT - 1:
                            dve.wait_ge(sem("selT_out"), tiles0 + tiles)
                            select(tiles0 + tiles, 0, ds(e + 1, 1))
                        elif u == GATHER_AT + 3:
                            gathered_lo(tiles0 + tiles, bank, 0)

                    def way_back(phase, u):
                        if tiles == 1 and phase == 0:
                            return
                        for s in range(tiles):
                            q = scat0 + (1 + phase * tiles + s)
                            last = phase == 1 and s == tiles - 1
                            y = y_last if last else y_st
                            b = 2 if tiles == 1 else 2 * s
                            dve.wait_ge(sem("yst_hi"), q if tiles > 1 else scat0 + 1)
                            tt(y[1][:, :, :], ps[:, b:b + 2, :].rearrange("p h (a n) -> p (h a) n", a=2),
                               y[0][:, :, :].bitcast(F32), ALU.subtract).then_inc(sem("yst_lo"), 1)
                            if not last:
                                add_scatter(q, bank, ds(e + 1, 1), range(6))
                    ffn(expert_unit, tiles, e, splits, way_back)

                with dve.If(count > P):
                    with dve.If(count > 2 * P):
                        expert(3)
                    with dve.Else():
                        expert(2)
                    dve.nop()
                with dve.Else():
                    expert(1)
                dve.nop()
            total = dve.value_load(counts[0:1, 2, N_EXP:N_EXP + 1], min_val=0, max_val=6 * N_EXP)
            add_scatter(total, 4, slice(N_EXP, N_EXP + 1), range(6))
            dve.drain().then_inc(sem("moe_done"), 1)
            dve.wait_ge(sem("moe_done"), 1)
            layer_norm(3, lambda i: None, lambda i: Y[:, i, :])


_OUTS = [((1, 128, 1024), "float32"), ((1, 256, 1024), "float32"), ((1, 1, 128, 256), "float32"),
         ((1, 1, 128, 32), "float32"), ((1, 1, 8, 64, 64), "float32"), ((1, 1, 8, 64, 64), "float32")]


def kernel(**inputs):
    import concourse.bacc as bacc
    from concourse.bass_utils import run_bass_kernel_spmd

    nc = bacc.Bacc("TRN2", target_bir_lowering=False, num_devices=1)
    arrays = {k: np.ascontiguousarray(v) for k, v in inputs.items()}
    q = arrays["w_q_b"].reshape(1, Q_LORA, HEADS, NOPE + ROPE)
    arrays["w_q_b"] = np.concatenate([q[..., :NOPE].reshape(1, Q_LORA, -1), q[..., NOPE:].reshape(1, Q_LORA, -1)], -1)
    kv = arrays["w_kv_b"].reshape(1, KV_LORA, HEADS, NOPE + DV)
    arrays["w_kv_b"] = np.concatenate([kv[..., :NOPE].reshape(1, KV_LORA, -1), kv[..., NOPE:].reshape(1, KV_LORA, -1)], -1)
    arrays |= {"const": CONST, "masks": MASKS, "ret_tables": RET_TABLES, "ranks": RANKS}
    feed, t = {}, {}
    for name, a in arrays.items():
        feed[f"in_{name}"] = a
        t[name] = nc.dram_tensor(f"in_{name}", a.shape, mybir.dt.from_np(a.dtype), kind="ExternalInput").ap()
    outs = [nc.dram_tensor(f"out_{i}", s, mybir.dt.from_np(np.dtype(d)), kind="ExternalOutput").ap()
            for i, (s, d) in enumerate(_OUTS)]
    build(nc, t, outs)
    r = run_bass_kernel_spmd(nc, [feed], core_ids=[0])
    return tuple(r.results[0][f"out_{i}"] for i in range(len(_OUTS)))
```

```python
from contextlib import ExitStack

import numpy as np
import concourse.bass as bass
from concourse import mybir
from concourse.bass import ds

F32 = mybir.dt.float32
F32R = mybir.dt.float32r
I32 = mybir.dt.int32
ALU = mybir.AluOpType
ACT = mybir.ActivationFunctionType
AX = mybir.AxisListType.X

P = 128
D = 1024
KD = D // P
TILES = 3
T_ALL = TILES * P
PAST = 128
Q_LORA, KV_LORA, ROPE, NOPE, HEADS, DV = 384, 256, 32, 64, 8, 64
HD = HEADS * DV
KQ, KKV = Q_LORA // P, KV_LORA // P
IN_EVEN = Q_LORA + KV_LORA + ROPE + 4 * HD
FF = 2816
N_EXP = 8
GRID_W = 64
ALPHA = (2.0 * 2) ** 0.25
ATT_SCALE = float(NOPE + ROPE) ** -0.5
RET_SCALE = float(DV) ** -0.5
LN_EPS, RMS_EPS = 1e-5, 1e-6

C_Q, C_KV, C_PE = 0, Q_LORA, Q_LORA + KV_LORA
C_RQ = C_PE + ROPE
C_RK, C_RV, C_RG = C_RQ + HD, C_RQ + 2 * HD, C_RQ + 3 * HD
PROJ_CHUNKS = [(0, 512), (512, C_RQ - 512), (C_RQ, 512), (C_RK, 512), (C_RV, 512), (C_RG, 512)]

UNIT = 2048
RAW = 3
SPLIT = 3
AHEAD = 2

PAIR = 256
PAIRS = FF // PAIR
PHASE_PAIRS = [range(0, 6), range(6, PAIRS)]
PHASE_DOWN = [[2] * len(p) for p in PHASE_PAIRS]
FFN_UNITS = 3 * PAIRS
GATHER_AT = FFN_UNITS - 5

MOD_CHUNKS = [(layer, v, h) for layer in (0, 1) for v in range(6) for h in (0, 1)]
MOD_FIRST = [0, 1, 2, 3]
MOD_AFTER_PROJ = [[4, 5], [6], [7, 8], [9, 12], [13, 14], [15]]
MOD_IN_FFN = [10, 11]
MOD_AFTER_CONV = [[16], [17, 18], [19, 20], [21]]
MOD_LAST = [22, 23]
MOD_ORDER = (MOD_FIRST + sum(MOD_AFTER_PROJ, []) + MOD_IN_FFN + sum(MOD_AFTER_CONV, []) + MOD_LAST)
MOD_POSTS = [sum(2 if MOD_CHUNKS[g][1] % 3 == 2 else 1 for g in MOD_ORDER[:i]) for i in range(len(MOD_ORDER) + 1)]
GATE_PLACE = [MOD_ORDER.index(g) for g in (4, 10, 16, 22)]
FFN_PHASE0 = 2 * len(PHASE_PAIRS[0]) + len(PHASE_DOWN[0])


def _stream():
    out, at = [], {}

    def add(name, n, key=None):
        at[name if key is None else (name, key)] = len(out)
        out.extend((name, key, i) for i in range(n))

    def mods(chunks):
        for g in chunks:
            add("mod", 2, g)
    mods(MOD_FIRST)
    for c, (_, width) in enumerate(PROJ_CHUNKS):
        add("proj", 2 if width == 512 else 1, c)
        mods(MOD_AFTER_PROJ[c])
    add("kv", 1), add("qa", 1), add("qb", 1), add("out0", 4)
    add("ffn", FFN_PHASE0, 0)
    mods(MOD_IN_FFN)
    add("ffn", FFN_UNITS - FFN_PHASE0, 1)
    for f in range(4):
        add("conv", 3, f)
        mods(MOD_AFTER_CONV[f])
    mods(MOD_LAST)
    add("out1", 4)
    return out, at


STREAM, AT = _stream()
U_MOE = len(STREAM)
U_KV, U_QA, U_QB, U_OUT0, U_OUT1 = (AT[x] for x in ("kv", "qa", "qb", "out0", "out1"))
assert FFN_UNITS % RAW == 0 and FFN_UNITS % SPLIT == 0


def dense_unit(u):
    return AT["ffn", 0] + u if u < FFN_PHASE0 else AT["ffn", 1] + u - FFN_PHASE0


def expert_unit(u):
    return U_MOE + u


R_COND, R_QG, R_CONVW, R_BMOD = 0, 16, 19, 43


def _constants():
    i = np.arange(P, dtype=np.float32)
    row, col = i[:, None], i[None, :]
    parts = {}
    parts["ident"] = np.eye(P, dtype=np.float32)
    parts["iota"] = np.broadcast_to(col, (P, P)).astype(np.float32)
    sel = np.zeros((P, 2, P), np.float32)
    sel[[0, 32], 0] = 1.0
    sel[[64, 96], 1] = 1.0
    parts["selrow"] = sel.reshape(P, -1)
    parts["selcol"] = np.ascontiguousarray(sel[:, :, 0])
    parts["decay_at"] = np.stack([i + 1, P - 1 - i, i, P - i], 1)
    parts["rank8"] = np.broadcast_to(100.0 - np.arange(8, dtype=np.float32), (P, 8)).astype(np.float32)
    parts["mhalf"] = np.full((P, 8), -0.5, np.float32)

    def tables(cos, sin):
        n = cos.shape[1]
        c = np.ones((TILES, P, 2 * n), np.float32)
        s = np.zeros((TILES, P, 2 * n), np.float32)
        c[1:] = np.repeat(cos, 2, axis=1).reshape(2, P, 2 * n)
        s[1:, :, 0::2] = -sin.reshape(2, P, n)
        s[1:, :, 1::2] = sin.reshape(2, P, n)
        return (a.transpose(1, 0, 2).reshape(P, -1) for a in (c, s))

    tok = np.arange(2 * P)
    n_freq = ROPE // 4
    freqs = (1.0 / (np.float32(10000.0) ** (np.arange(n_freq, dtype=np.float32) / n_freq))).astype(np.float32)
    r, c = (tok // GRID_W).astype(np.float32), (tok % GRID_W).astype(np.float32)
    ang = np.concatenate([r[:, None] * freqs, c[:, None] * freqs], -1)
    parts["cos_q"], parts["sin_q"] = tables(np.cos(ang), np.sin(ang))
    theta = (1.0 / (np.float32(10000.0) ** np.linspace(0.0, 1.0, DV // 2, dtype=np.float32))).astype(np.float32)
    ang = tok.astype(np.float32)[:, None] * theta
    ret_tables = np.concatenate(list(tables(np.cos(ang), np.sin(ang))), 1)
    ranks = np.concatenate([(row < col).astype(np.float32), np.ones((P, P), np.float32)], 1)
    at, cols = 0, {}
    for k, v in parts.items():
        cols[k] = (at, at + v.shape[1])
        at += v.shape[1]
    masks = np.concatenate([np.maximum(col - row, 0), np.maximum(row - col, 0),
                            (col >= row), (row >= col)], 1).astype(np.float32)
    return np.concatenate(list(parts.values()), 1).astype(np.float32), cols, masks, ret_tables, ranks


CONST, CONST_AT, MASKS, RET_TABLES, RANKS = _constants()


def weight_unit(w, n, expert=None):
    def chunk(mat, c0, width, k0, nk):
        half = (nk + 1) // 2
        src = mat.rearrange("(k p) n -> p k n", p=P)
        return [(b - a, src[:, k0 + a:k0 + b, c0:c0 + width]) for a, b in ((0, half), (half, nk))]

    def rows(mat, k0):
        src = mat.rearrange("(k p) n -> p k n", p=P)
        return [(1, src[:, k0 + a:k0 + a + 1, :]) for a in (0, 1)]

    def ffn(gate, up, down, i):
        for phase in (0, 1):
            pairs, downs = PHASE_PAIRS[phase], PHASE_DOWN[phase]
            if i < 2 * len(pairs):
                c, k0 = pairs[i // 2] * PAIR, 4 * (i % 2)
                return [(4, m.rearrange("(k p) n -> p k n", p=P)[:, k0:k0 + 4, c:c + PAIR]) for m in (gate, up)]
            i -= 2 * len(pairs)
            if i < len(downs):
                return rows(down, 2 * pairs[0] + 2 * i)
            i -= len(downs)

    if n >= U_MOE:
        return ffn(w["exp_gate"][0][expert], w["exp_up"][0][expert], w["exp_down"][0][expert], n - U_MOE)
    name, key, i = STREAM[n]
    if name == "mod":
        layer, v, half = MOD_CHUNKS[key]
        return chunk(w["w_mod"][layer], (2 * v + half) * 512, 512, 4 * i, 4)
    if name == "proj":
        c0, width = PROJ_CHUNKS[key]
        return chunk(w["w_in_mix"][0], c0, width, 4 * i, 4 if width == 512 else KD)
    if name == "kv":
        return rows(w["w_kv_b"][0], 0)
    if name == "qa":
        return chunk(w["w_q_b"][0], 0, HD, 0, KQ)
    if name == "qb":
        return chunk(w["w_q_b"][0], HD, HEADS * ROPE, 0, KQ)
    if name == "ffn":
        return ffn(w["ffn_gate"][0], w["ffn_up"][0], w["ffn_down"][0], i + FFN_PHASE0 * key)
    if name == "conv":
        return chunk(w["w_in_conv"][0], (1, 2, 0)[i] * D + key * 256, 256, 0, KD)
    return rows(w["w_out_mix" if name == "out0" else "w_out_conv"][0], 2 * i)


def unit_parts(n):
    name, key, _ = STREAM[n] if n < U_MOE else ("moe", None, 0)
    first, words = {"qa": (2 * HD, KQ * HD), "qb": (2 * HEADS * ROPE, KQ * HEADS * ROPE)}.get(name, (UNIT // 2, UNIT))
    if name == "proj" and PROJ_CHUNKS[key][1] < 512:
        first, words = (c * PROJ_CHUNKS[key][1] for c in (KD // 2, KD))
    return slice(0, first), slice(first, words)


def build(nc, t, outs):
    ctx = ExitStack()
    with ctx:
        sems = {}

        def sem(name):
            if name not in sems:
                sems[name] = ctx.enter_context(nc.semaphore(name))
            return sems[name]

        KB = 1024
        base = nc.sbuf_base
        base += (-base) % 64
        arena_bytes = nc.sbuf_usable_end - base - 256
        ctx.enter_context(nc.sbuf_tensor("arena", [P, (arena_bytes - 64) // 4], F32))
        at = [base + 64]

        def region(size):
            start = at[0]
            at[0] += size
            assert at[0] <= base + arena_bytes, (at[0] - base, arena_bytes)
            return start

        def place(name, shape, dtype, where, offset=0):
            return nc.alloc_sbuf_tensor_at(name, shape, dtype, offset=where + offset)

        def own(name, shape, dtype=F32):
            words = int(np.prod(shape[1:]))
            return place(name, shape, dtype, region((words * 4 + 31) // 32 * 32))

        raw = own("raw", [P, RAW, UNIT])
        w_hi = own("w_hi", [P, SPLIT, UNIT], F32R)
        w_lo = own("w_lo", [P, SPLIT, UNIT], F32R)
        X = own("X", [P, TILES, D])
        R_H, R_G, R_P, R_Y = region(24 * KB), region(24 * KB), region(36 * KB), region(12 * KB)
        R_S = region(9 * KB)
        const = own("const", [P, CONST.shape[1]])
        gate_bc = own("gate_bc", [P, 2, D])
        st_cond = own("st_cond", [P, KD, P], F32R)
        mod_col = own("mod_col", [P, 8, KD, 2])
        cols0 = own("cols0", [P, 96])
        cols1 = own("cols1", [P, 112])
        cond_f = own("cond_f", [P, 16])
        cond_hi = own("cond_hi", [P, 16], F32R)
        cond_lo = own("cond_lo", [P, 16], F32R)
        small = own("small", [P, 64])
        lg = own("lg", [P, 16])
        dec = own("dec", [P, 4, HEADS])
        cdec = own("cdec", [P, 2, 4])

        def cst(name):
            a, b = CONST_AT[name]
            return const[:, a:b]

        ident = cst("ident")

        hT = [place(f"hT_{x}", [P, KD, T_ALL], F32R, R_H, o * KB) for x, o in (("hi", 0), ("lo", 12))]
        qnT = [place(f"qnT_{x}", [P, KQ, T_ALL], F32R, R_H, o) for x, o in (("hi", 0), ("lo", 4608))]
        ckvT = [place(f"ckvT_{x}", [P, KKV, 4 * P], F32R, R_H, 9216 + o * KB) for x, o in (("hi", 0), ("lo", 4))]
        V23 = place("V23", [P, 2, HD], F32, R_H, 17408)
        mask = place("mask", [P, HEADS, P], F32, R_H, 0)
        mask_b = place("mask_b", [P, HEADS, P], F32, R_H, 4 * KB)
        k_dec = place("k_dec", [P, 4, HD], F32, R_H, 8 * KB)
        s0 = place("s0", [P, 2, 4, DV], F32, R_H, 16 * KB)
        s1 = place("s1", [P, 2, 4, DV], F32, R_H, 18 * KB)
        s_ctx = place("s_ctx", [P, 2, 4, DV], F32, R_H, 20 * KB)
        hn = place("hn", [P, HD], F32, R_H, 22 * KB)
        H_tok = [place(f"H_{x}", [P, TILES, D], F32R, R_H, o * KB) for x, o in (("hi", 0), ("lo", 12))]

        last_rows = place("last_rows", [P, 2, D], F32, R_H, 0)

        ln_rows = place("ln_rows", [P, 2, D], F32, R_G, 0)
        gate_bias = place("gate_bias", [P, D], F32, R_G, 8 * KB)
        m4 = place("m4", [P, 512], F32, R_G, 12 * KB)
        gate_bias_last = place("gate_bias_last", [P, D], F32, R_P, 20 * KB)
        m4_last = [place(f"m4_last{j}", [P, 512], F32, R_S, o * KB) for j, o in enumerate((0, 7))]
        hf = place("hf", [P, 2, 4, P], F32, R_G, 14 * KB)
        vec_rows = place("vec_rows", [P, 2, P], F32, R_G, 18 * KB)
        qR = place("qR", [P, TILES, HEADS * ROPE], F32, R_G, 0)
        rope_tmp = place("rope_tmp", [P, TILES, HEADS * ROPE], F32, R_G, 3 * KB)
        qNT = place("qNT", [P, 4, T_ALL], F32, R_G, 6 * KB)
        qRT = place("qRT", [P, 2, T_ALL], F32, R_G, 12 * KB)
        kpe4 = place("kpe4", [P, 4, 4, ROPE], F32, R_G, 15 * KB)
        V01 = place("V01", [P, 2, HD], F32, R_G, 17 * KB)
        ret_tmp = place("ret_tmp", [P, HD], F32, R_G, 21 * KB)
        kpe_r = place("kpe_r", [P, 3, ROPE], F32, R_G, 23 * KB)
        rqT = place("rqT", [P, 4, T_ALL], F32, R_G, 0)
        rkT = place("rkT", [P, 4, T_ALL], F32, R_G, 6 * KB)
        qdT = place("qdT", [P, 2, 4, 2 * P], F32, R_G, 12 * KB)
        q_dec = place("q_dec", [P, 2, HD], F32, R_G, 20 * KB)
        gT = [place(f"gT_{x}", [P, KD, T_ALL], F32R, R_G, o * KB) for x, o in (("hi", 0), ("lo", 12))]

        proj = place("proj", [P, TILES, IN_EVEN], F32, R_P)
        kpeT = place("kpeT", [P, 4 * P], F32, R_P, 32640)
        mask_c = place("mask_c", [P, 4, P], F32, R_P, 34 * KB - 128)
        prodT = [place(f"prodT_{x}", [P, 12, T_ALL], F32R, R_P, o * KB) for x, o in (("hi", 0), ("lo", 18))]
        byT = [place(f"byT_{x}", [P, KD, T_ALL], F32R, R_P, o * KB) for x, o in (("hi", 0), ("lo", 12))]
        conv_c = place("conv_c", [P, 2, T_ALL], F32, R_P, 24 * KB)
        zpad = place("zpad", [P, 2, T_ALL + 4], F32, R_P, 27 * KB)
        conv_y = place("conv_y", [P, 2, T_ALL], F32, R_P, 31 * KB)
        hfT = place("hfT", [P, KD, T_ALL], F32, R_P, 0)
        rt = place("rt", [P, 12, TILES, N_EXP], F32, R_P, 24 * KB)
        mix = [place(f"mix_{x}", [P, TILES, HD], F32, R_Y, o * KB) for x, o in (("att", 0), ("ret", 6))]
        Y = place("Y", [P, TILES, D], F32, R_Y)
        mixT = [place(f"mixT_{x}", [P, KD, T_ALL], F32R, R_H, o * KB) for x, o in (("hi", 0), ("lo", 12))]
        kNT = place("kNT", [P, 4, 4 * P], F32, R_S)
        y_st = [place(f"y_{x}", [P, 4, PAIR], F32R, R_P, o * KB) for x, o in (("hi", 0), ("lo", 4))]
        y_last = [gT[0][:, 4 * x:4 * x + 4, P:T_ALL] for x in (0, 1)]
        g_rows = place("g_rows", [P, KD, T_ALL], F32, R_G, 12 * KB)[:, 0:4, P:T_ALL]
        g_rows_more = place("g_rows_more", [P, 4, PAIR], F32, R_P, 8 * KB)
        E = place("E", [P, 2, 3 * P], F32, R_Y, 6 * KB)
        ET = place("ET", [P, 2, 3 * P], F32, R_Y, 9 * KB)
        ckv_c = place("ckv_c", [P, KV_LORA], F32, R_S, 0)
        kv_gain = place("kv_gain", [P, KV_LORA], F32, R_S, 1 * KB)
        junk = place("junk", [P, Q_LORA], F32, R_G, 3 * KB)
        prod = place("prod", [P, 3, PAIR], F32, R_S)
        sel = place("sel", [P, TILES, P], F32R, R_S, 3 * KB)
        ret_s = place("ret_s", [P, 2, 4, P], F32, R_S)
        selT = place("selT", [P, 3, T_ALL], F32R, R_S, 4608)
        rank_tab = place("rank_tab", [P, 2, P], F32, R_P, 28 * KB)
        ret_tab = place("ret_tab", [P, 2, TILES, DV], F32, R_Y)
        posm = own("posm", [P, TILES, N_EXP + 1])
        comb = own("comb", [P, TILES, N_EXP + 1])
        counts = own("counts", [P, 3, N_EXP + 1], I32)
        rtr_w = own("rtr_w", [P, KD, N_EXP])
        rt_bias = own("rt_bias", [P, N_EXP])
        stats = own("stats", [P, TILES, 2, 6])
        mv = own("mv", [P, TILES, 4])
        den = own("den", [P, TILES, HEADS])
        mx = own("mx", [P, 2, 2])

        ps = ctx.enter_context(nc.psum_tensor("ps", [P, 8, 512], F32))

        block = ctx.enter_context(nc.Block())

        def val(k, per, e):
            return k if e is None else e * per + k

        def act_split(act, n, e=None):
            s = n % SPLIT
            if n >= SPLIT:
                act.wait_ge(sem("w_used"), val(n - SPLIT + 1, FFN_UNITS, e))
            for part, cols in enumerate(unit_parts(n)):
                act.wait_ge(sem(f"raw_landed{n % RAW}_{part}"), val(16 * (n // RAW + 1), 16 * FFN_UNITS // RAW, e))
                nc.scalar.copy(w_hi[:, s, cols], raw[:, n % RAW, cols]).then_inc(sem("w_hi_ready"), 1)

        def dve_split(dve, n, e=None):
            s = n % SPLIT
            for part, cols in enumerate(unit_parts(n)):
                dve.wait_ge(sem("w_hi_ready"), val(2 * n + part + 1, 2 * FFN_UNITS, e))
                nc.vector.tensor_tensor(w_lo[:, s, cols], raw[:, n % RAW, cols], w_hi[:, s, cols].bitcast(F32),
                                        ALU.subtract).then_inc(sem("w_ready"), 1)

        def splitter(one):
            done = [0]

            def upto(n):
                while done[0] < min(n + AHEAD + 1, U_MOE + AHEAD + 1):
                    one(done[0])
                    done[0] += 1
            return upto

        def split_in_loop(eng, one, u, e):
            if u + AHEAD < FFN_UNITS:
                if u:
                    one(eng, U_MOE + u + AHEAD, e)
            else:
                with eng.If(e < N_EXP - 1):
                    one(eng, U_MOE + u + AHEAD, e)
                eng.nop()

        class Weights:
            def __init__(self, pe, n, e=None):
                pe.wait_ge(sem("w_ready"), val(2 * n + 2, 2 * FFN_UNITS, e))
                self.hi, self.lo = w_hi[:, n % SPLIT, :], w_lo[:, n % SPLIT, :]

            def used(self, ins):
                ins.then_inc(sem("w_used"), 1)

        def product3(out, a, b, start, stop):
            nc.tensor.matmul(out, a[0], b[0], start=start, stop=False)
            nc.tensor.matmul(out, a[0], b[1], start=False, stop=False)
            return nc.tensor.matmul(out, a[1], b[0], start=False, stop=stop)

        def mod_sums(g):
            return m4_last[MOD_LAST.index(g)][:, :] if g in MOD_LAST else m4[:, :]

        ckv_dst, kpe_dst = outs[2], outs[3]

        @block.sync
        def _(sp):
            def load(n, e=None):
                for (nk, src), (part, cols) in zip(weight_unit(t, n, e), enumerate(unit_parts(n))):
                    if n >= RAW:
                        parts = part + 1 if cols.stop <= unit_parts(n - RAW)[part].stop else 2
                        sp.wait_ge(sem("w_ready"), val(2 * (n - RAW) + parts, 2 * FFN_UNITS, e))
                    dst = raw[:, n % RAW, cols].rearrange("p (k n) -> p k n", k=nk)
                    sp.dma_start(dst, src).then_inc(sem(f"raw_landed{n % RAW}_{part}"), 16)

            def rows(at, n, part, src, name="rows_in"):
                sp.dma_start(vec_rows[at:at + n, part, :], src).then_inc(sem(name), 16)

            rows(0, 8, 0, t["c_ctx"].rearrange("(r n) -> r n", n=P), "cond_in")
            rows(8, 8, 0, t["c"].rearrange("b (r n) -> (b r) n", n=P), "cond_in")
            sp.dma_start(const[:, :], t["const"]).then_inc(sem("const_in"), 16)
            load(0)
            rows(R_QG, 3, 0, t["q_a_gain"].rearrange("b (r n) -> (b r) n", n=P))
            rows(R_CONVW, 24, 0, t["conv_w"].rearrange("a b (r n) -> (a b r) n", n=P))
            rows(R_BMOD, 48, 0, t["b_mod"][0].rearrange("(r n) -> r n", n=P))
            rows(0, 48, 1, t["b_mod"][1].rearrange("(r n) -> r n", n=P))
            rows(48, 32, 1, t["ln_g"].rearrange("l s (r n) -> (l s r) n", n=P))
            rows(80, 32, 1, t["ln_b"].rearrange("l s (r n) -> (l s r) n", n=P))
            for n in range(1, U_MOE):
                load(n)
            with sp.Fori(0, N_EXP) as e:
                for u in range(FFN_UNITS):
                    load(U_MOE + u, e)
            for i in range(TILES):
                sp.wait_ge(sem(f"y_ready{i}"), 1)
                dst = outs[0][0] if i == 0 else outs[1][0, (i - 1) * P:i * P, :]
                sp.dma_start(dst, X[:, i, :]).then_inc(sem("y_stored"), 16)
            sp.wait_ge(sem("y_stored"), 16 * TILES)

        def rope(tt, chain, dst, src, cos, sin, tmp):
            chain(tt(tmp[..., 0::2], src[..., 1::2], sin[..., 0::2], ALU.mult))
            chain(tt(tmp[..., 1::2], src[..., 0::2], sin[..., 1::2], ALU.mult))
            chain(tt(dst, src, cos, ALU.mult))
            return tt(dst, dst, tmp, ALU.add)

        @block.gpsimd
        def _(pool):
            step = [0]

            def chain(ins):
                step[0] += 1
                ins.then_inc(sem("pool_step"), 1)
                pool.wait_ge(sem("pool_step"), step[0])

            def get(dst, src, name):
                pool.dma_start(dst, src).then_inc(sem(name), 16)

            pool.wait_ge(sem("w_used"), 3)
            get(X[:, 0, :], t["x_prompt"][0], "x_in")
            get(X[:, 1:3, :], t["x_sample"][0].rearrange("(t p) d -> p t d", p=P), "x_in")
            pool.wait_ge(sem("w_used"), 2 * len(MOD_FIRST))
            get(gate_bias[:, :], t["b_mod"][0][2 * D:3 * D].unsqueeze(0).broadcast_to([P, D]), "gbias_in")
            get(lg[:, 0:8], t["ret_decay_fwd"].broadcast_to([P, 8]), "dec_in")
            get(lg[:, 8:16], t["ret_decay_bwd"].broadcast_to([P, 8]), "dec_in")
            get(ckv_c[:, :], t["cache_ckv"][0, 0], "cache_in")
            get(kv_gain[:, :], t["kv_a_gain"].broadcast_to([P, KV_LORA]), "cache_in")
            get(ret_tab[:, :, :, :], t["ret_tables"].rearrange("p (a i d) -> p a i d", a=2, i=TILES), "ret_tab_in")
            get(rtr_w[:, :, :], t["router_w"][0].rearrange("(k p) n -> p k n", p=P), "rtr_in")
            get(rt_bias[:, :], t["router_b"].broadcast_to([P, N_EXP]), "rtr_in")
            get(mask_c[:, :, :], t["masks"].rearrange("p (a n) -> p a n", a=4), "mask_in")
            pool.wait_ge(sem("hT_ready"), 2 * TILES)
            get(kpe4[:, 3, 0, :], t["cache_kpe"][0, 0], "kpe_in")

            pool.wait_ge(sem("rms_ms"), 1)
            pool.tensor_tensor(small[:, 8:14], small[:, 0:6], cst("mhalf")[:, 0:6], ALU.pow).then_inc(sem("rms_pow"), 1)
            pool.wait_ge(sem("ret_tab_in"), 16)
            for which, c0 in enumerate((C_RQ, C_RK)):
                pool.wait_ge(sem("proj_in"), 3 + which)
                for i in range(TILES):
                    v = proj[:, i, c0:c0 + HD].rearrange("p (h d) -> p h d", h=HEADS)
                    cs = ret_tab[:, 0, i:i + 1, :].broadcast_to([P, HEADS, DV])
                    sn = ret_tab[:, 1, i:i + 1, :].broadcast_to([P, HEADS, DV])
                    rope(pool.tensor_tensor, chain, v, v, cs, sn,
                         ret_tmp[:, :].rearrange("p (h d) -> p h d", h=HEADS)).then_inc(sem("ret_roped"), 1)
                    pool.wait_ge(sem("ret_roped"), which * TILES + i + 1)
            pool.wait_ge(sem("ckv_ready"), TILES)
            get(ckv_dst[0, 0], proj[:, 0, C_KV:C_KV + KV_LORA], "small_out")
            get(kpe_dst[0, 0], proj[:, 0, C_PE:C_PE + ROPE], "small_out")
            pool.wait_ge(sem("att_done"), TILES)
            for d_, name in enumerate(("state_ret_fwd", "state_ret_bwd")):
                for two in (0, 1):
                    get(s0[64 * two:64 * two + 64, d_, :, :],
                        t[name][0, 0].rearrange("(c two) d v -> two d c v", two=2)[two], "s0_in")
            pool.wait_ge(sem("sctx_ready"), 2)
            for d_ in (0, 1):
                for two in (0, 1):
                    get(outs[4 + d_][0, 0].rearrange("(c two) d v -> two d c v", two=2)[two],
                        s_ctx[64 * two:64 * two + 64, d_, :, :], "small_out")
            for i in range(TILES):
                pool.wait_ge(sem("hn_var"), i + 1)
                pool.tensor_tensor(small[:, 24:32], small[:, 16:24], cst("mhalf"), ALU.pow).then_inc(sem("hn_pow"), 1)
            for k in range(4):
                layer, sub = k // 2, k % 2
                if k == 0:
                    pool.wait_ge(sem("mix_ready"), TILES)
                elif k == 3:
                    pool.wait_ge(sem("x_full"), 3 * TILES)
                    chain(pool.memset(selT[:, 0, :].bitcast(F32), 0.0))
                    chain(pool.memset(y_last[0].bitcast(F32), 0.0))
                    pool.memset(y_last[1].bitcast(F32), 0.0).then_inc(sem("yst_lo"), 1)
                    pool.wait_ge(sem("gathers_done"), 1)
                else:
                    pool.wait_ge(sem("x_full"), TILES * k)
                for j, name in enumerate(("ln_g", "ln_b")):
                    get((last_rows if k == 3 else ln_rows)[:, j, :], t[name][layer, sub].unsqueeze(0).broadcast_to([P, D]), "ln_rows_in")
                if k < 2:
                    nl, nv = ((0, 5), (1, 2))[k]
                    pool.wait_ge(sem("post_done"), MOD_POSTS[GATE_PLACE[k] + 2])
                    get(gate_bias[:, :], t["b_mod"][nl][nv * D:(nv + 1) * D].unsqueeze(0).broadcast_to([P, D]), "gbias_in")
                for i in range(TILES):
                    if k == 3 and i == 2:
                        pool.wait_ge(sem("x_ready"), TILES * k + 1)
                        pool.wait_ge(sem("ln_rows_in"), 32 * (k + 1))
                        chain(pool.tensor_tensor(X[:, 0, :], X[:, 0, :], last_rows[:, 0, :], ALU.mult))
                        pool.tensor_tensor(X[:, 0, :], X[:, 0, :], last_rows[:, 1, :], ALU.add).then_inc(sem("y_ready0"), 1)
                    pool.wait_ge(sem("ln_var"), TILES * k + i + 1)
                    pool.tensor_tensor(mv[:, i, 3:4], mv[:, i, 2:3], cst("mhalf")[:, 0:1], ALU.pow).then_inc(sem("ln_pow"), 1)
                if k == 2:
                    get(gate_bias_last[:, :], t["b_mod"][1][5 * D:6 * D].unsqueeze(0).broadcast_to([P, D]), "gbias_in")
                    get(rank_tab[:, :, :], t["ranks"].rearrange("p (a n) -> p a n", a=2), "ranks_in")
                if k < 3:
                    pool.wait_ge(sem("xT_ready"), 2 * TILES * (k + 2))
                    pool.wait_ge(sem("ln_rows_in"), 32 * (k + 1))
                    for i in range(TILES):
                        chain(pool.tensor_tensor(X[:, i, :], X[:, i, :], ln_rows[:, 0, :], ALU.mult))
                        pool.tensor_tensor(X[:, i, :], X[:, i, :], ln_rows[:, 1, :], ALU.add).then_inc(sem("x_full"), 1)
            pool.wait_ge(sem("small_out"), 16 * 6)

        @block.tensor
        def _(pe):
            mm = nc.tensor.matmul

            pending = []

            def mod_products(g):
                place_ = MOD_ORDER.index(g)
                if place_ >= 1:
                    pe.wait_ge(sem("m4_ready"), place_)
                for half in (0, 1):
                    w = Weights(pe, AT["mod", g] + half)
                    for k in range(4):
                        kc, cols = 4 * half + k, slice(k * 512, (k + 1) * 512)
                        mm(ps[:, 6, :], st_cond[:, kc, :], w.hi[:, cols], start=kc == 0, stop=False)
                        last = mm(ps[:, 6, :], st_cond[:, kc, :], w.lo[:, cols], start=False, stop=kc == KD - 1)
                    w.used(last)

            def mod_post(g, conds=(0, 1)):
                place_ = MOD_ORDER.index(g)
                pe.wait_ge(sem("m4_ready"), place_ + 1)
                posts = MOD_POSTS[place_]
                if posts >= 1:
                    pe.wait_ge(sem("post_done"), posts)
                if MOD_CHUNKS[g][1] % 3 == 2:
                    for cond in conds:
                        if cond:
                            pe.wait_ge(sem("post_done"), posts + 1)
                        mm(ps[:, 7, :], cst("selrow")[:, cond * P:(cond + 1) * P], mod_sums(g),
                           start=True, stop=True).then_inc(sem("post_ready"), 1)
                else:
                    for k in range(4):
                        last = mm(ps[:, 7, 2 * k:2 * k + 2], m4[:, k * P:(k + 1) * P], cst("selcol"),
                                  start=True, stop=True)
                    last.then_inc(sem("post_ready"), 1)

            def modulations(chunks, flush=False):
                for g in chunks:
                    if pending:
                        mod_post(pending.pop())
                    mod_products(g)
                    pending.append(g)
                if flush and pending:
                    mod_post(pending.pop())

            def turn_x(k, tiles=range(TILES)):
                for i in tiles:
                    if k:
                        pe.wait_ge(sem("x_ready"), TILES * (k - 1) + i + 1)
                    for half in (0, 1):
                        for j in range(4):
                            kc = 4 * half + j
                            last = nc.tensor.transpose(ps[:, 2 * i + half, j * P:(j + 1) * P],
                                                       X[:, i, kc * P:(kc + 1) * P], ident)
                        last.then_inc(sem("xT_ready"), 1)

            def input_ready(k, i, half):
                pe.wait_ge(sem("hT_ready"), 2 * TILES * k + 2 * i + half + 1)

            pe.wait_ge(sem("cond_in"), 32)
            pe.wait_ge(sem("const_in"), 16)
            nc.tensor.transpose(ps[:, 0, 0:16], vec_rows[0:16, 0, :], ident[0:16, 0:16]).then_inc(sem("cond_turned"), 1)
            pe.wait_ge(sem("rows_in"), 16 * 6)
            nc.tensor.transpose(ps[:, 1, 0:91], vec_rows[0:91, 0, :], ident[0:91, 0:91])
            nc.tensor.transpose(ps[:, 1, 96:208], vec_rows[0:112, 1, :], ident[0:112, 0:112]).then_inc(sem("cols_ready"), 1)
            pe.wait_ge(sem("cond_ready"), 4)
            modulations(MOD_FIRST, flush=True)
            pe.wait_ge(sem("x_in"), 32)
            pe.wait_ge(sem("cols_done"), 2)
            turn_x(0)

            for c, (_, width) in enumerate(PROJ_CHUNKS):
                n = AT["proj", c]
                if c >= 2:
                    pe.wait_ge(sem("proj_in"), c - 1)
                halves = [(0, KD)] if width < 512 else [(0, 4), (4, 8)]
                for a, b in halves:
                    w = Weights(pe, n)
                    for i in range(TILES):
                        if c == 0:
                            input_ready(0, i, a // 4)
                        for k in range(a, b):
                            cols = slice((k - a) * width, (k - a + 1) * width)
                            last = product3(ps[:, (c % 2) * 3 + i, 0:width], [x[:, k, i * P:(i + 1) * P] for x in hT],
                                            (w.hi[:, cols], w.lo[:, cols]), k == 0, k == KD - 1)
                    w.used(last)
                    n += 1
                modulations(MOD_AFTER_PROJ[c])
            modulations([], flush=True)

            turned = 0

            def turn_bank():
                nonlocal turned
                if turned == 7:
                    pe.wait_ge(sem("lat_hi"), 6)
                elif turned >= 2:
                    pe.wait_ge(sem("lat_lo"), turned - 1)
                turned += 1
                return 6 + (turned - 1) % 2
            pe.wait_ge(sem("post_done"), MOD_POSTS[MOD_ORDER.index(10)])
            pe.wait_ge(sem("cache_in"), 32)
            pe.wait_ge(sem("ckv_ready"), TILES)
            for k in range(KKV):
                b = turn_bank()
                for i in range(4):
                    src = ckv_c[:, k * P:(k + 1) * P] if i == 3 else proj[:, i, C_KV + k * P:C_KV + (k + 1) * P]
                    last = nc.tensor.transpose(ps[:, b, i * P:(i + 1) * P], src, ident)
                last.then_inc(sem("lat_turned"), 1)
            for k in range(KQ):
                b = turn_bank()
                for i in range(TILES):
                    last = nc.tensor.transpose(ps[:, b, i * P:(i + 1) * P], proj[:, i, k * P:(k + 1) * P], ident)
                last.then_inc(sem("lat_turned"), 1)
            b = turn_bank()
            pe.wait_ge(sem("kpe4_ready"), 1)
            for i in range(4):
                last = nc.tensor.transpose(ps[:, b, i * P:(i + 1) * P],
                                           kpe4[:, i, :, :].rearrange("p r d -> p (r d)"), ident)
            last.then_inc(sem("lat_turned"), 1)

            outn = 0

            def mla_bank():
                nonlocal outn
                outn += 1
                if outn == 1:
                    pe.wait_ge(sem("proj_in"), 6)
                if outn > 6:
                    pe.wait_ge(sem("mla_in"), outn - 6)
                return (outn - 1) % 6
            w = Weights(pe, U_KV)
            pe.wait_ge(sem("lat_lo"), KKV)
            kv = [(w.hi[:, k * D:(k + 1) * D], w.lo[:, k * D:(k + 1) * D]) for k in range(KKV)]
            for i in range(4):
                b = mla_bank()
                for k in range(KKV):
                    last = product3(ps[:, b, :], [x[:, k, i * P:(i + 1) * P] for x in ckvT],
                                    [x[:, HD:2 * HD] for x in kv[k]], k == 0, k == KKV - 1)
                last.then_inc(sem("mla_out"), 1)
            for hp in range(4):
                b = mla_bank()
                for k in range(KKV):
                    last = product3(ps[:, b, :], [x[:, hp * P:(hp + 1) * P] for x in kv[k]],
                                    [x[:, k, :] for x in ckvT], k == 0, k == KKV - 1)
                if hp < 3:
                    last.then_inc(sem("mla_out"), 1)
            w.used(last)
            w = Weights(pe, U_QA)
            pe.wait_ge(sem("lat_lo"), KKV + KQ)
            for hp in range(4):
                b = mla_bank()
                for k in range(KQ):
                    cols = slice(k * HD + hp * P, k * HD + (hp + 1) * P)
                    last = product3(ps[:, b, 0:T_ALL], (w.hi[:, cols], w.lo[:, cols]),
                                    [x[:, k, :] for x in qnT], k == 0, k == KQ - 1)
                if hp < 3:
                    last.then_inc(sem("mla_out"), 1)
            w.used(last)
            w = Weights(pe, U_QB)
            for i in range(TILES):
                b = mla_bank()
                for k in range(KQ):
                    cols = slice(k * HEADS * ROPE, (k + 1) * HEADS * ROPE)
                    last = product3(ps[:, b, 0:HEADS * ROPE], [x[:, k, i * P:(i + 1) * P] for x in qnT],
                                    (w.hi[:, cols], w.lo[:, cols]), k == 0, k == KQ - 1)
                if i < TILES - 1:
                    last.then_inc(sem("mla_out"), 1)
            w.used(last)
            pe.wait_ge(sem("qR_ready"), TILES)
            for k in range(2):
                b = turn_bank()
                for i in range(TILES):
                    last = nc.tensor.transpose(ps[:, b, i * P:(i + 1) * P], qR[:, i, k * P:(k + 1) * P], ident)
                last.then_inc(sem("lat_turned"), 1)
            pe.wait_ge(sem("qRT_in"), 2)
            pe.wait_ge(sem("mla_in"), 15)

            items = [(i, h) for i in range(TILES) for h in range(HEADS)]

            def scores(m):
                i, h = items[m]
                keys = slice(0, P) if i == 0 else slice(P, 4 * P)
                nk = 1 if i == 0 else 3
                if m >= 2:
                    pe.wait_ge(sem("e_ready"), m - 1)
                rows, rr = slice(64 * (h % 2), 64 * (h % 2) + 64), slice(32 * (h % 4), 32 * (h % 4) + 32)
                mm(ps[:, m % 2, 0:nk * P], qNT[rows, h // 2, i * P:(i + 1) * P], kNT[rows, h // 2, keys],
                   start=True, stop=False)
                mm(ps[:, m % 2, 0:nk * P], qRT[rr, h // 4, i * P:(i + 1) * P], kpeT[rr, keys],
                   start=False, stop=True).then_inc(sem("s_ready"), 1)

            def turn_e(m):
                i, h = items[m]
                pe.wait_ge(sem("e_ready"), m + 1)
                if m >= 2:
                    pe.wait_ge(sem("eT_ready"), m - 1)
                for j in range(1 if i == 0 else 3):
                    last = nc.tensor.transpose(ps[:, 2 + m % 2, j * P:(j + 1) * P], E[:, m % 2, j * P:(j + 1) * P], ident)
                last.then_inc(sem("eT_turned"), 1)

            def values(m):
                i, h = items[m]
                pe.wait_ge(sem("eT_ready"), m + 1)
                tiles = [0] if i == 0 else [1, 2, 3]
                for j, kt in enumerate(tiles):
                    v = V01[:, kt, :] if kt < 2 else V23[:, kt - 2, :]
                    last = mm(ps[:, 4 + i, h * DV:(h + 1) * DV], ET[:, m % 2, j * P:(j + 1) * P],
                              v[:, h * DV:(h + 1) * DV], start=j == 0, stop=j == len(tiles) - 1)
                last.then_inc(sem("o_ready"), 1)

            for m in range(len(items) + 2):
                if m < len(items):
                    scores(m)
                if 0 <= m - 1 < len(items):
                    turn_e(m - 1)
                if m >= 2:
                    values(m - 2)

            pe.wait_ge(sem("ret_roped"), 2 * TILES)
            rturn = 0

            def ret_bank():
                nonlocal rturn
                if rturn >= 2:
                    pe.wait_ge(sem("ret_turned_in"), rturn - 1)
                rturn += 1
                return (rturn - 1) % 2
            for c0 in (C_RQ, C_RK):
                for k in range(4):
                    b = ret_bank()
                    for i in range(TILES):
                        last = nc.tensor.transpose(ps[:, b, i * P:(i + 1) * P], proj[:, i, c0 + k * P:c0 + (k + 1) * P], ident)
                    last.then_inc(sem("ret_turned"), 1)
            for i in (1, 2):
                for d_ in (0, 1):
                    b = ret_bank()
                    pe.wait_ge(sem("q_dec_ready"), 2 * (i - 1) + d_ + 1)
                    for k in range(4):
                        last = nc.tensor.transpose(ps[:, b, k * P:(k + 1) * P], q_dec[:, d_, k * P:(k + 1) * P], ident)
                    last.then_inc(sem("ret_turned"), 1)
            for j, i in enumerate((0, 0, 1, 2)):
                pe.wait_ge(sem("k_dec_ready"), j + 1)
                if j == 1 or j == 2:
                    pe.wait_ge(sem("sctx_ready"), j)
                elif j == 3:
                    pe.wait_ge(sem("state_in"), 1)
                for h in range(HEADS):
                    r = slice(64 * (h % 2), 64 * (h % 2) + 64)
                    last = mm(ps[r, 2, (h // 2) * DV:(h // 2 + 1) * DV], k_dec[:, j, h * DV:(h + 1) * DV],
                              proj[:, i, C_RV + h * DV:C_RV + (h + 1) * DV], start=True, stop=True)
                last.then_inc(sem("state_out"), 1)
            pe.wait_ge(sem("ret_turned_in"), 12)
            pe.wait_ge(sem("state_in"), 2)
            pe.wait_ge(sem("s0_in"), 16 * 4)
            pe.wait_ge(sem("att_done"), TILES)

            def ret_scores(m):
                i, parity = m // 2, m % 2
                if m >= 2:
                    pe.wait_ge(sem("rs_ready"), m - 1)
                for j in range(4):
                    h = 2 * j + parity
                    r = slice(64 * (h % 2), 64 * (h % 2) + 64)
                    last = mm(ps[:, m % 2, j * P:(j + 1) * P], rkT[r, h // 2, i * P:(i + 1) * P],
                              rqT[r, h // 2, i * P:(i + 1) * P], start=True, stop=True)
                last.then_inc(sem("rs_out"), 1)

            def ret_values(m):
                i, parity = m // 2, m % 2
                pe.wait_ge(sem("rs_ready"), m + 1)
                if parity:
                    pe.wait_ge(sem("ret_even"), i + 1)
                for j in range(4):
                    h = 2 * j + parity
                    r = slice(64 * (h % 2), 64 * (h % 2) + 64)
                    out = ps[:, 4 + i, h * DV:(h + 1) * DV]
                    last = mm(out, ret_s[:, m % 2, j, :], proj[:, i, C_RV + h * DV:C_RV + (h + 1) * DV],
                              start=True, stop=i == 0)
                    if i:
                        fwd, bwd = (s0, s1) if i == 1 else (s1, s0)
                        q = slice((i - 1) * P, i * P)
                        mm(out, qdT[r, 0, h // 2, q], fwd[r, 0, h // 2, :], start=False, stop=False)
                        last = mm(out, qdT[r, 1, h // 2, q], bwd[r, 1, h // 2, :], start=False, stop=True)
                last.then_inc(sem("ret_out" if parity else "ret_even"), 1)

            for m in range(7):
                if m < 6:
                    ret_scores(m)
                if m >= 1:
                    ret_values(m - 1)

            def turn_mix(chunks):
                for k in chunks:
                    if k >= 2:
                        pe.wait_ge(sem("mixT_ready"), k - 1)
                    for i in range(TILES):
                        last = nc.tensor.transpose(ps[:, 6 + k % 2, i * P:(i + 1) * P],
                                                   mix[k // 4][:, i, (k % 4) * P:(k % 4 + 1) * P], ident)
                    last.then_inc(sem("mix_turned"), 1)

            pe.wait_ge(sem("ret_in"), TILES)
            turn_mix(range(4))

            def down(src, widths, unit, acc, tiles, first, last_phase, ready, e=None, by_tile=False):
                k = 0
                for u, nk in enumerate(widths):
                    w = Weights(pe, unit + u, e)
                    for kk in range(nk):
                        ready(k + kk)
                    tiled = by_tile and u == len(widths) - 1
                    order = [(i, kk) for kk in range(nk) for i in range(tiles)]
                    for i, kk in sorted(order) if tiled else order:
                        for half in (0, 1):
                            cols = slice(kk * D + half * 512, kk * D + half * 512 + 512)
                            last = product3(ps[:, acc(i, half), :], [x[:, k + kk, i * P:(i + 1) * P] for x in src],
                                            (w.hi[:, cols], w.lo[:, cols]), first and k + kk == 0,
                                            last_phase and k + kk == sum(widths) - 1)
                        if tiled and kk == nk - 1 and i < tiles - 1:
                            last.then_inc(sem("acc_out"), 1)
                    k += nk
                    w.used(last)
                    yield u

            def all_banks(i, half):
                return 2 * i + half

            def ready_mix(k):
                if k == 4:
                    pe.wait_ge(sem("mix_ready"), TILES)
                    turn_mix(range(4, KD))
                if k >= 4:
                    pe.wait_ge(sem("mixT_ready"), k + 1)
                elif k == 0:
                    pe.wait_ge(sem("mixT_ready"), 4)

            for _ in down(mixT, [2] * 4, U_OUT0, all_banks, TILES, True, True, ready_mix, by_tile=True):
                pass

            def ffn(src, unit, tiles, e, before_tile=lambda u, i: None, after_unit=lambda u: None,
                    after_phase=lambda phase: None):
                pairs0 = 0 if e is None else PAIRS
                per = None if e is None else PAIRS
                single = tiles == 1
                acc = (lambda i, half: 2 + half) if single else all_banks

                def turn_prod(c):
                    pe.wait_ge(sem("prod_ready"), val(pairs0 + c + 1, per, e))
                    prev = c - 1 if tiles == 3 else c - 2
                    if pairs0 + prev >= 0 and prev >= 0:
                        pe.wait_ge(sem("pT_lo"), val(pairs0 + prev + 1, per, e))
                    for i in range(tiles):
                        b = (7 if i == 2 else 6) if tiles == 3 else 6 + c % 2
                        o = (i % 2) * PAIR
                        for j in (0, 1):
                            last = nc.tensor.transpose(ps[:, b, o + j * P:o + (j + 1) * P], prod[:, i, j * P:(j + 1) * P], ident)
                    last.then_inc(sem("pT_turned"), 1)

                u = 0
                for phase in (0, 1):
                    pairs = PHASE_PAIRS[phase]
                    waiting = None
                    for c in pairs:
                        for half in (0, 1):
                            w = Weights(pe, unit(u), e)
                            for i in range(tiles):
                                before_tile(u, i)
                                b = (c + phase) % 2 * tiles + i
                                for k in range(4):
                                    last = product3(ps[:, b, :].rearrange("p (s n) -> p s n", s=2),
                                                    [x[:, 4 * half + k, i * P:(i + 1) * P] for x in src],
                                                    [x.rearrange("p (s k n) -> p k s n", s=2, k=4)[:, k] for x in (w.hi, w.lo)],
                                                    half == 0 and k == 0, half == 1 and k == 3)
                            w.used(last)
                            if half == 0 and waiting is not None:
                                turn_prod(waiting)
                            after_unit(u)
                            u += 1
                        waiting = c
                    if not single:
                        pe.wait_ge(sem("prod_ready"), val(pairs0 + waiting + 1, per, e))
                    last_pair = waiting

                    def ready(k):
                        if k % 2 == 0:
                            pe.wait_ge(sem("pT_lo"), val(pairs0 + pairs[0] + k // 2 + 1, per, e))
                    for d_ in down(prodT, PHASE_DOWN[phase], unit(u), acc, tiles, phase == 0 or not single,
                                   phase == 1 or not single, ready, e, by_tile=e is None and phase == 1):
                        if d_ == 0:
                            turn_prod(last_pair)
                        after_unit(u + d_)
                    u += len(PHASE_DOWN[phase])
                    after_phase(phase)

            def dense_phase(phase):
                if phase == 0:
                    modulations(MOD_IN_FFN, flush=True)
                    pe.wait_ge(sem("post_done"), MOD_POSTS[MOD_ORDER.index(16)])
                    pe.wait_ge(sem("dense_in"), TILES)

            def dense_input(u, i):
                if u == 0 and i < 2:
                    turn_x(1, (0, 1) if i == 0 else (2,))
                if u < 2:
                    input_ready(1, i, u)
            ffn(hT, dense_unit, TILES, None, before_tile=dense_input, after_phase=dense_phase)

            turn_x(2)
            input_ready(2, TILES - 1, 1)
            m = 0
            for f in range(4):
                for third in range(3):
                    w = Weights(pe, AT["conv", f] + third)
                    for j in (0, 1):
                        if f:
                            pe.wait_ge(sem(("conv_c_in", "z_ready", "by_ready")[third]), 2 * (f - 1) + j + 1)
                        for k in range(KD):
                            cols = slice(k * 256 + j * P, k * 256 + (j + 1) * P)
                            last = product3(ps[:, m % 6, 0:T_ALL], (w.hi[:, cols], w.lo[:, cols]),
                                            [x[:, k, :] for x in hT], k == 0, k == KD - 1)
                        m += 1
                        if j == 0:
                            last.then_inc(sem("conv_out"), 1)
                    w.used(last)
                modulations(MOD_AFTER_CONV[f])
            modulations([], flush=True)

            def ready_conv(k):
                if k == 0:
                    pe.wait_ge(sem("by_lo"), KD)
            for g in MOD_LAST:
                mod_products(g)
            for _ in down(byT, [2] * 4, U_OUT1, all_banks, TILES, True, True, ready_conv, by_tile=True):
                pass
            mod_post(MOD_LAST[0], (0,))

            pe.wait_ge(sem("rtr_in"), 32)
            turn_x(3, (0, 1))
            for i in range(TILES):
                pe.wait_ge(sem("hf_ready"), 3 * 2 * TILES + 2 * i + 2)
                if i == 1:
                    turn_x(3, (2,))
                for k in range(KD):
                    last = mm(ps[:, 6, i * N_EXP:(i + 1) * N_EXP], hfT[:, k, i * P:(i + 1) * P], rtr_w[:, k, :],
                              start=k == 0, stop=k == KD - 1)
            last.then_inc(sem("logits_out"), 1)
            for n in range(2 * TILES):
                i, q = n // 2, n % 2
                for k in range(4):
                    last = nc.tensor.transpose(ps[:, n, k * P:(k + 1) * P],
                                               hfT[:, 4 * q + k, i * P:(i + 1) * P], ident)
                last.then_inc(sem("Ht_turned"), 1)
            pe.wait_ge(sem("chosen"), 1)
            pe.wait_ge(sem("ranks_in"), 16)
            for lag in range(TILES):
                mm(ps[:, 6, lag * N_EXP:TILES * N_EXP], rank_tab[:, 1 if lag else 0, :],
                   rt[:, 0, 0:TILES - lag, :], start=lag == 0, stop=lag == TILES - 1)
            for j in range(TILES):
                last = mm(ps[:, 6, 3 * N_EXP:4 * N_EXP], rank_tab[:, 1, :], rt[:, 0, j, :], start=j == 0, stop=j == TILES - 1)
            last.then_inc(sem("ranks_out"), 1)

            pe.wait_ge(sem("counts_ready"), 1)
            pe.wait_ge(sem("Ht_hi"), 2 * TILES)
            pe.wait_ge(sem("Ht_lo"), 2 * TILES)

            def gather(g, bank):
                pe.wait_ge(sem("sel_ready"), g + 1)
                for half in (0, 1):
                    cols = slice(half * 512, half * 512 + 512)
                    for x in (0, 1):
                        for i in range(TILES):
                            last = mm(ps[:, bank + half, :], sel[:, i, :], H_tok[x][:, i, cols],
                                      start=x + i == 0, stop=x == 1 and i == TILES - 1)
                    last.then_inc(sem("g_out"), 1)

            def turn_rows(g, bank, rows):
                for half in (0, 1):
                    pe.wait_ge(sem("g_in"), g * 2 + 2)
                    for k in range(4):
                        kc = 4 * half + k
                        last = nc.tensor.transpose(ps[:, bank + half, k * P:(k + 1) * P],
                                                   rows[:, kc // 2, kc % 2 * P:(kc % 2 + 1) * P], ident)
                    last.then_inc(sem("g_turned"), 1)

            def turn_selection(bank):
                for i in range(TILES):
                    last = nc.tensor.transpose(ps[:, bank, i * P:(i + 1) * P], sel[:, i, :].bitcast(F32), ident)
                last.then_inc(sem("selT_out"), 1)

            def scatter(q, bank, slot, y, steps):
                if 0 in steps:
                    pe.wait_ge(sem("yst_lo"), q + 1)
                for m in steps:
                    i, half = m // 2, m % 2
                    pe.wait_ge(sem("y_added"), q * 6 + (m + 5))
                    out = ps[:, bank + m % 2, :].rearrange("p (a n) -> p a n", a=2)
                    for x in (0, 1):
                        last = mm(out, selT[:, slot, i * P:(i + 1) * P], y[x][:, 2 * half:2 * half + 2, :],
                                  start=x == 0, stop=x == 1)
                    last.then_inc(sem("y_out"), 1)

            mod_post(MOD_LAST[0], (1,))
            gather(0, 4)
            mod_post(MOD_LAST[1])
            turn_rows(0, 4, g_rows)
            pe.wait_ge(sem("post_done"), MOD_POSTS[-1])
            with pe.Fori(0, N_EXP) as e:
                count = pe.value_load(counts[0:1, 0, ds(e, 1)], min_val=0, max_val=T_ALL)
                tiles0 = pe.value_load(counts[0:1, 1, ds(e, 1)], min_val=0, max_val=3 * N_EXP)
                scat0 = pe.value_load(counts[0:1, 2, ds(e, 1)], min_val=0, max_val=6 * N_EXP)

                def expert(tiles):
                    bank = 6 if tiles == 3 else 4
                    pe.wait_ge(sem("y_added"), scat0 * 6 + 6)
                    pe.wait_ge(sem("g_hi"), tiles0 * 2 + 2)
                    pe.wait_ge(sem("g_lo"), tiles0 * 2 + 2)
                    if tiles > 1:
                        scatter(scat0, bank, 0, y_last, range(6))
                        pe.wait_ge(sem("y_added"), scat0 * 6 + 12)
                        turn_selection(bank)
                        for s in range(1, tiles):
                            g = tiles0 + s
                            pe.wait_ge(sem("selT_ready"), g)
                            gather(g, bank)
                            turn_rows(g, bank, g_rows_more)
                            pe.wait_ge(sem("g_hi"), g * 2 + 2)
                            pe.wait_ge(sem("g_lo"), g * 2 + 2)
                            turn_selection(bank)

                    def between(u):
                        if tiles == 1 and u < 3:
                            scatter(scat0, bank, 0, y_last, range(2 * u, 2 * u + 2))
                        elif tiles == 1 and u == 4:
                            pe.wait_ge(sem("y_added"), scat0 * 6 + 12)
                            turn_selection(bank)
                        elif u == GATHER_AT:
                            pe.wait_ge(sem("selT_ready"), tiles0 + tiles)
                            if tiles == 3:
                                pe.wait_ge(sem("pT_lo"), val(PAIRS + PAIRS, PAIRS, e))
                            else:
                                pe.wait_ge(sem("y_added"), scat0 * 6 + (6 * (tiles if tiles > 1 else 0) + 12))
                            gather(tiles0 + tiles, bank)
                        elif u == GATHER_AT + 2:
                            turn_rows(tiles0 + tiles, bank, g_rows)

                    def scatters(phase):
                        if tiles == 1:
                            return
                        if phase == 0:
                            pe.wait_ge(sem("selT_ready"), tiles0 + tiles)
                        else:
                            pe.wait_ge(sem("g_hi"), (tiles0 + tiles) * 2 + 2)
                            pe.wait_ge(sem("g_lo"), (tiles0 + tiles) * 2 + 2)
                        for s in range(tiles - phase):
                            scatter(scat0 + (1 + phase * tiles + s), bank, tiles - 1 - s, y_st, range(6))
                    ffn(gT, expert_unit, tiles, e, after_unit=between, after_phase=scatters)

                with pe.If(count > P):
                    with pe.If(count > 2 * P):
                        expert(3)
                    with pe.Else():
                        expert(2)
                    pe.nop()
                with pe.Else():
                    expert(1)
                pe.nop()
            total = pe.value_load(counts[0:1, 2, N_EXP:N_EXP + 1], min_val=0, max_val=6 * N_EXP)
            pe.wait_ge(sem("y_added"), total * 6 + 6)
            pe.wait_ge(sem("g_hi"), 2)
            pe.nop().then_inc(sem("gathers_done"), 1)
            scatter(total, 4, 0, y_last, range(6))

        @block.scalar
        def _(act):
            split = splitter(lambda n: act_split(act, n))
            step = [0]

            def chain(ins):
                step[0] += 1
                ins.then_inc(sem("act_step"), 1)
                act.wait_ge(sem("act_step"), step[0])

            def modulations(chunks):
                for g in chunks:
                    split(AT["mod", g])
                    split(AT["mod", g] + 1)
                    act.wait_ge(sem("w_used"), AT["mod", g] + 2)
                    nc.scalar.copy(mod_sums(g), ps[:, 6, :]).then_inc(sem("m4_ready"), 1)

            def modulate(norm, shift, scale, dst=None):
                for n in range(2 * TILES):
                    i, half = n // 2, n % 2
                    done = 2 * TILES * norm + n
                    cols = slice(i * P, (i + 1) * P)
                    act.wait_ge(sem("xT_ready"), done + 1)
                    if dst is None:
                        if n >= 2:
                            act.wait_ge(sem("hT_ready"), done - 1)
                        out = hf[:, n % 2, :, :]
                    else:
                        out = dst[:, 4 * half:4 * half + 4, cols]
                    cond = min(i, 1)
                    for j in range(4):
                        k = 4 * half + j
                        last = nc.scalar.activation(out[:, j, :], ps[:, n, j * P:(j + 1) * P], ACT.Identity,
                                                    bias=mod_col[:, shift, k, cond:cond + 1],
                                                    scale=mod_col[:, scale, k, cond:cond + 1])
                    last.then_inc(sem("hf_ready"), 1)
                    if dst is None:
                        act.wait_ge(sem("hf_ready"), done + 1)
                        nc.scalar.copy(hT[0][:, 4 * half:4 * half + 4, cols], out).then_inc(sem("hT_hi"), 1)

            act.wait_ge(sem("cond_turned"), 1)
            chain(nc.scalar.activation(cond_f[:, :], ps[:, 0, 0:16], ACT.Silu))
            nc.scalar.copy(cond_hi[:, :], cond_f[:, :]).then_inc(sem("cond_hi"), 1)
            act.wait_ge(sem("cols_ready"), 1)
            nc.scalar.copy(cols1[:, :], ps[:, 1, 96:208]).then_inc(sem("cols_done"), 1)
            nc.scalar.copy(cols0[:, 0:91], ps[:, 1, 0:91]).then_inc(sem("cols_done"), 1)
            modulations(MOD_FIRST)
            act.wait_ge(sem("post_done"), MOD_POSTS[len(MOD_FIRST)])
            modulate(0, 0, 1)
            for c, (c0, width) in enumerate(PROJ_CHUNKS):
                n = AT["proj", c]
                for _ in range(1 if width < 512 else 2):
                    split(n)
                    n += 1
                act.wait_ge(sem("w_used"), n)
                src = ps[:, (c % 2) * 3:(c % 2) * 3 + 3, 0:width]
                nc.scalar.activation(proj[:, :, c0:c0 + width], src, ACT.Copy,
                                     scale=RET_SCALE if c0 == C_RK else 1.0).then_inc(sem("proj_in"), 1)
                if c == 0:
                    act.wait_ge(sem("lsig_in"), 1)
                    nc.scalar.activation(small[:, 48:64], small[:, 32:48], ACT.Exp).then_inc(sem("lsig_exp"), 1)
                modulations(MOD_AFTER_PROJ[c])
                if c == 1:
                    act.wait_ge(sem("proj_in"), 2)
                    for i in range(TILES):
                        for j, (a, b) in enumerate(((C_Q, Q_LORA), (C_KV, KV_LORA))):
                            if i + j:
                                act.wait_ge(sem("rms_ss"), 2 * i + j)
                            nc.scalar.activation(junk[:, 0:b], proj[:, i, a:a + b], ACT.Square,
                                                 accum_out=small[:, 16 + 3 * j + i:17 + 3 * j + i]).then_inc(sem("rms_ss"), 1)
            act.wait_ge(sem("proj_in"), 6)
            for i in range(TILES):
                nc.scalar.activation(proj[:, i, C_RG:C_RG + HD], proj[:, i, C_RG:C_RG + HD], ACT.Silu).then_inc(sem("rg_ready"), 1)
            for m in range(KKV + KQ):
                act.wait_ge(sem("lat_turned"), m + 1)
                b = 6 + m % 2
                if m == 0:
                    act.wait_ge(sem("w_used"), U_KV)
                if m < KKV:
                    nc.scalar.copy(ckvT[0][:, m, :], ps[:, b, :]).then_inc(sem("lat_hi"), 1)
                else:
                    k = m - KKV
                    nc.scalar.activation(qnT[0][:, k, :], ps[:, b, 0:T_ALL], ACT.Copy,
                                         scale=cols0[:, R_QG + k:R_QG + k + 1]).then_inc(sem("lat_hi"), 1)
            act.wait_ge(sem("lat_turned"), 6)
            nc.scalar.copy(kpeT[:, :], ps[:, 7, :]).then_inc(sem("lat_hi"), 1)
            split(U_KV)
            for m in range(15):
                if m == 8:
                    split(U_QA)
                if m == 12:
                    split(U_QB)
                done = {7: U_KV, 11: U_QA, 14: U_QB}.get(m)
                if done is None:
                    act.wait_ge(sem("mla_out"), m + 1 - sum(m > x for x in (7, 11)))
                else:
                    act.wait_ge(sem("w_used"), done + 1)
                b = m % 6
                if m < 2:
                    nc.scalar.copy(V01[:, m, :], ps[:, b, :]).then_inc(sem("mla_in"), 1)
                elif m < 4:
                    nc.scalar.copy(V23[:, m - 2, :], ps[:, b, :]).then_inc(sem("mla_in"), 1)
                elif m < 8:
                    nc.scalar.copy(kNT[:, m - 4, :], ps[:, b, :]).then_inc(sem("mla_in"), 1)
                elif m < 12:
                    nc.scalar.copy(qNT[:, m - 8, :], ps[:, b, 0:T_ALL]).then_inc(sem("mla_in"), 1)
                else:
                    nc.scalar.copy(qR[:, m - 12, :], ps[:, b, 0:HEADS * ROPE]).then_inc(sem("mla_in"), 1)
            for k in range(2):
                act.wait_ge(sem("lat_turned"), 7 + k)
                nc.scalar.copy(qRT[:, k, :], ps[:, 6 + k % 2, 0:T_ALL]).then_inc(sem("qRT_in"), 1)
            for m in range(TILES * HEADS):
                i, h = m // HEADS, m % HEADS
                w_ = P if i == 0 else 3 * P
                act.wait_ge(sem("mx_ready"), m + 1)
                if m >= 2:
                    act.wait_ge(sem("eT_turned"), m - 1)
                nc.scalar.activation(E[:, m % 2, 0:w_], ps[:, m % 2, 0:w_], ACT.Exp, bias=mx[:, m % 2, 1:2],
                                     scale=ATT_SCALE, accum_out=den[:, i, h:h + 1]).then_inc(sem("e_ready"), 1)
            act.wait_ge(sem("att_done"), TILES)
            act.wait_ge(sem("lg_ready"), 1)
            act.wait_ge(sem("mask_in"), 16)
            for j, (a, d_) in enumerate(((0, 0), (1, 0), (2, 1), (3, 1))):
                nc.scalar.activation(dec[:, j, :], lg[:, 8 * d_:8 * d_ + 8], ACT.Exp, scale=cst("decay_at")[:, a:a + 1])
            for two in (0, 1):
                r = slice(64 * two, 64 * two + 64)
                last = nc.scalar.activation(cdec[r, :, :], lg[r, :].rearrange("p (d c two) -> p d c two", d=2, two=2)[:, :, :, two],
                                            ACT.Exp, scale=float(P))
            last.then_inc(sem("dec_ready"), 1)
            for m in range(12):
                act.wait_ge(sem("ret_turned"), m + 1)
                b = m % 2
                if m < 8:
                    dst = (rqT if m < 4 else rkT)[:, m % 4, :]
                    last = nc.scalar.copy(dst, ps[:, b, 0:T_ALL])
                else:
                    i, d_ = (m - 8) // 2, (m - 8) % 2
                    last = nc.scalar.copy(qdT[:, d_, :, i * P:(i + 1) * P], ps[:, b, :].rearrange("p (c n) -> p c n", c=4))
                last.then_inc(sem("ret_turned_in"), 1)
                if m < HEADS:
                    nc.scalar.activation(mask[:, m, :], mask_c[:, 0, :], ACT.Exp, scale=lg[:, m:m + 1])
                    nc.scalar.activation(mask_b[:, m, :], mask_c[:, 1, :], ACT.Exp, scale=lg[:, 8 + m:9 + m]).then_inc(sem("mask_exp"), 1)
            for j in range(2):
                act.wait_ge(sem("state_out"), j + 1)
                nc.scalar.copy(s_ctx[:, j, :, :], ps[:, 2, 0:4 * DV].rearrange("p (c v) -> p c v", c=4)).then_inc(sem("sctx_ready"), 1)
            for i in range(TILES):
                act.wait_ge(sem("ret_out"), i + 1)
                nc.scalar.copy(mix[1][:, i, :], ps[:, 4 + i, :]).then_inc(sem("ret_in"), 1)

            def mix_hi(chunks):
                for k in chunks:
                    act.wait_ge(sem("mix_turned"), k + 1)
                    nc.scalar.copy(mixT[0][:, k, :], ps[:, 6 + k % 2, 0:T_ALL]).then_inc(sem("mixT_hi"), 1)
            mix_hi(range(4))
            split(U_OUT0)
            split(U_OUT0 + 1)
            act.wait_ge(sem("small_out"), 16 * 6)
            mix_hi(range(4, KD))
            split(U_OUT0 + 2)
            split(U_OUT0 + 3)
            act.wait_ge(sem("folded"), 1)
            modulate(1, 2, 3)

            def ffn(unit, tiles, e, splits, after_phase):
                pairs0 = 0 if e is None else PAIRS
                per = None if e is None else PAIRS

                def hidden_hi(c):
                    act.wait_ge(sem("pT_turned"), val(pairs0 + c + 1, per, e))
                    k = 2 * (c - PHASE_PAIRS[0 if c < 6 else 1][0])
                    for i in range(tiles):
                        b = (7 if i == 2 else 6) if tiles == 3 else 6 + c % 2
                        o = (i % 2) * PAIR
                        last = nc.scalar.copy(prodT[0][:, k:k + 2, i * P:(i + 1) * P],
                                              ps[:, b, o:o + PAIR].rearrange("p (j n) -> p j n", j=2))
                    last.then_inc(sem("pT_hi"), 1)
                u = 0
                for phase in (0, 1):
                    waiting = None
                    for c in PHASE_PAIRS[phase]:
                        for half in (0, 1):
                            splits(u)
                            u += 1
                            if half == 0 and waiting is not None:
                                hidden_hi(waiting)
                        waiting = c
                        act.wait_ge(sem("w_used"), val(unit(u - 1) + 1, FFN_UNITS, e))
                        for i in range(tiles):
                            b = (c + phase) % 2 * tiles + i
                            last = nc.scalar.activation(prod[:, i, :], ps[:, b, 0:PAIR], ACT.Silu)
                        last.then_inc(sem("sg_ready"), 1)
                    for d_ in range(len(PHASE_DOWN[phase])):
                        splits(u)
                        u += 1
                        if d_ == 0:
                            hidden_hi(waiting)
                    after_phase(phase, u)

            def dense_phase(phase, u):
                if phase == 0:
                    act.wait_ge(sem("w_used"), dense_unit(u - 1) + 1)
                    for i in (1, 2):
                        nc.scalar.copy(Y[:, i, :].rearrange("p (a n) -> p a n", a=2),
                                       ps[:, 2 * i:2 * i + 2, :]).then_inc(sem("dense_in"), 1)
                    modulations(MOD_IN_FFN)
            ffn(dense_unit, TILES, None, lambda u: split(dense_unit(u)), dense_phase)
            act.wait_ge(sem("folded"), 2)
            modulate(2, 4, 5)
            for f in range(4):
                for third in range(3):
                    unit = AT["conv", f] + third
                    split(unit)
                    for j in (0, 1):
                        m = 6 * f + 2 * third + j
                        if j == 0:
                            act.wait_ge(sem("conv_out"), 3 * f + third + 1)
                        else:
                            act.wait_ge(sem("w_used"), unit + 1)
                        if third == 0:
                            if f:
                                act.wait_ge(sem("z_ready"), 2 * (f - 1) + j + 1)
                            nc.scalar.copy(conv_c[:, j, :], ps[:, m % 6, 0:T_ALL]).then_inc(sem("conv_c_in"), 1)
                        if third == 2:
                            act.wait_ge(sem("by_ready"), 2 * f + j + 1)
                            nc.scalar.copy(byT[0][:, 2 * f + j, :], conv_y[:, j, :]).then_inc(sem("by_hi"), 1)
                modulations(MOD_AFTER_CONV[f])
            modulations(MOD_LAST)
            for u in range(4):
                split(U_OUT1 + u)
            split(U_MOE)
            act.wait_ge(sem("folded"), 3)
            modulate(3, 6, 7, dst=hfT)
            for n in range(2 * TILES):
                i, q = n // 2, n % 2
                act.wait_ge(sem("Ht_turned"), n + 1)
                nc.scalar.copy(H_tok[0][:, i, q * 512:(q + 1) * 512], ps[:, n, :]).then_inc(sem("Ht_hi"), 1)
            act.wait_ge(sem("chosen_max"), 1)
            nc.scalar.activation(small[:, 8:8 + TILES], small[:, 0:TILES], ACT.Exp).then_inc(sem("gate_exp"), 1)
            act.wait_ge(sem("counts_ready"), 1)

            def rows_in(g, bank, rows):
                for half in (0, 1):
                    act.wait_ge(sem("g_out"), g * 2 + (half + 1))
                    nc.scalar.copy(rows[:, 2 * half:2 * half + 2, :],
                                   ps[:, bank + half, :].rearrange("p (a n) -> p a n", a=2)).then_inc(sem("g_in"), 1)

            def gathered_hi(g, bank, s):
                for half in (0, 1):
                    act.wait_ge(sem("g_turned"), g * 2 + (half + 1))
                    nc.scalar.copy(gT[0][:, 4 * half:4 * half + 4, s * P:(s + 1) * P],
                                   ps[:, bank + half, :].rearrange("p (k n) -> p k n", k=4)).then_inc(sem("g_hi"), 1)

            def selection_in(g, bank, slot):
                act.wait_ge(sem("selT_out"), g + 1)
                nc.scalar.copy(selT[:, slot, :], ps[:, bank, 0:T_ALL]).then_inc(sem("selT_ready"), 1)

            rows_in(0, 4, g_rows)
            act.wait_ge(sem("x_full"), 3 * TILES)
            gathered_hi(0, 4, 0)
            with act.Fori(0, N_EXP) as e:
                count = act.value_load(counts[0:1, 0, ds(e, 1)], min_val=0, max_val=T_ALL)
                tiles0 = act.value_load(counts[0:1, 1, ds(e, 1)], min_val=0, max_val=3 * N_EXP)
                scat0 = act.value_load(counts[0:1, 2, ds(e, 1)], min_val=0, max_val=6 * N_EXP)

                def expert(tiles):
                    bank = 6 if tiles == 3 else 4
                    nc.scalar.activation(small[:, 48:49], small[:, 49:50], ACT.Silu)
                    if tiles > 1:
                        selection_in(tiles0, bank, tiles - 1)
                        for s in range(1, tiles):
                            g = tiles0 + s
                            rows_in(g, bank, g_rows_more)
                            gathered_hi(g, bank, s)
                            selection_in(g, bank, tiles - 1 - s)

                    def splits(u):
                        split_in_loop(act, act_split, u, e)
                        if tiles == 1 and u == 5:
                            selection_in(tiles0, bank, 0)
                        elif u == GATHER_AT + 1:
                            rows_in(tiles0 + tiles, bank, g_rows)
                        elif u == GATHER_AT + 3:
                            gathered_hi(tiles0 + tiles, bank, 0)

                    def stage(phase, u):
                        if tiles == 1 and phase == 0:
                            return
                        act.wait_ge(sem("w_used"), val(expert_unit(u), FFN_UNITS, e))
                        for s in range(tiles):
                            last = phase == 1 and s == tiles - 1
                            if not last:
                                act.wait_ge(sem("y_out"), (scat0 + (1 + phase * tiles + s)) * 6)
                            b = 2 if tiles == 1 else 2 * s
                            nc.scalar.copy((y_last if last else y_st)[0][:, :, :],
                                           ps[:, b:b + 2, :].rearrange("p h (a n) -> p (h a) n", a=2)).then_inc(sem("yst_hi"), 1)
                    ffn(expert_unit, tiles, e, splits, stage)
                    split_in_loop(act, act_split, FFN_UNITS, e)

                with act.If(count > P):
                    with act.If(count > 2 * P):
                        expert(3)
                    with act.Else():
                        expert(2)
                    act.nop()
                with act.Else():
                    expert(1)
                act.nop()

        @block.vector
        def _(dve):
            split = splitter(lambda n: dve_split(dve, n))
            step = [0]
            tt, ts = nc.vector.tensor_tensor, nc.vector.tensor_scalar
            stt = nc.vector.scalar_tensor_tensor

            def chain(ins):
                step[0] += 1
                ins.then_inc(sem("dve_step"), 1)
                dve.wait_ge(sem("dve_step"), step[0])

            def mod_out(g, conds=(0, 1)):
                layer, v, half = MOD_CHUNKS[g]
                posts = MOD_POSTS[MOD_ORDER.index(g)]
                if v % 3 == 2:
                    if half == 0:
                        dve.wait_ge(sem("gbias_in"), 16 * (2 * layer + v // 3 + 1))
                    for cond in conds:
                        dve.wait_ge(sem("post_ready"), posts + cond + 1)
                        cols = slice(half * 512, half * 512 + 512)
                        bias = gate_bias_last if g in MOD_LAST else gate_bias
                        tt(gate_bc[:, cond, cols], ps[:, 7, :], bias[:, cols], ALU.add).then_inc(sem("post_done"), 1)
                else:
                    dve.wait_ge(sem("post_ready"), posts + 1)
                    bcol = (cols0[:, R_BMOD:R_BMOD + 48] if layer == 0 else cols1[:, 0:48])
                    b = bcol[:, v * KD + 4 * half:v * KD + 4 * half + 4].unsqueeze(2).broadcast_to([P, 4, 2])
                    src = ps[:, 7, 0:8].rearrange("p (k c) -> p k c", c=2)
                    slot = 4 * layer + 2 * (v // 3) + v % 3
                    stt(mod_col[:, slot, 4 * half:4 * half + 4, :], src, float(v % 3), b, ALU.add, ALU.add).then_inc(sem("post_done"), 1)

            pending = []

            def modulations(chunks, flush=False):
                for g in chunks:
                    split(AT["mod", g])
                    if pending:
                        mod_out(pending.pop())
                    split(AT["mod", g] + 1)
                    pending.append(g)
                if flush and pending:
                    mod_out(pending.pop())

            def fold(k, posts):
                shift, scale = mod_col[:, 2 * (k + 1), :, :], mod_col[:, 2 * (k + 1) + 1, :, :]
                g, b = (cols1[:, 48 + 32 * v + 8 * k:56 + 32 * v + 8 * k].unsqueeze(2).broadcast_to([P, KD, 2]) for v in (0, 1))
                dve.wait_ge(sem("post_done"), posts)
                tmp = small[:, 16:32].rearrange("p (k c) -> p k c", c=2)
                chain(tt(tmp, scale, b, ALU.mult))
                chain(tt(shift, shift, tmp, ALU.add))
                tt(scale, scale, g, ALU.mult).then_inc(sem("folded"), 1)

            def input_lo(norm, i):
                for half in (0, 1):
                    n = 2 * i + half
                    part = (slice(None), slice(4 * half, 4 * half + 4), slice(i * P, (i + 1) * P))
                    dve.wait_ge(sem("hT_hi"), 2 * TILES * norm + n + 1)
                    tt(hT[1][part], hf[:, n % 2, :, :], hT[0][part].bitcast(F32), ALU.subtract).then_inc(sem("hT_ready"), 1)

            def layer_norm(k, summed, ready):
                halves = lambda ap: ap.rearrange("p (a n) -> p a n", a=2)

                def weigh(i):
                    ready(i)
                    s, y, g = summed(i), halves(Y[:, i, :]), halves(gate_bc[:, min(i, 1), :])
                    chain(tt(y, s, g, ALU.mult))

                def moments(i):
                    if k:
                        dve.wait_ge(sem("x_full"), TILES * (k - 1) + i + 1)
                    alpha = 1.0 if k == 1 else ALPHA
                    chain(stt(X[:, i, :], X[:, i, :], alpha, Y[:, i, :], ALU.mult, ALU.add))
                    nc.vector.bn_stats(stats[:, i, 0, :], X[:, i, 0:512])
                    chain(nc.vector.bn_stats(stats[:, i, 1, :], X[:, i, 512:D]))
                    chain(nc.vector.bn_aggr(mv[:, i, 0:2], stats[:, i, :, :].rearrange("p a n -> p (a n)")))
                    ts(mv[:, i, 2:3], mv[:, i, 1:2], LN_EPS, None, ALU.add).then_inc(sem("ln_var"), 1)

                def normalise(i):
                    if k == 3 and i:
                        dve.wait_ge(sem("ln_rows_in"), 32 * (k + 1))
                        chain(stt(X[:, i, :], X[:, i, :], mv[:, i, 0:1], last_rows[:, 0, :], ALU.subtract, ALU.mult))
                        dve.wait_ge(sem("ln_pow"), TILES * k + i + 1)
                        stt(X[:, i, :], X[:, i, :], mv[:, i, 3:4], last_rows[:, 1, :], ALU.mult, ALU.add).then_inc(sem(f"y_ready{i}"), 1)
                        return
                    dve.wait_ge(sem("ln_pow"), TILES * k + i + 1)
                    ts(X[:, i, :], X[:, i, :], mv[:, i, 0:1], mv[:, i, 3:4], ALU.subtract, ALU.mult).then_inc(sem("x_ready"), 1)

                def follow(i):
                    if k < 2:
                        input_lo(k + 1, i)

                weigh(0), moments(0)
                weigh(1), normalise(0), moments(1)
                weigh(2), normalise(1), follow(0), moments(2)
                follow(1), normalise(2), follow(2)

            def sums_ready(k, last_unit):
                def wait(i):
                    if i < TILES - 1:
                        dve.wait_ge(sem("acc_out"), (TILES - 1) * k + i + 1)
                    else:
                        dve.wait_ge(sem("w_used"), last_unit + 1)
                return wait

            dve.wait_ge(sem("cond_hi"), 1)
            chain(tt(cond_lo[:, :], cond_f[:, :], cond_hi[:, :].bitcast(F32), ALU.subtract))
            for g, (src, o) in enumerate(((cond_hi, 0), (cond_lo, 0), (cond_hi, 8), (cond_lo, 8))):
                nc.vector.tensor_copy(st_cond[:, :, 32 * g:32 * g + 32],
                                      src[:, o:o + 8].bitcast(F32).unsqueeze(2).broadcast_to([P, KD, 32])).then_inc(sem("cond_ready"), 1)
            split(0)
            dve.wait_ge(sem("cols_done"), 2)
            modulations(MOD_FIRST, flush=True)
            for i in range(TILES):
                input_lo(0, i)
            dve.wait_ge(sem("dec_in"), 32)
            chain(ts(small[:, 32:48], lg[:, :], -1.0, None, ALU.mult))
            chain(tt(small[:, 32:48], small[:, 32:48], lg[:, :], ALU.min))
            ts(small[:, 32:48], small[:, 32:48], 1.0, None, ALU.mult).then_inc(sem("lsig_in"), 1)
            for c in (0, 1):
                for m in range(2 - c):
                    split(AT["proj", c] + m)
                modulations(MOD_AFTER_PROJ[c])
            dve.wait_ge(sem("lsig_exp"), 1)
            u_, s_ = small[:, 48:64], small[:, 32:48]
            chain(ts(s_, u_, 2.0, None, ALU.add))
            chain(nc.vector.reciprocal(s_, s_))
            chain(tt(u_, u_, s_, ALU.mult))
            chain(tt(s_, u_, u_, ALU.mult))
            pl = small[:, 0:16]
            chain(ts(pl, s_, 1.0 / 17, None, ALU.mult))
            for m in range(15, 1, -2):
                chain(stt(pl, pl, 1.0 / m, s_, ALU.add, ALU.mult))
            chain(stt(pl, pl, 1.0, u_, ALU.add, ALU.mult))
            chain(ts(lg[:, :], lg[:, :], 0.0, None, ALU.min))
            stt(lg[:, :], pl, -2.0, lg[:, :], ALU.mult, ALU.add).then_inc(sem("lg_ready"), 1)
            dve.wait_ge(sem("lg_ready"), 1)
            dve.wait_ge(sem("rms_ss"), 2 * TILES)
            chain(ts(small[:, 0:3], small[:, 16:19], 1.0 / Q_LORA, RMS_EPS, ALU.mult, ALU.add))
            ts(small[:, 3:6], small[:, 19:22], 1.0 / KV_LORA, RMS_EPS, ALU.mult, ALU.add).then_inc(sem("rms_ms"), 1)
            for c in range(2, 6):
                for m in range(2):
                    split(AT["proj", c] + m)
                modulations(MOD_AFTER_PROJ[c])
            modulations([], flush=True)
            fold(0, MOD_POSTS[MOD_ORDER.index(10)])
            fold(1, MOD_POSTS[MOD_ORDER.index(10)])
            dve.wait_ge(sem("rms_pow"), 1)
            dve.wait_ge(sem("cache_in"), 32)
            cosq, sinq = (cst(x).rearrange("p (i d) -> p i d", i=TILES) for x in ("cos_q", "sin_q"))
            for i in range(TILES):
                stt(proj[:, i, C_KV:C_KV + KV_LORA], proj[:, i, C_KV:C_KV + KV_LORA], small[:, 11 + i:12 + i],
                    kv_gain[:, :], ALU.mult, ALU.mult)
                ts(proj[:, i, 0:Q_LORA], proj[:, i, 0:Q_LORA], small[:, 8 + i:9 + i], None, ALU.mult).then_inc(sem("ckv_ready"), 1)
            rope(tt, chain, kpe_r[:, :, :], proj[:, :, C_PE:C_PE + ROPE], cosq, sinq,
                 rope_tmp[:, :, 0:ROPE]).then_inc(sem("kpe_r"), 1)
            dve.wait_ge(sem("kpe_r"), 1)
            nc.vector.tensor_copy(kpe4[:, 0:3, :, :], kpe_r[:, :, :].unsqueeze(2).broadcast_to([P, 3, 4, ROPE]))
            dve.wait_ge(sem("kpe_in"), 16)
            nc.vector.tensor_copy(kpe4[:, 3, 1:4, :], kpe4[:, 3, 0:1, :].broadcast_to([P, 3, ROPE])).then_inc(sem("kpe4_ready"), 1)
            for m in range(KKV + KQ):
                dve.wait_ge(sem("lat_hi"), m + 1)
                b = 6 + m % 2
                if m < KKV:
                    tt(ckvT[1][:, m, :], ps[:, b, :], ckvT[0][:, m, :].bitcast(F32), ALU.subtract).then_inc(sem("lat_lo"), 1)
                else:
                    k = m - KKV
                    stt(qnT[1][:, k, :], ps[:, b, 0:T_ALL], cols0[:, R_QG + k:R_QG + k + 1],
                        qnT[0][:, k, :].bitcast(F32), ALU.mult, ALU.subtract).then_inc(sem("lat_lo"), 1)
            split(U_KV)
            split(U_QA)
            split(U_QB)
            for i in range(TILES):
                dve.wait_ge(sem("mla_in"), 13 + i)
                v = qR[:, i, :].rearrange("p (h d) -> p h d", h=HEADS)
                rope(tt, chain, v, v, cosq[:, i:i + 1, :].broadcast_to([P, HEADS, ROPE]),
                     sinq[:, i:i + 1, :].broadcast_to([P, HEADS, ROPE]),
                     rope_tmp[:, i, :].rearrange("p (h d) -> p h d", h=HEADS)).then_inc(sem("qR_ready"), 1)
            items = TILES * HEADS

            def maximum(m):
                w_ = P if m < HEADS else 3 * P
                dve.wait_ge(sem("s_ready"), m + 1)
                if m >= 2:
                    dve.wait_ge(sem("e_ready"), m - 1)
                nc.vector.tensor_reduce(mx[:, m % 2, 0:1], ps[:, m % 2, 0:w_], AX, ALU.max).then_inc(sem("mx_raw"), 1)
                dve.wait_ge(sem("mx_raw"), m + 1)
                ts(mx[:, m % 2, 1:2], mx[:, m % 2, 0:1], -ATT_SCALE, None, ALU.mult).then_inc(sem("mx_ready"), 1)

            def weights_in(m):
                w_ = P if m < HEADS else 3 * P
                dve.wait_ge(sem("eT_turned"), m + 1)
                if m >= 2:
                    dve.wait_ge(sem("o_ready"), m - 1)
                nc.vector.tensor_copy(ET[:, m % 2, 0:w_], ps[:, 2 + m % 2, 0:w_]).then_inc(sem("eT_ready"), 1)

            for m in range(items + 1):
                if m < items:
                    maximum(m)
                if m >= 1:
                    weights_in(m - 1)
            dve.wait_ge(sem("ret_roped"), 2 * TILES)
            for i in range(TILES):
                dve.wait_ge(sem("o_ready"), HEADS * (i + 1))
                dve.wait_ge(sem("e_ready"), HEADS * (i + 1))
                chain(nc.vector.reciprocal(den[:, i, :], den[:, i, :]))
                tt(mix[0][:, i, :].rearrange("p (h d) -> p h d", h=HEADS),
                   ps[:, 4 + i, :].rearrange("p (h d) -> p h d", h=HEADS),
                   den[:, i, :].unsqueeze(2).broadcast_to([P, HEADS, DV]), ALU.mult).then_inc(sem("att_done"), 1)

            heads = lambda ap: ap.rearrange("p (h d) -> p h d", h=HEADS)
            over = lambda j: dec[:, j, :].unsqueeze(2).broadcast_to([P, HEADS, DV])
            dve.wait_ge(sem("dec_ready"), 1)
            dve.wait_ge(sem("ret_roped"), 2 * TILES)
            dve.wait_ge(sem("att_done"), TILES)
            for j, (i, d_) in enumerate(((0, 1), (0, 2), (1, 1), (2, 2))):
                tt(heads(k_dec[:, j, :]), heads(proj[:, i, C_RK:C_RK + HD]), over(d_), ALU.mult).then_inc(sem("k_dec_ready"), 1)
            for i in (1, 2):
                for d_ in (0, 1):
                    if i == 2:
                        dve.wait_ge(sem("ret_turned"), 9 + d_)
                    tt(heads(q_dec[:, d_, :]), heads(proj[:, i, C_RQ:C_RQ + HD]), over(0 if d_ == 0 else 3),
                       ALU.mult).then_inc(sem("q_dec_ready"), 1)
            dve.wait_ge(sem("mask_exp"), HEADS)
            over_h = lambda j: mask_c[:, j:j + 1, :].broadcast_to([P, HEADS, P])
            chain(tt(mask[:, :, :], mask[:, :, :], over_h(2), ALU.mult))
            chain(tt(mask_b[:, :, :], mask_b[:, :, :], over_h(3), ALU.mult))
            chain(tt(mask[:, :, :], mask[:, :, :], mask_b[:, :, :], ALU.add))
            dve.wait_ge(sem("s0_in"), 16 * 4)
            for d_ in (0, 1):
                chain(tt(s1[:, d_, :, :], s0[:, d_, :, :], cdec[:, d_, :].unsqueeze(2).broadcast_to([P, 4, DV]), ALU.mult))
                dve.wait_ge(sem("state_out"), 3 + d_)
                tt(s1[:, d_, :, :], ps[:, 2, 0:4 * DV].rearrange("p (c v) -> p c v", c=4), s1[:, d_, :, :],
                   ALU.add).then_inc(sem("state_in"), 1)

            def masked(m):
                dve.wait_ge(sem("rs_out"), m + 1)
                tt(ret_s[:, m % 2, :, :], ps[:, m % 2, :].rearrange("p (j n) -> p j n", j=4),
                   mask[:, m % 2::2, :], ALU.mult).then_inc(sem("rs_ready"), 1)

            def head_norm(i):
                dve.wait_ge(sem("ret_in"), i + 1)
                sm = small[:, 16:24]
                y = heads(mix[1][:, i, :])
                chain(nc.vector.tensor_reduce(sm, y, AX, ALU.add))
                chain(ts(sm, sm, 1.0 / DV, None, ALU.mult))
                chain(tt(y, y, sm.unsqueeze(2).broadcast_to([P, HEADS, DV]), ALU.subtract))
                chain(tt(heads(hn[:, :]), y, y, ALU.mult))
                chain(nc.vector.tensor_reduce(sm, heads(hn[:, :]), AX, ALU.add))
                ts(sm, sm, 1.0 / DV, LN_EPS, ALU.mult, ALU.add).then_inc(sem("hn_var"), 1)
                chain(tt(y, y, heads(proj[:, i, C_RG:C_RG + HD]), ALU.mult))
                dve.wait_ge(sem("hn_pow"), i + 1)
                tt(y, y, small[:, 24:32].unsqueeze(2).broadcast_to([P, HEADS, DV]), ALU.mult).then_inc(sem("mix_ready"), 1)
                dve.wait_ge(sem("mix_ready"), i + 1)

            for m in range(6):
                if m % 2 == 0 and m >= 2:
                    dve.wait_ge(sem("ret_out"), m // 2)
                masked(m)

            def mix_lo(chunks):
                for k in chunks:
                    dve.wait_ge(sem("mixT_hi"), k + 1)
                    tt(mixT[1][:, k, :], ps[:, 6 + k % 2, 0:T_ALL], mixT[0][:, k, :].bitcast(F32), ALU.subtract).then_inc(sem("mixT_ready"), 1)
            mix_lo(range(4))
            dve.wait_ge(sem("rg_ready"), TILES)
            split(U_OUT0)
            for i in range(TILES):
                head_norm(i)
            split(U_OUT0 + 1)
            mix_lo(range(4, KD))
            split(U_OUT0 + 2)
            split(U_OUT0 + 3)
            acc = lambda i: ps[:, 2 * i:2 * i + 2, :]
            layer_norm(0, acc, sums_ready(0, U_OUT0 + 3))

            def ffn(unit, tiles, e, splits, after_phase):
                pairs0 = 0 if e is None else PAIRS
                per = None if e is None else PAIRS

                def hidden_lo(c):
                    dve.wait_ge(sem("pT_hi"), val(pairs0 + c + 1, per, e))
                    k = 2 * (c - PHASE_PAIRS[0 if c < 6 else 1][0])
                    for i in range(tiles):
                        b = (7 if i == 2 else 6) if tiles == 3 else 6 + c % 2
                        o = (i % 2) * PAIR
                        last = tt(prodT[1][:, k:k + 2, i * P:(i + 1) * P],
                                  ps[:, b, o:o + PAIR].rearrange("p (j n) -> p j n", j=2),
                                  prodT[0][:, k:k + 2, i * P:(i + 1) * P].bitcast(F32), ALU.subtract)
                    last.then_inc(sem("pT_lo"), 1)
                u = 0
                for phase in (0, 1):
                    waiting = None
                    for c in PHASE_PAIRS[phase]:
                        for half in (0, 1):
                            splits(u)
                            u += 1
                            if half == 0 and waiting is not None:
                                hidden_lo(waiting)
                        waiting = c
                        dve.wait_ge(sem("sg_ready"), val(pairs0 + c + 1, per, e))
                        for i in range(tiles):
                            b = (c + phase) % 2 * tiles + i
                            last = tt(prod[:, i, :], prod[:, i, :], ps[:, b, PAIR:2 * PAIR], ALU.mult)
                        last.then_inc(sem("prod_ready"), 1)
                    for d_ in range(len(PHASE_DOWN[phase])):
                        splits(u)
                        u += 1
                        if d_ == 0:
                            hidden_lo(waiting)
                    after_phase(phase, u)

            def dense_phase(phase, u):
                if phase == 0:
                    dve.wait_ge(sem("w_used"), dense_unit(u - 1) + 1)
                    nc.vector.tensor_copy(Y[:, 0, :].rearrange("p (a n) -> p a n", a=2), acc(0)).then_inc(sem("dense_in"), 1)
                    modulations(MOD_IN_FFN, flush=True)
                    dve.wait_ge(sem("dense_in"), TILES)
                    dve.wait_ge(sem("post_done"), MOD_POSTS[MOD_ORDER.index(MOD_IN_FFN[-1]) + 1])
                    dve.wait_ge(sem("x_full"), TILES)
                    for i in range(TILES):
                        chain(tt(Y[:, i, :], Y[:, i, :], gate_bc[:, min(i, 1), :], ALU.mult))
                        chain(stt(X[:, i, :], X[:, i, :], ALPHA, Y[:, i, :], ALU.mult, ALU.add))
            ffn(dense_unit, TILES, None, lambda u: split(dense_unit(u)), dense_phase)
            layer_norm(1, acc, sums_ready(1, dense_unit(FFN_UNITS - 1)))

            spans = ((0, 0, P), (P + 2, P, 2 * P))
            zz = zpad[:, :, :]
            for a in (0, P + 1, P + 2, T_ALL + 3):
                last = nc.vector.memset(zz[:, :, a:a + 1], 0.0)
                chain(last)
            cw = lambda tap, k: cols0[:, R_CONVW + tap * KD + k:R_CONVW + tap * KD + k + 1]
            for f in range(4):
                for third in range(3):
                    unit = AT["conv", f] + third
                    split(unit)
                    for j in (0, 1):
                        m, k = 6 * f + 2 * third + j, 2 * f + j
                        bank = ps[:, m % 6, :]
                        if third == 1:
                            dve.wait_ge(sem("conv_c_in"), k + 1)
                            if j == 0:
                                dve.wait_ge(sem("conv_out"), 3 * f + third + 1)
                            else:
                                dve.wait_ge(sem("w_used"), unit + 1)
                            for z0, t0, nt in spans:
                                last = tt(zz[:, j, z0 + 1:z0 + 1 + nt], bank[:, t0:t0 + nt], conv_c[:, j, t0:t0 + nt], ALU.mult)
                            last.then_inc(sem("z_ready"), 1)
                            dve.wait_ge(sem("z_ready"), k + 1)
                            if f:
                                dve.wait_ge(sem("by_hi"), 2 * (f - 1) + j + 1)
                            for z0, t0, nt in spans:
                                y = conv_y[:, j, t0:t0 + nt]
                                chain(ts(y, zz[:, j, z0:z0 + nt], cw(0, k), None, ALU.mult))
                                chain(stt(y, zz[:, j, z0 + 1:z0 + 1 + nt], cw(1, k), y, ALU.mult, ALU.add))
                                chain(stt(y, zz[:, j, z0 + 2:z0 + 2 + nt], cw(2, k), y, ALU.mult, ALU.add))
                        elif third == 2:
                            if j == 0:
                                dve.wait_ge(sem("conv_out"), 3 * f + third + 1)
                            else:
                                dve.wait_ge(sem("w_used"), unit + 1)
                            tt(conv_y[:, j, :], bank[:, 0:T_ALL], conv_y[:, j, :], ALU.mult).then_inc(sem("by_ready"), 1)
                            dve.wait_ge(sem("by_hi"), k + 1)
                            tt(byT[1][:, k, :], conv_y[:, j, :], byT[0][:, k, :].bitcast(F32), ALU.subtract).then_inc(sem("by_lo"), 1)
                modulations(MOD_AFTER_CONV[f])
            modulations([], flush=True)
            fold(2, MOD_POSTS[MOD_ORDER.index(22)])
            for g in MOD_LAST:
                split(AT["mod", g])
                split(AT["mod", g] + 1)
            for u in range(4):
                split(U_OUT1 + u)
            layer_norm(2, acc, sums_ready(2, U_OUT1 + 3))
            split(U_MOE)
            mod_out(MOD_LAST[0], (0,))
            for m in range(6):
                nc.vector.memset(Y[:, m // 2, (m % 2) * 512:(m % 2) * 512 + 512], 0.0).then_inc(sem("y_added"), 1)

            dve.wait_ge(sem("logits_out"), 1)
            R = lambda j: rt[:, j, :, :]
            per_tile = lambda ap: ap.unsqueeze(2).broadcast_to([P, TILES, N_EXP])
            b8 = lambda ap: ap.unsqueeze(1).broadcast_to([P, TILES, N_EXP])
            dve.wait_ge(sem("rtr_in"), 32)
            chain(tt(R(1), ps[:, 6, 0:24].rearrange("p (i n) -> p i n", i=TILES), b8(rt_bias[:, :]), ALU.add))
            m1, m2, ix = small[:, 32:35], small[:, 36:39], small[:, 40:43]

            def best(logits, top, eq, one):
                chain(nc.vector.tensor_reduce(top, logits, AX, ALU.max))
                chain(tt(eq, logits, per_tile(top), ALU.is_equal))
                chain(tt(eq, eq, b8(cst("rank8")), ALU.mult))
                chain(nc.vector.tensor_reduce(ix, eq, AX, ALU.max))
                chain(tt(one, eq, per_tile(ix), ALU.is_equal))
            best(R(1), m1, R(2), R(3))
            chain(stt(R(4), R(3), -1e30, R(1), ALU.mult, ALU.add))
            best(R(4), m2, R(2), R(5))
            tt(R(0), R(3), R(5), ALU.add).then_inc(sem("chosen"), 1)
            dve.wait_ge(sem("chosen"), 1)
            tt(small[:, 0:TILES], m2, m1, ALU.subtract).then_inc(sem("chosen_max"), 1)
            for n in range(2 * TILES):
                i, q = n // 2, n % 2
                dve.wait_ge(sem("Ht_hi"), n + 1)
                tt(H_tok[1][:, i, q * 512:(q + 1) * 512], ps[:, n, :],
                   H_tok[0][:, i, q * 512:(q + 1) * 512].bitcast(F32), ALU.subtract).then_inc(sem("Ht_lo"), 1)
            dve.wait_ge(sem("gate_exp"), 1)
            ex, w1 = small[:, 8:11], small[:, 16:19]
            chain(ts(w1, ex, 1.0, None, ALU.add))
            chain(nc.vector.reciprocal(w1, w1))
            chain(tt(ex, ex, w1, ALU.mult))
            chain(tt(R(3), R(3), per_tile(w1), ALU.mult))
            chain(tt(R(5), R(5), per_tile(ex), ALU.mult))
            chain(nc.vector.memset(comb[:, :, 0:1], 0.0))
            chain(tt(comb[:, :, 1:N_EXP + 1], R(3), R(5), ALU.add))
            dve.wait_ge(sem("ranks_out"), 1)
            chain(nc.vector.memset(posm[:, :, N_EXP:], -1.0))
            pm = posm[:, :, 0:N_EXP]
            chain(stt(pm, ps[:, 6, 0:24].rearrange("p (i n) -> p i n", i=TILES), 1.0, R(0), ALU.add, ALU.mult))
            chain(ts(pm, pm, -1.0, None, ALU.add))
            cnt, big, huge = (R(j)[:, 0, :] for j in (1, 2, 4))
            sums = [rt[:, 8 + 2 * j:10 + 2 * j, :, :].rearrange("p r i n -> p r (i n)") for j in (0, 1)]
            for a in sums:
                chain(nc.vector.memset(a[:, :, 0:N_EXP + 1], 0.0))
            chain(nc.vector.tensor_copy(cnt, ps[:, 6, 24:32]))
            chain(ts(big, cnt, float(P), None, ALU.is_gt))
            chain(ts(huge, cnt, float(2 * P), None, ALU.is_gt))
            chain(nc.vector.tensor_copy(counts[:, 0, 0:N_EXP], cnt))
            ones = sums[0][:, :, N_EXP + 1:2 * N_EXP + 1]
            for row, (w_big, w_huge) in enumerate(((1.0, 1.0), (3.0, 2.0))):
                chain(ts(ones[:, row, :], huge, w_huge, 1.0, ALU.mult, ALU.add))
                chain(stt(ones[:, row, :], big, w_big, ones[:, row, :], ALU.mult, ALU.add))
            for j, shift in enumerate((1, 2, 4, 8)):
                a, b = sums[j % 2], sums[1 - j % 2]
                chain(tt(b[:, :, N_EXP:2 * N_EXP + 1], a[:, :, N_EXP:2 * N_EXP + 1],
                         a[:, :, N_EXP - shift:2 * N_EXP + 1 - shift], ALU.add))
            nc.vector.tensor_copy(counts[:, 1:3, :], sums[0][:, :, N_EXP:2 * N_EXP + 1]).then_inc(sem("counts_ready"), 1)
            dve.wait_ge(sem("counts_ready"), 1)


            def select(g, s, column):
                for i in range(TILES):
                    last = ts(sel[:, i, :], cst("iota"), float(s * P), posm[:, i, column], ALU.add, ALU.is_equal)
                last.then_inc(sem("sel_ready"), 1)

            def gathered_lo(g, bank, s):
                for half in (0, 1):
                    cols = slice(s * P, (s + 1) * P)
                    dve.wait_ge(sem("g_hi"), g * 2 + (half + 1))
                    tt(gT[1][:, 4 * half:4 * half + 4, cols], ps[:, bank + half, :].rearrange("p (k n) -> p k n", k=4),
                       gT[0][:, 4 * half:4 * half + 4, cols].bitcast(F32), ALU.subtract).then_inc(sem("g_lo"), 1)

            def add_scatter(q, bank, column, steps):
                for m in steps:
                    i, half = m // 2, m % 2
                    y = Y[:, i, half * 512:half * 512 + 512]
                    dve.wait_ge(sem("y_added"), q * 6 + (m + 1))
                    dve.wait_ge(sem("y_out"), q * 6 + (m + 1))
                    stt(y, ps[:, bank + m % 2, :], comb[:, i, column], y, ALU.mult, ALU.add).then_inc(sem("y_added"), 1)

            select(0, 0, slice(0, 1))
            mod_out(MOD_LAST[0], (1,))
            mod_out(MOD_LAST[1])
            gathered_lo(0, 4, 0)
            with dve.Fori(0, N_EXP) as e:
                count = dve.value_load(counts[0:1, 0, ds(e, 1)], min_val=0, max_val=T_ALL)
                tiles0 = dve.value_load(counts[0:1, 1, ds(e, 1)], min_val=0, max_val=3 * N_EXP)
                scat0 = dve.value_load(counts[0:1, 2, ds(e, 1)], min_val=0, max_val=6 * N_EXP)

                def expert(tiles):
                    bank = 6 if tiles == 3 else 4
                    if tiles > 1:
                        add_scatter(scat0, bank, ds(e, 1), range(6))
                        for s in range(1, tiles):
                            g = tiles0 + s
                            dve.wait_ge(sem("selT_out"), g)
                            select(g, s, ds(e, 1))
                            gathered_lo(g, bank, s)

                    def splits(u):
                        if tiles == 1 and 1 <= u < 4:
                            add_scatter(scat0, bank, ds(e, 1), range(2 * u - 2, 2 * u))
                        split_in_loop(dve, dve_split, u, e)
                        if u == GATHER_AT - 1:
                            dve.wait_ge(sem("selT_out"), tiles0 + tiles)
                            select(tiles0 + tiles, 0, ds(e + 1, 1))
                        elif u == GATHER_AT + 3:
                            gathered_lo(tiles0 + tiles, bank, 0)

                    def way_back(phase, u):
                        if tiles == 1 and phase == 0:
                            return
                        for s in range(tiles):
                            q = scat0 + (1 + phase * tiles + s)
                            last = phase == 1 and s == tiles - 1
                            y = y_last if last else y_st
                            b = 2 if tiles == 1 else 2 * s
                            dve.wait_ge(sem("yst_hi"), q if tiles > 1 else scat0 + 1)
                            tt(y[1][:, :, :], ps[:, b:b + 2, :].rearrange("p h (a n) -> p (h a) n", a=2),
                               y[0][:, :, :].bitcast(F32), ALU.subtract).then_inc(sem("yst_lo"), 1)
                            if not last:
                                add_scatter(q, bank, ds(e + 1, 1), range(6))
                    ffn(expert_unit, tiles, e, splits, way_back)
                    split_in_loop(dve, dve_split, FFN_UNITS, e)

                with dve.If(count > P):
                    with dve.If(count > 2 * P):
                        expert(3)
                    with dve.Else():
                        expert(2)
                    dve.nop()
                with dve.Else():
                    expert(1)
                dve.nop()
            total = dve.value_load(counts[0:1, 2, N_EXP:N_EXP + 1], min_val=0, max_val=6 * N_EXP)

            def last_scatter(i):
                add_scatter(total, 4, slice(N_EXP, N_EXP + 1), (2 * i, 2 * i + 1))
                dve.wait_ge(sem("y_added"), total * 6 + (2 * i + 8))
            layer_norm(3, lambda i: Y[:, i, :].rearrange("p (a n) -> p a n", a=2), last_scatter)


_OUTS = [((1, 128, 1024), "float32"), ((1, 256, 1024), "float32"), ((1, 1, 128, 256), "float32"),
         ((1, 1, 128, 32), "float32"), ((1, 1, 8, 64, 64), "float32"), ((1, 1, 8, 64, 64), "float32")]


def kernel(**inputs):
    import concourse.bacc as bacc
    from concourse.bass_utils import run_bass_kernel_spmd

    nc = bacc.Bacc("TRN2", target_bir_lowering=False, num_devices=1)
    arrays = {k: np.ascontiguousarray(v) for k, v in inputs.items()}
    q = arrays["w_q_b"].reshape(1, Q_LORA, HEADS, NOPE + ROPE)
    arrays["w_q_b"] = np.concatenate([q[..., :NOPE].reshape(1, Q_LORA, -1), q[..., NOPE:].reshape(1, Q_LORA, -1)], -1)
    kv = arrays["w_kv_b"].reshape(1, KV_LORA, HEADS, NOPE + DV)
    arrays["w_kv_b"] = np.concatenate([kv[..., :NOPE].reshape(1, KV_LORA, -1), kv[..., NOPE:].reshape(1, KV_LORA, -1)], -1)
    arrays |= {"const": CONST, "masks": MASKS, "ret_tables": RET_TABLES, "ranks": RANKS}
    feed, t = {}, {}
    for name, a in arrays.items():
        feed[f"in_{name}"] = a
        t[name] = nc.dram_tensor(f"in_{name}", a.shape, mybir.dt.from_np(a.dtype), kind="ExternalInput").ap()
    outs = [nc.dram_tensor(f"out_{i}", s, mybir.dt.from_np(np.dtype(d)), kind="ExternalOutput").ap()
            for i, (s, d) in enumerate(_OUTS)]
    build(nc, t, outs)
    r = run_bass_kernel_spmd(nc, [feed], core_ids=[0])
    return tuple(r.results[0][f"out_{i}"] for i in range(len(_OUTS)))
```
